# Optimizing a Trainium2 kernel written in Bass

```python
import math
import jax, jax.numpy as jnp
from jax import lax
import numpy as np

D_MODEL = 1024
BATCH = 1
SEQ = 256
DEPTH = 2

CHUNK = 64
PLE_DIM = 256

SSD_HEAD_DIM = 64
SSD_HEADS = D_MODEL // SSD_HEAD_DIM
SSD_INNER = SSD_HEADS * SSD_HEAD_DIM
SSD_GROUPS = 4
SSD_STATE = 128
SSD_CONV = 4
SSD_CONV_DIM = SSD_INNER + 2 * SSD_GROUPS * SSD_STATE

ATTN_HEAD_DIM = 64
ATTN_Q_HEADS = 16
ATTN_KV_HEADS = 4
ATTN_Q_WIDTH = ATTN_Q_HEADS * ATTN_HEAD_DIM
ATTN_KV_WIDTH = ATTN_KV_HEADS * ATTN_HEAD_DIM
ATTN_WINDOW = 128
WINDOW_CHUNKS = ATTN_WINDOW // CHUNK
ROPE_THETA = 10000.0

POOL_WINDOWS = (2, 4, 8, 16)
POOL_GROUPS = len(POOL_WINDOWS)
POOL_WIDTH = 1024
POOL_GROUP_DIM = POOL_WIDTH // POOL_GROUPS

N_BRANCHES = 3
BRANCH_WIDTH = 1024

IN_SIZES = (SSD_INNER, SSD_CONV_DIM, SSD_HEADS, ATTN_Q_WIDTH, ATTN_KV_WIDTH, ATTN_KV_WIDTH, POOL_WIDTH, N_BRANCHES * D_MODEL)
N_IN = SSD_INNER + SSD_CONV_DIM + SSD_HEADS + ATTN_Q_WIDTH + 2 * ATTN_KV_WIDTH + POOL_WIDTH + N_BRANCHES * D_MODEL

MOE_GROUPS = 4
MOE_EXPERTS_PER_GROUP = 4
MOE_TOP_K = 2
MOE_HIDDEN = 256

DEEPNORM_ALPHA = (2.0 * DEPTH) ** 0.25
DEEPNORM_BETA = (8.0 * DEPTH) ** -0.25
LN_EPS = 1e-5
RMS_EPS = 1e-5

kernel_name = "hybrid_ssd_swa_pool_hmoe_deepnorm"

def _split(u, sizes):
    out, start = [], 0
    for n in sizes:
        out.append(u[..., start:start + n])
        start += n
    return out

def layer_norm(x, g, b):
    xf = x.astype(jnp.float32)
    mu = jnp.mean(xf, axis=-1, keepdims=True)
    var = jnp.mean(jnp.square(xf - mu), axis=-1, keepdims=True)
    y = (xf - mu) * lax.rsqrt(var + LN_EPS)
    return (y * g.astype(jnp.float32) + b.astype(jnp.float32)).astype(x.dtype)

def rope_tables(positions):
    inv = ROPE_THETA ** (-jnp.arange(0, ATTN_HEAD_DIM, 2, dtype=jnp.float32) / ATTN_HEAD_DIM)
    ang = positions.astype(jnp.float32)[..., None] * inv
    return jnp.cos(ang), jnp.sin(ang)

def apply_rope(t, cos, sin):
    t1, t2 = jnp.split(t.astype(jnp.float32), 2, axis=-1)
    c, s = cos[:, :, None, :], sin[:, :, None, :]
    return jnp.concatenate([t1 * c - t2 * s, t2 * c + t1 * s], axis=-1).astype(t.dtype)

def causal_depthwise_conv(u, w, b):
    out = lax.conv_general_dilated(
        u, w[:, None, :].astype(u.dtype), window_strides=(1,), padding=[(SSD_CONV - 1, 0)],
        dimension_numbers=('NWC', 'WIO', 'NWC'), feature_group_count=u.shape[-1])
    return out + b.astype(u.dtype)

def ssd_mixer(z, xbc, dt_raw, conv_w, conv_b, dt_bias, a_log, d_skip, norm_w):
    bsz, slen, _ = z.shape
    nc = slen // CHUNK
    r = SSD_HEADS // SSD_GROUPS
    f32 = jnp.float32
    xbc = jax.nn.silu(causal_depthwise_conv(xbc, conv_w, conv_b)).astype(f32)
    xs, bm, cm = _split(xbc, (SSD_INNER, SSD_GROUPS * SSD_STATE, SSD_GROUPS * SSD_STATE))
    dt = jax.nn.softplus(dt_raw.astype(f32) + dt_bias.astype(f32))
    a = -jnp.exp(a_log.astype(f32))
    xh = xs.reshape(bsz, nc, CHUNK, SSD_GROUPS, r, SSD_HEAD_DIM)
    dt_c = dt.reshape(bsz, nc, CHUNK, SSD_GROUPS, r)
    x_dt = xh * dt_c[..., None]
    bm = bm.reshape(bsz, nc, CHUNK, SSD_GROUPS, SSD_STATE)
    cm = cm.reshape(bsz, nc, CHUNK, SSD_GROUPS, SSD_STATE)
    a_cs = jnp.cumsum(dt_c * a.reshape(SSD_GROUPS, r), axis=2)
    seg = a_cs[:, :, :, None] - a_cs[:, :, None]
    causal = jnp.tril(jnp.ones((CHUNK, CHUNK), dtype=bool))
    decay = jnp.exp(jnp.where(causal[:, :, None, None], seg, -jnp.inf))
    cb = jnp.einsum('bclgn,bcsgn->bclsg', cm, bm)
    y_diag = jnp.einsum('bclsg,bclsgr,bcsgrp->bclgrp', cb, decay, x_dt)
    decay_to_end = jnp.exp(a_cs[:, :, -1:] - a_cs)
    states = jnp.einsum('bclgn,bclgr,bclgrp->bcgrpn', bm, decay_to_end, x_dt)
    chunk_decay = jnp.exp(a_cs[:, :, -1])

    def step(h, inp):
        st, dec = inp
        return h * dec[..., None, None] + st, h

    h0 = jnp.zeros((bsz, SSD_GROUPS, r, SSD_HEAD_DIM, SSD_STATE), f32)
    _, h_in = lax.scan(step, h0, (jnp.moveaxis(states, 1, 0), jnp.moveaxis(chunk_decay, 1, 0)))
    h_in = jnp.moveaxis(h_in, 0, 1)
    y_off = jnp.einsum('bclgn,bcgrpn,bclgr->bclgrp', cm, h_in, jnp.exp(a_cs))
    y = y_diag + y_off + xh * d_skip.astype(f32).reshape(SSD_GROUPS, r)[:, :, None]
    y = y.reshape(bsz, slen, SSD_INNER)
    gy = (y * jax.nn.silu(z.astype(f32))).reshape(bsz, slen, SSD_GROUPS, SSD_INNER // SSD_GROUPS)
    gy = gy * lax.rsqrt(jnp.mean(gy * gy, axis=-1, keepdims=True) + RMS_EPS)
    return (gy.reshape(bsz, slen, SSD_INNER) * norm_w.astype(f32)).astype(z.dtype)

def swa_sink_attention(q, k, v, sinks, cos, sin):
    bsz, slen, _ = q.shape
    nc = slen // CHUNK
    r = ATTN_Q_HEADS // ATTN_KV_HEADS
    kw = WINDOW_CHUNKS * CHUNK
    q = apply_rope(q.reshape(bsz, slen, ATTN_Q_HEADS, ATTN_HEAD_DIM), cos, sin)
    k = apply_rope(k.reshape(bsz, slen, ATTN_KV_HEADS, ATTN_HEAD_DIM), cos, sin)
    v = v.reshape(bsz, slen, ATTN_KV_HEADS, ATTN_HEAD_DIM)
    qb = q.reshape(bsz, nc, CHUNK, ATTN_KV_HEADS, r, ATTN_HEAD_DIM)

    def band(t):
        tp = jnp.pad(t, ((0, 0), ((WINDOW_CHUNKS - 1) * CHUNK, 0), (0, 0), (0, 0)))
        parts = [tp[:, i * CHUNK:i * CHUNK + slen].reshape(bsz, nc, CHUNK, ATTN_KV_HEADS, ATTN_HEAD_DIM)
                 for i in range(WINDOW_CHUNKS)]
        return jnp.concatenate(parts, axis=2)

    kb, vb = band(k), band(v)
    key_chunk = jnp.arange(nc)[:, None] - (WINDOW_CHUNKS - 1) + jnp.arange(kw)[None, :] // CHUNK
    valid = key_chunk >= 0
    scores = jnp.einsum('bcqgrd,bckgd->bcgrqk', qb, kb).astype(jnp.float32) * (ATTN_HEAD_DIM ** -0.5)
    scores = jnp.where(valid[None, :, None, None, None, :], scores, -jnp.inf)
    sink = sinks.astype(jnp.float32).reshape(1, 1, ATTN_KV_HEADS, r, 1, 1)
    m = jnp.maximum(jnp.max(scores, axis=-1, keepdims=True), sink)
    e = jnp.exp(scores - m)
    probs = e / (jnp.sum(e, axis=-1, keepdims=True) + jnp.exp(sink - m))
    out = jnp.einsum('bcgrqk,bckgd->bcqgrd', probs.astype(vb.dtype), vb)
    return out.reshape(bsz, slen, ATTN_Q_WIDTH)

def multiscale_pool(u, pool_w, pool_scale):
    bsz, slen, _ = u.shape
    ug = u.astype(jnp.float32).reshape(bsz, slen, POOL_GROUPS, POOL_GROUP_DIM)
    cs = jnp.cumsum(ug, axis=1)
    t = jnp.arange(1, slen + 1, dtype=jnp.float32)
    means = []
    for gi, w in enumerate(POOL_WINDOWS):
        c = cs[:, :, gi]
        c_shift = jnp.pad(c, ((0, 0), (w, 0), (0, 0)))[:, :slen]
        means.append((c - c_shift) / jnp.minimum(t, w)[None, :, None])
    pooled = jnp.stack(means, axis=2) - ug
    mixed = jnp.einsum('bsgc,gcd->bsgd', pooled, pool_w.astype(jnp.float32))
    return (mixed.reshape(bsz, slen, POOL_WIDTH) * pool_scale.astype(jnp.float32)).astype(u.dtype)

def mixing_sublayer(h, cos, sin, w_in, ssd_conv_w, ssd_conv_b, ssd_dt_bias, ssd_a_log, ssd_d,
                    ssd_norm_w, attn_sinks, pool_w, pool_scale, w_branch, w_out):
    bsz, slen, _ = h.shape
    u = h @ w_in
    z, xbc, dt_raw, q, k, v, pu, gate_logits = _split(u, IN_SIZES)
    y_ssd = ssd_mixer(z, xbc, dt_raw, ssd_conv_w, ssd_conv_b, ssd_dt_bias, ssd_a_log, ssd_d, ssd_norm_w)
    y_att = swa_sink_attention(q, k, v, attn_sinks, cos, sin)
    y_pool = multiscale_pool(pu, pool_w, pool_scale)
    gates = jax.nn.sigmoid(gate_logits.reshape(bsz, slen, N_BRANCHES, D_MODEL))
    merged = (gates[:, :, 0] * (y_ssd @ w_branch[0])
              + gates[:, :, 1] * (y_att @ w_branch[1])
              + gates[:, :, 2] * (y_pool @ w_branch[2]))
    return merged @ w_out

def hierarchical_moe(h, rg_w, rg_b, re_w, re_b, w_gate, w_up, w_down):
    bsz, slen, _ = h.shape
    g_logits = (h @ rg_w + rg_b).astype(jnp.float32)
    g_probs = jax.nn.softmax(g_logits, axis=-1)
    g_idx = jnp.argmax(g_logits, axis=-1)
    g_weight = jnp.max(g_probs, axis=-1)
    e_logits = (h @ re_w + re_b).astype(jnp.float32).reshape(bsz, slen, MOE_GROUPS, MOE_EXPERTS_PER_GROUP)
    e_sel = jnp.take_along_axis(e_logits, g_idx[..., None, None], axis=2)[:, :, 0]
    top_v, top_i = lax.top_k(e_sel, MOE_TOP_K)
    top_w = jax.nn.softmax(top_v, axis=-1)
    within = jnp.sum(jax.nn.one_hot(top_i, MOE_EXPERTS_PER_GROUP, dtype=jnp.float32) * top_w[..., None], axis=-2)
    combine = (g_weight[..., None, None]
               * jax.nn.one_hot(g_idx, MOE_GROUPS, dtype=jnp.float32)[..., None]
               * within[:, :, None, :]).astype(h.dtype)
    out = jnp.zeros_like(h)
    for gi in range(MOE_GROUPS):
        hg = jnp.einsum('bsd,edf->bsef', h, w_gate[gi])
        hu = jnp.einsum('bsd,edf->bsef', h, w_up[gi])
        act = jax.nn.silu(hg) * hu * combine[:, :, gi, :, None]
        out = out + jnp.einsum('bsef,efd->bsd', act, w_down[gi])
    return out

def setup_inputs(seed: int = 0) -> dict:
    key = jax.random.key(seed)
    ks = iter(jax.random.split(key, 40))
    nrm = lambda shape, s: jax.random.normal(next(ks), shape, jnp.float32) * s
    L = DEPTH
    x = jax.random.normal(next(ks), (BATCH, SEQ, D_MODEL), jnp.float32)
    p = jax.random.normal(next(ks), (DEPTH, BATCH, SEQ, PLE_DIM), jnp.float32)
    offs = jax.random.randint(next(ks), (BATCH, 1), 0, 64) * CHUNK
    positions = (offs + jnp.arange(SEQ)[None, :]).astype(jnp.int32)
    dt0 = jnp.exp(jax.random.uniform(next(ks), (L, SSD_HEADS)) * (math.log(0.1) - math.log(0.001)) + math.log(0.001))
    ssd_dt_bias = dt0 + jnp.log(-jnp.expm1(-dt0))
    ssd_a_log = jnp.log(jax.random.uniform(next(ks), (L, SSD_HEADS), minval=1.0, maxval=16.0))
    return {
        "x": x, "p": p, "positions": positions,
        "w_in": nrm((L, D_MODEL, N_IN), D_MODEL ** -0.5),
        "ssd_conv_w": nrm((L, SSD_CONV, SSD_CONV_DIM), SSD_CONV ** -0.5),
        "ssd_conv_b": nrm((L, SSD_CONV_DIM), 0.01),
        "ssd_dt_bias": ssd_dt_bias,
        "ssd_a_log": ssd_a_log,
        "ssd_d": 1.0 + nrm((L, SSD_HEADS), 0.1),
        "ssd_norm_w": 1.0 + nrm((L, SSD_INNER), 0.1),
        "attn_sinks": nrm((L, ATTN_Q_HEADS), 1.0),
        "pool_w": nrm((L, POOL_GROUPS, POOL_GROUP_DIM, POOL_GROUP_DIM), POOL_GROUP_DIM ** -0.5),
        "pool_scale": 1.0 + nrm((L, POOL_WIDTH), 0.1),
        "w_branch": nrm((L, N_BRANCHES, BRANCH_WIDTH, D_MODEL), BRANCH_WIDTH ** -0.5),
        "w_out": nrm((L, D_MODEL, D_MODEL), D_MODEL ** -0.5 * DEEPNORM_BETA),
        "ln1_g": 1.0 + nrm((L, D_MODEL), 0.1),
        "ln1_b": nrm((L, D_MODEL), 0.02),
        "router_group_w": nrm((L, D_MODEL, MOE_GROUPS), D_MODEL ** -0.5),
        "router_group_b": nrm((L, MOE_GROUPS), 0.01),
        "router_expert_w": nrm((L, D_MODEL, MOE_GROUPS * MOE_EXPERTS_PER_GROUP), D_MODEL ** -0.5),
        "router_expert_b": nrm((L, MOE_GROUPS * MOE_EXPERTS_PER_GROUP), 0.01),
        "exp_w_gate": nrm((L, MOE_GROUPS, MOE_EXPERTS_PER_GROUP, D_MODEL, MOE_HIDDEN), D_MODEL ** -0.5),
        "exp_w_up": nrm((L, MOE_GROUPS, MOE_EXPERTS_PER_GROUP, D_MODEL, MOE_HIDDEN), D_MODEL ** -0.5),
        "exp_w_down": nrm((L, MOE_GROUPS, MOE_EXPERTS_PER_GROUP, MOE_HIDDEN, D_MODEL), MOE_HIDDEN ** -0.5 * DEEPNORM_BETA),
        "ln2_g": 1.0 + nrm((L, D_MODEL), 0.1),
        "ln2_b": nrm((L, D_MODEL), 0.02),
        "ple_w_proj": nrm((L, PLE_DIM, D_MODEL), PLE_DIM ** -0.5 * DEEPNORM_BETA),
        "ple_w_gate": nrm((L, D_MODEL, D_MODEL), D_MODEL ** -0.5),
        "ln3_g": 1.0 + nrm((L, D_MODEL), 0.1),
        "ln3_b": nrm((L, D_MODEL), 0.02),
    }

def reference(x, p, positions, w_in, ssd_conv_w, ssd_conv_b, ssd_dt_bias, ssd_a_log, ssd_d, ssd_norm_w,
              attn_sinks, pool_w, pool_scale, w_branch, w_out, ln1_g, ln1_b,
              router_group_w, router_group_b, router_expert_w, router_expert_b,
              exp_w_gate, exp_w_up, exp_w_down, ln2_g, ln2_b,
              ple_w_proj, ple_w_gate, ln3_g, ln3_b):
    cos, sin = rope_tables(positions)
    h = x
    for i in range(DEPTH):
        mix = mixing_sublayer(h, cos, sin, w_in[i], ssd_conv_w[i], ssd_conv_b[i], ssd_dt_bias[i],
                              ssd_a_log[i], ssd_d[i], ssd_norm_w[i], attn_sinks[i], pool_w[i],
                              pool_scale[i], w_branch[i], w_out[i])
        h = layer_norm(DEEPNORM_ALPHA * h + mix, ln1_g[i], ln1_b[i])
        ffn = hierarchical_moe(h, router_group_w[i], router_group_b[i], router_expert_w[i],
                               router_expert_b[i], exp_w_gate[i], exp_w_up[i], exp_w_down[i])
        h = layer_norm(DEEPNORM_ALPHA * h + ffn, ln2_g[i], ln2_b[i])
        ple = (p[i] @ ple_w_proj[i]) * jax.nn.sigmoid(h @ ple_w_gate[i])
        h = layer_norm(DEEPNORM_ALPHA * h + ple, ln3_g[i], ln3_b[i])
    return h


_drawn_inputs = setup_inputs


def setup_inputs(seed=0):
    import zlib

    import numpy as np

    out = dict(_drawn_inputs(seed))
    spreads = {}
    factors = {'ssd_conv_b': 8.0,
     'ssd_d': 3.085,
     'attn_sinks': 8.0,
     'router_group_b': 8.0,
     'router_expert_b': 29.331}
    for name, (base, spread) in spreads.items():
        noise = np.random.default_rng([zlib.crc32(name.encode()), seed]).standard_normal(out[name].shape)
        drawn = base * np.exp(spread * noise) if base else spread * noise
        out[name] = __import__('jax').numpy.asarray(drawn.astype(out[name].dtype))
    for name, factor in factors.items():
        out[name] = (out[name] * factor).astype(out[name].dtype)
    return out
```

```python
from contextlib import ExitStack

import numpy as np

import concourse.bass as bass
from concourse import mybir

F32 = mybir.dt.float32
I32 = mybir.dt.int32
ALU = mybir.AluOpType
ACT = mybir.ActivationFunctionType
AX = mybir.AxisListType

P = 128
DEPTH, SEQ, D = 2, 256, 1024
TT = SEQ // P
KT = D // P
HALF = 512
PLE = 256
SSD_HEADS, SSD_P, SSD_GROUPS, SSD_N, SSD_CONV = 16, 64, 4, 128, 4
SSD_R = SSD_HEADS // SSD_GROUPS
GW = SSD_R * SSD_P
XBC = D + 2 * SSD_GROUPS * SSD_N
XBC_T = XBC // P
Q_HEADS, KV_HEADS, HD = 16, 4, 64
ROT = HD // 2
CHUNK = 64
POOL_WINDOWS = (2, 4, 8, 16)
MOE_G, MOE_E = 4, 4
NE = MOE_G * MOE_E
HID = 256
ALPHA = (2.0 * DEPTH) ** 0.25
EPS = 1e-5
NEG = -1e30

COL_Z, COL_XBC = 0, D
COL_DT = COL_XBC + XBC
COL_Q = COL_DT + SSD_HEADS
COL_KV = COL_Q + Q_HEADS * HD
COL_PU = COL_KV + 2 * KV_HEADS * HD
COL_GATE = COL_PU + D

UNITS = (
    [("q", 0), ("q", 1), ("kv", 0), ("pu", 0), ("pu", 1)]
    + [("xbc", n) for n in range(4)] + [("dt", 0), ("pool_w", 0)]
    + [("gate", 4), ("gate", 5), ("branch", 4), ("branch", 5), ("z", 0), ("z", 1)]
    + [("gate", 2), ("gate", 3), ("branch", 2), ("branch", 3)]
    + [("gate", 0), ("gate", 1), ("branch", 0), ("branch", 1), ("out", 0), ("out", 1)]
    + [x for e in range(0, NE, 2) for x in (("gu", e), ("gu", e + 1), ("down", e))]
    + [("ple_proj", 0), ("ple_gate", 0), ("ple_gate", 1)]
)
RING = 3
UNIT_W = 8 * HALF
NU = len(UNITS)
assert NU % RING == 0
UNIT_AT = {u: i for i, u in enumerate(UNITS)}
UNIT_DMAS = 2

ROUNDS = [(0, 0), (1, 0), (0, 1), (1, 1)]
SSD_ROUNDS = [(g, c) for g in range(SSD_GROUPS) for c in range(TT)]


def job_table():
    jobs = []

    def job(name, bank):
        jobs.append((name, bank))

    def pair(name, n):
        for t in range(TT):
            job((name, t), 2 * (n % 2) + t)

    def transposes(name):
        for t in range(TT):
            for j in range(2):
                job((name, t, j), 4 + 2 * t + j)

    transposes("hT1")
    pair("q0", 0)
    pair("q1", 1)
    pair("kv", 0)
    pair("pu0", 1)
    pair("pu1", 0)
    job("vec", 4)
    for t in range(TT):
        job(("qT", t, 0), 5)
        job(("qT", t, 1), 6)
        job(("kT", t), 7)
    pair("xbc0", 1)
    job(("scores", 0, 0), 4)
    job(("scores", 0, 1), 5)
    pair("xbc1", 0)
    pair("xbc2", 1)
    for b in range(4):
        job(("scores", 1, b), 4 + b)
    pair("xbc3", 0)
    job("dt", 2)
    for j in range(4):
        job(("pooled", j), 4 + j)
    for j in range(4):
        job(("mixed", j), 4 + j)
    pair("g_pool0", 0)
    for r in range(4):
        if r == 1:
            pair("g_pool1", 1)
        if r == 2:
            pair("b_pool0", 0)
            pair("b_pool1", 1)
        nb = 2 if r % 2 == 0 else 4
        for b in range(nb):
            job(("PT", r, b), 4 + b)
        for g in range(2):
            job(("PV", r, g), 4 + 2 * (r % 2 == 0) + g)
        if r + 2 < 4:
            for b in range(nb):
                job(("scores", r + 2, b), 4 + b)
    pair("z0", 0)
    pair("z1", 1)
    job("dsum", 4)
    for j in range(4):
        job(("xT", j), 4 + j)
    pair("g_att0", 0)
    pair("g_att1", 1)
    pair("b_att0", 0)
    pair("b_att1", 1)
    for n, (g, c) in enumerate(SSD_ROUNDS):
        if c == 0:
            job(("cb", g), 4)
        job(("seg", n), 5)
        if n >= 1:
            job(("y", n - 1), 6 + (n - 1) % 2)
        if n == 3:
            pair("g_ssd0", 0)
        if n == 6:
            pair("g_ssd1", 1)
    job(("y", len(SSD_ROUNDS) - 1), 7)
    transposes("yT")
    pair("b_ssd0", 0)
    pair("b_ssd1", 1)
    transposes("mT")
    pair("out0", 0)
    pair("out1", 1)
    transposes("hT2")
    job("router", 4)
    for e in range(NE):
        job(("hg", e), 2 * (e % 2))
        job(("hu", e), 2 * (e % 2) + 1)
        if e == 1:
            job("combT", 5)
            for b in range(NE // 2):
                job(("comb", b), 4 + (b + 2) % 4)
    for t in range(TT):
        for j in range(2):
            job(("acc", t, j), 4 + 2 * t + j)
    job("pT", 0)
    for t in range(TT):
        for j in range(2):
            job(("proj", t, j), [1, 2, 3, 0][2 * t + j])
    transposes("hT3")
    pair("pg0", 1)
    pair("pg1", 0)
    return jobs


JOBS = job_table()
NBANK = 8
JOB_AT, BANK_JOBS = {}, [0] * NBANK
for _name, _bank in JOBS:
    assert _name not in JOB_AT, _name
    JOB_AT[_name] = (_bank, BANK_JOBS[_bank])
    BANK_JOBS[_bank] += 1

CONST_COLS = {}
_at = 0
for _n, _w in (("ident", P), ("upto", P), ("after", P), ("mask0", P), ("mask1", 192),
               ("band0", 4 * SEQ), ("band1", 4 * P), ("inv", ROT), ("weight4", 4)):
    CONST_COLS[_n] = (_at, _w)
    _at += _w
NCONST = _at


def shape_constants():
    a, b = np.arange(P)[:, None], np.arange(P)[None, :]
    c = {}
    c["ident"] = a == b
    c["upto"] = a <= b
    c["after"] = a > b
    own = a // CHUNK
    c["mask0"] = np.where((own == 0) & (b // CHUNK == 1), NEG, 0.0)
    k = np.arange(192)[None, :] // CHUNK
    c["mask1"] = np.where(k - own * 1 == 2, NEG, 0.0) + np.where((own == 1) & (k == 0), NEG, 0.0)
    t, s = np.arange(P)[:, None], np.arange(SEQ)[None, :]
    band0, band1 = [], []
    for w in POOL_WINDOWS:
        inside = (t <= s) & (t > s - w)
        band0.append(inside / np.minimum(s + 1, w) - (t == s))
        band1.append(((t <= b) & (t > b - w)) / w - (t == b))
    c["band0"] = np.concatenate(band0, 1)
    c["band1"] = np.concatenate(band1, 1)
    inv = np.float32(10000.0) ** (-np.arange(0, HD, 2, dtype=np.float32) / np.float32(HD))
    c["inv"] = np.broadcast_to(inv[None, :], (P, ROT))
    c["weight4"] = np.broadcast_to(np.array([[4, 3, 2, 1]]), (P, 4))
    out = np.zeros((P, NCONST), np.float32)
    for n, (o, w) in CONST_COLS.items():
        out[:, o:o + w] = c[n]
    return out


VEC_ROWS = SSD_CONV * XBC_T + XBC_T + KT + KT
V_CB = SSD_CONV * XBC_T
V_PS = V_CB + XBC_T
V_NW = V_PS + KT
ROWS = {"dt_bias": (0, 16), "a_log": (16, 16), "d": (32, 16), "sinks": (48, 16), "rb": (64, 20)}
RROW = 84

PARAM_INC = 13 * 16
ROUND = float(3 * 2 ** 22)
TWO_PI = (6.28125, 0.0019350051879882812, 3.019915981956753e-07)
PI_F = 3.1415925
COMBINE = 20
DVE_STEPS = 117


def program(nc, x, p, positions, w_in, conv_w, conv_b, dt_bias, a_log, ssd_d, norm_w, sinks, pool_w,
            pool_scale, w_branch, w_out, ln1_g, ln1_b, rg_w, rg_b, re_w, re_b, w_gate, w_up, w_down,
            ln2_g, ln2_b, ple_proj, ple_gate, ln3_g, ln3_b, consts, out):
    with ExitStack() as ctx:
        def sb(name, shape, dt=F32):
            return ctx.enter_context(nc.sbuf_tensor(name, [P] + shape, dt))

        def sem(name):
            return ctx.enter_context(nc.semaphore(name))

        ring = sb("ring", [RING, UNIT_W])
        cst = sb("cst", [NCONST])
        h = sb("h", [TT, D])
        hT = sb("hT", [KT, SEQ])
        G = sb("G", [2, TT, D])
        xin = sb("xin", [2, 4, 3 + SEQ])
        xconv = sb("xconv", [XBC_T, SEQ])
        xtok = sb("xtok", [TT, D])
        xdt = sb("xdt", [TT, D])
        qT = sb("qT", [KT, SEQ])
        kT = sb("kT", [KV_HEADS, SEQ])
        vv = sb("vv", [TT, KV_HEADS * HD])
        poolT = sb("poolT", [KT, SEQ])
        P0 = sb("P0", [8, P])
        P1 = sb("P1", [8, 2 * P])
        PTs = sb("PTs", [2, 2, 4, P])
        segs = sb("segs", [2, SSD_R, P])
        E = sb("E", [2, SSD_R, P])
        cbm = sb("cbm", [2, 3, P])
        lnp = sb("lnp", [2, D])
        tA = sb("tA", [HALF])
        tB = sb("tB", [HALF])
        attT = xin[:, :, :, :].rearrange("p a b c -> p (a b c)")[:, 0:D * TT].rearrange(
            "p (f s) -> p f s", f=KT)
        xde = P0[:, :, :].rearrange("p a b -> p (a b)")
        pT = PTs[:, 0, 0, :, :].rearrange("p a b -> p (a b)").rearrange("p (k s) -> p k s", k=2)
        combs = PTs[:, 1, 0, :, :].rearrange("p a b -> p (a b)")[:, 0:SEQ]
        act_s = segs[:, :, :].rearrange("p a b c -> p a (b c)")
        act_t = E[:, :, :].rearrange("p a b c -> p a (b c)")
        yT = xconv[:, 0:KT, :]
        comb = xconv
        vecrows = sb("vecrows", [P])
        vecT = sb("vecT", [VEC_ROWS])
        rows = sb("rows", [RROW])
        rw = sb("rw", [KT, 20])
        prow = sb("prow", [TT, PLE])
        posi = sb("posi", [TT], I32)
        posf = sb("posf", [TT])
        cosT = sb("cosT", [TT, ROT])
        sinT = sb("sinT", [TT, ROT])
        nsinT = sb("nsinT", [TT, ROT])
        ang = sb("ang", [4, TT, ROT])
        sm = sb("sm", [12, TT * SSD_HEADS])
        dtv = sb("dtv", [TT, SSD_HEADS])
        dA = sb("dA", [TT, SSD_HEADS])
        nega = sb("nega", [SSD_HEADS])
        dexp = sb("dexp", [2, SSD_HEADS])
        amax = sb("amax", [8, 8])
        gss = sb("gss", [3, TT, SSD_GROUPS])
        stats = sb("stats", [TT, 2, 6])
        mv = sb("mv", [TT, 2])
        rstd = sb("rstd", [2, TT])
        rt = sb("rt", [24, TT, 16])
        bank = [ctx.enter_context(nc.psum_tensor(f"bank{i}", [P, HALF], F32)) for i in range(NBANK)]

        def const(name):
            o, w = CONST_COLS[name]
            return cst[:, o:o + w]

        ident, upto, after = const("ident"), const("upto"), const("after")
        band0 = const("band0").rearrange("p (w s) -> p w s", w=4)
        weight4 = const("weight4")
        band1 = const("band1").rearrange("p (w s) -> p w s", w=4)

        unit_full = [sem(f"unit_full{s}") for s in range(RING)]
        unit_free = sem("unit_free")
        bank_full = [sem(f"bank_full{b}") for b in range(NBANK)]
        bank_free = [sem(f"bank_free{b}") for b in range(NBANK)]
        start_loads = sem("start_loads")
        dve_step = sem("dve_step")
        pos_loaded = sem("pos_loaded")
        sines_done = sem("sines_done")
        angles_ready = sem("angles_ready")
        params_full = sem("params_full")
        params_free = sem("params_free")
        lnp_full = sem("lnp_full")
        lnp_free = sem("lnp_free")
        h_ready = sem("h_ready")
        qrot_ready = sem("qrot_ready")
        conv_done = sem("conv_done")
        silu_done = sem("silu_done")
        probs_ready = sem("probs_ready")
        scores_ready = sem("scores_ready")
        exp_done = sem("exp_done")
        dt_pre = sem("dt_pre")
        dt_exp = sem("dt_exp")
        dA_ready = sem("dA_ready")
        dsum_exp = sem("dsum_exp")
        xdt_ready = sem("xdt_ready")
        seg_built = sem("seg_built")
        seg_exp = sem("seg_exp")
        decay_ready = sem("decay_ready")
        merge_step = sem("merge_step")
        gy_ms = sem("gy_ms")
        gy_sqrt = sem("gy_sqrt")
        ssd_ready = sem("ssd_ready")
        merged_ready = sem("merged_ready")
        var_ready = sem("var_ready")
        sqrt_done = sem("sqrt_done")
        rexp_in = sem("rexp_in")
        rexp_out = sem("rexp_out")
        combine_ready = sem("combine_ready")
        hsilu_done = sem("hsilu_done")
        act_ready = sem("act_ready")
        stored = sem("stored")
        passed_wait = sem("passed_wait")

        def full(name, L):
            b, k = JOB_AT[name]
            return bank_full[b], L * BANK_JOBS[b] + (k + 1)

        def free(name, L):
            b, k = JOB_AT[name]
            return bank_free[b], L * BANK_JOBS[b] + (k + 1)

        def taken(name, L):
            b, k = JOB_AT[name]
            return bank_free[b], L * BANK_JOBS[b] + (k + 2)

        def ps(name):
            return bank[JOB_AT[name][0]]

        def slot(unit):
            return ring[:, UNIT_AT[unit] % RING, :]

        block = ctx.enter_context(nc.Block())

        @block.sync
        def _(sp):
            sp.dma_start(cst[:], consts).then_inc(start_loads, 16)
            for t in range(TT):
                sp.dma_start(h[:, t, :], x[0, t * P:(t + 1) * P, :]).then_inc(start_loads, 16)
            with sp.Fori(0, DEPTH) as L:
                for u, (kind, n) in enumerate(UNITS):
                    dst = ring[:, u % RING, :]
                    k8 = dst.rearrange("p (k n) -> p k n", k=KT)
                    sp.wait_ge(unit_free, L * NU + (u + 1))
                    sp.sem_inc(passed_wait, 1)
                    pairs = []
                    if kind in ("q", "kv", "pu", "xbc", "gate", "z", "dt"):
                        col = {"q": COL_Q, "kv": COL_KV, "pu": COL_PU, "xbc": COL_XBC,
                               "gate": COL_GATE, "z": COL_Z, "dt": COL_DT}[kind] + n * HALF
                        w = SSD_HEADS if kind == "dt" else HALF
                        src = w_in[L].rearrange("(k p) n -> p k n", p=P)[:, :, col:col + w]
                        pairs = [(k8[:, 0:4, 0:w], src[:, 0:4]), (k8[:, 4:8, 0:w], src[:, 4:8])]
                    elif kind in ("branch", "out", "ple_gate"):
                        m = {"branch": w_branch, "out": w_out, "ple_gate": ple_gate}[kind]
                        m = m[L, n // 2] if kind == "branch" else m[L]
                        c = (n % 2) * HALF
                        src = m.rearrange("(k p) n -> p k n", p=P)[:, :, c:c + HALF]
                        pairs = [(k8[:, 0:4, :], src[:, 0:4]), (k8[:, 4:8, :], src[:, 4:8])]
                    elif kind == "gu":
                        for i, m in enumerate((w_gate, w_up)):
                            pairs.append((dst[:, i * 2048:(i + 1) * 2048].rearrange("p (k n) -> p k n", k=KT),
                                          m[L, n // 4, n % 4].rearrange("(k p) n -> p k n", p=P)))
                    elif kind == "down":
                        for i in range(2):
                            e = n + i
                            pairs.append((dst[:, i * 2048:(i + 1) * 2048].rearrange("p (k n) -> p k n", k=2),
                                          w_down[L, e // 4, e % 4].rearrange("(k p) n -> p k n", p=P)))
                    elif kind == "pool_w":
                        for i in range(2):
                            pairs.append((dst[:, i * 1024:(i + 1) * 1024].rearrange("p (g k n) -> p g k n", g=2, k=2),
                                          pool_w[L, 2 * i:2 * i + 2].rearrange("g (k p) n -> p g k n", p=P)))
                    elif kind == "ple_proj":
                        for i in range(2):
                            pairs.append((dst[:, i * D:(i + 1) * D], ple_proj[L, i * P:(i + 1) * P, :]))
                    for d, s in pairs:
                        sp.dma_start(d, s).then_inc(unit_full[u % RING], 16)
            for t in range(TT):
                sp.wait_ge(h_ready, 6 * DEPTH + 1 + t)
                sp.dma_start(out[0, t * P:(t + 1) * P, :], h[:, t, :]).then_inc(stored, 16)
            sp.wait_ge(stored, 32)

        @block.tensor
        def _(pe):
            mm, tr = nc.tensor.matmul, nc.tensor.transpose

            def done(ins, name):
                ins.then_inc(bank_full[JOB_AT[name][0]], 1)

            pe.sem_inc(unit_free, RING)
            for b in range(NBANK):
                pe.sem_inc(bank_free[b], 1)
            pe.wait_ge(start_loads, 48)
            with pe.Fori(0, DEPTH) as L:

                def arrived(unit):
                    u = UNIT_AT[unit]
                    pe.wait_ge(unit_full[u % RING], L * (NU // RING * 32) + 32 * (u // RING + 1))

                def transposes(name, src, ready):
                    for t in range(TT):
                        pe.wait_ge(*ready(t))
                        for j in range(2):
                            pe.wait_ge(*free((name, t, j), L))
                            for i in range(4):
                                f = (4 * j + i) * P
                                last = tr(ps((name, t, j))[:, i * P:(i + 1) * P], src[:, t, f:f + P], ident)
                            done(last, (name, t, j))

                def tokens(name, unit, lhs, lhs_ready=None):
                    arrived(unit)
                    w = slot(unit).rearrange("p (k n) -> p k n", k=KT)
                    for t in range(TT):
                        if lhs_ready is not None:
                            pe.wait_ge(*lhs_ready(t))
                        pe.wait_ge(*free((name, t), L))
                        for k in range(KT):
                            last = mm(ps((name, t))[:, :], lhs[:, k, t * P:(t + 1) * P], w[:, k, :],
                                      start=k == 0, stop=k == KT - 1)
                        done(last, (name, t))
                    last_of_unit(last)

                def last_of_unit(ins):
                    pe.drain().then_inc(unit_free, 1)

                def features(name, unit):
                    arrived(unit)
                    w = slot(unit).rearrange("p (k n) -> p k n", k=KT)
                    for b in range(2):
                        pe.wait_ge(*free((name, b), L))
                        for i in range(2):
                            f = (2 * b + i) * P
                            for k in range(KT):
                                last = mm(ps((name, b))[:, i * SEQ:(i + 1) * SEQ], w[:, k, f:f + P],
                                          hT[:, k, :], start=k == 0, stop=k == KT - 1)
                        done(last, (name, b))
                    last_of_unit(last)

                def qk_transposes(t):
                    pe.wait_ge(qrot_ready, L * TT + (t + 1))
                    rot = G[:, t, :, :].rearrange("p a b -> p (a b)")
                    for n, name in enumerate((("qT", t, 0), ("qT", t, 1), ("kT", t))):
                        pe.wait_ge(*free(name, L))
                        for i in range(4):
                            last = tr(ps(name)[:, i * P:(i + 1) * P],
                                      rot[:, (4 * n + i) * P:(4 * n + i + 1) * P], ident)
                        done(last, name)

                def scores(r):
                    t, half = ROUNDS[r]
                    per = 4 if t == 0 else 2
                    pe.wait_ge(*taken(("kT", 1), L))
                    for b in range(8 // per):
                        pe.wait_ge(*free(("scores", r, b), L))
                        for i in range(per):
                            head = 8 * half + (2 * i + b if t == 0 else 4 * (b // 2) + 2 * i + b % 2)
                            q0 = HD * (head % 2)
                            if t == 0:
                                o = ps(("scores", r, b))[:, i * P:(i + 1) * P]
                                keys = slice(0, P)
                            else:
                                o = ps(("scores", r, b))[:, i * 256:i * 256 + 192]
                                keys = slice(CHUNK, SEQ)
                            last = mm(o, qT[q0:q0 + HD, head // 2, t * P:(t + 1) * P],
                                      kT[q0:q0 + HD, head // 4, keys], start=True, stop=True)
                        done(last, ("scores", r, b))

                def probs_transposes(r):
                    t, half = ROUNDS[r]
                    pe.wait_ge(probs_ready, L * 4 + (r + 1))
                    for b in range(2 if t == 0 else 4):
                        name = ("PT", r, b)
                        pe.wait_ge(*free(name, L))
                        for i in range(4):
                            src = P0[:, 4 * b + i, :] if t == 0 else \
                                P1[:, 4 * (b // 2) + i, (b % 2) * P:(b % 2 + 1) * P]
                            last = tr(ps(name)[:, i * P:(i + 1) * P], src, ident)
                        done(last, name)

                def values(r):
                    t, half = ROUNDS[r]
                    for g in range(2):
                        name = ("PV", r, g)
                        kv = 2 * half + g
                        pe.wait_ge(*free(name, L))
                        for kb in range(t + 1):
                            b = g if t == 0 else 2 * g + kb
                            pe.wait_ge(*taken(("PT", r, b), L))
                            last = mm(ps(name)[0:HD, :], vv[:, kb, kv * HD:(kv + 1) * HD],
                                      PTs[:, b // 2, b % 2, :, :].rearrange("p a b -> p (a b)") if t else
                                      PTs[:, 0, b, :, :].rearrange("p a b -> p (a b)"),
                                      start=kb == 0, stop=kb == t)
                        done(last, name)

                transposes("hT1", h, lambda t: (h_ready, L * 6 + (t + 1)))
                pe.wait_ge(*taken(("hT1", 1, 1), L))
                tokens("q0", ("q", 0), hT)
                tokens("q1", ("q", 1), hT)
                tokens("kv", ("kv", 0), hT)
                tokens("pu0", ("pu", 0), hT)
                tokens("pu1", ("pu", 1), hT)

                pe.wait_ge(params_full, L * PARAM_INC + PARAM_INC)
                pe.wait_ge(*free("vec", L))
                done(tr(ps("vec")[:, 0:VEC_ROWS], vecrows[0:VEC_ROWS, :], ident[0:VEC_ROWS, 0:VEC_ROWS]), "vec")
                for t in range(TT):
                    qk_transposes(t)
                features("xbc0", ("xbc", 0))
                scores(0)
                features("xbc1", ("xbc", 1))
                features("xbc2", ("xbc", 2))
                scores(1)
                features("xbc3", ("xbc", 3))

                arrived(("dt", 0))
                pe.wait_ge(*free("dt", L))
                w = slot(("dt", 0)).rearrange("p (k n) -> p k n", k=KT)
                for t in range(TT):
                    for k in range(KT):
                        last = mm(ps("dt")[:, t * 16:(t + 1) * 16], hT[:, k, t * P:(t + 1) * P],
                                  w[:, k, 0:SSD_HEADS], start=k == 0, stop=k == KT - 1)
                done(last, "dt")
                last_of_unit(last)

                pe.wait_ge(*taken(("pu1", 1), L))
                for j in range(4):
                    pe.wait_ge(*free(("pooled", j), L))
                    for i in range(2):
                        f = 2 * j + i
                        o = ps(("pooled", j))[:, i * SEQ:(i + 1) * SEQ]
                        mm(o[:, 0:P], xtok[:, 0, f * P:(f + 1) * P], band0[:, j, 0:P], start=True, stop=True)
                        mm(o[:, P:SEQ], xtok[:, 0, f * P:(f + 1) * P], band0[:, j, P:SEQ], start=True, stop=False)
                        last = mm(o[:, P:SEQ], xtok[:, 1, f * P:(f + 1) * P], band1[:, j, :],
                                  start=False, stop=True)
                    done(last, ("pooled", j))
                arrived(("pool_w", 0))
                w = slot(("pool_w", 0))[:, 0:2048].rearrange("p (g k n) -> p g k n", g=4, k=2)
                pooled = xdt[:, :, :].rearrange("p a b -> p (a b)").rearrange("p (f s) -> p f s", f=KT)
                for j in range(4):
                    pe.wait_ge(*taken(("pooled", j), L))
                    pe.wait_ge(*free(("mixed", j), L))
                    for i in range(2):
                        for k in range(2):
                            last = mm(ps(("mixed", j))[:, i * SEQ:(i + 1) * SEQ], w[:, j, k, i * P:(i + 1) * P],
                                      pooled[:, 2 * j + k, :], start=k == 0, stop=k == 1)
                    done(last, ("mixed", j))
                last_of_unit(last)

                tokens("g_pool0", ("gate", 4), hT)
                probs_transposes(0)
                values(0)
                scores(2)
                tokens("g_pool1", ("gate", 5), hT)
                probs_transposes(1)
                values(1)
                scores(3)
                pe.wait_ge(*taken(("mixed", 3), L))
                tokens("b_pool0", ("branch", 4), poolT)
                tokens("b_pool1", ("branch", 5), poolT)
                probs_transposes(2)
                values(2)
                probs_transposes(3)
                values(3)
                tokens("z0", ("z", 0), hT)
                tokens("z1", ("z", 1), hT)

                pe.wait_ge(dA_ready, L + 1)
                pe.wait_ge(*free("dsum", L))
                mm(ps("dsum")[:, 0:16], after, dA[:, 0, :], start=True, stop=True)
                done(mm(ps("dsum")[:, 16:32], upto, dA[:, 1, :], start=True, stop=True), "dsum")
                pe.wait_ge(silu_done, L * 4 + 4)
                for j in range(4):
                    t, half = j // 2, j % 2
                    pe.wait_ge(*free(("xT", j), L))
                    for i in range(4):
                        last = tr(ps(("xT", j))[:, i * P:(i + 1) * P],
                                  xconv[:, 4 * half + i, t * P:(t + 1) * P], ident)
                    done(last, ("xT", j))
                tokens("g_att0", ("gate", 2), hT)
                tokens("g_att1", ("gate", 3), hT)
                pe.wait_ge(*taken(("PV", 3, 1), L))
                tokens("b_att0", ("branch", 2), attT)
                tokens("b_att1", ("branch", 3), attT)

                def y(n):
                    g, c = SSD_ROUNDS[n]
                    pe.wait_ge(decay_ready, L * 8 + (n + 1))
                    pe.wait_ge(*free(("y", n), L))
                    for r in range(SSD_R):
                        hd = SSD_R * g + r
                        last = mm(ps(("y", n))[:, r * SSD_P:(r + 1) * SSD_P], E[:, n % 2, r, :],
                                  xdt[:, c, hd * SSD_P:(hd + 1) * SSD_P], start=True, stop=True)
                    if c == 1:
                        last = mm(ps(("y", n))[:, GW:2 * GW], cbm[:, g % 2, 2, :],
                                  xde[:, g * GW:(g + 1) * GW], start=True, stop=True)
                    done(last, ("y", n))

                pe.wait_ge(xdt_ready, L + 1)
                for n, (g, c) in enumerate(SSD_ROUNDS):
                    if c == 0:
                        pe.wait_ge(*free(("cb", g), L))
                        for i, (s, l) in enumerate(((0, 0), (1, 1), (0, 1))):
                            last = mm(ps(("cb", g))[:, i * P:(i + 1) * P], xconv[:, 8 + g, s * P:(s + 1) * P],
                                      xconv[:, 12 + g, l * P:(l + 1) * P], start=True, stop=True)
                        done(last, ("cb", g))
                    pe.wait_ge(seg_built, L * 8 + (n + 1))
                    pe.wait_ge(*free(("seg", n), L))
                    for r in range(SSD_R):
                        last = mm(ps(("seg", n))[:, r * P:(r + 1) * P], segs[:, n % 2, r, :], upto,
                                  start=True, stop=True)
                    done(last, ("seg", n))
                    if n >= 1:
                        y(n - 1)
                    if n == 3:
                        tokens("g_ssd0", ("gate", 0), hT)
                    if n == 6:
                        tokens("g_ssd1", ("gate", 1), hT)
                y(len(SSD_ROUNDS) - 1)
                transposes("yT", xtok, lambda t: (ssd_ready, L * TT + (t + 1)))
                pe.wait_ge(*taken(("yT", 1, 1), L))
                tokens("b_ssd0", ("branch", 0), yT)
                tokens("b_ssd1", ("branch", 1), yT)
                transposes("mT", G[:, 0, :, :], lambda t: (merged_ready, L * TT + (t + 1)))
                pe.wait_ge(*taken(("mT", 1, 1), L))
                tokens("out0", ("out", 0), hT)
                tokens("out1", ("out", 1), hT)

                transposes("hT2", h, lambda t: (h_ready, L * 6 + (t + 3)))
                pe.wait_ge(*taken(("hT2", 1, 1), L))
                pe.wait_ge(*free("router", L))
                for t in range(TT):
                    for k in range(KT):
                        last = mm(ps("router")[:, t * 20:(t + 1) * 20], hT[:, k, t * P:(t + 1) * P],
                                  rw[:, k, :], start=k == 0, stop=k == KT - 1)
                done(last, "router")

                def gate_up(e):
                    arrived(("gu", e))
                    for i, name in enumerate((("hg", e), ("hu", e))):
                        w = slot(("gu", e))[:, i * 2048:(i + 1) * 2048].rearrange("p (k n) -> p k n", k=KT)
                        pe.wait_ge(*free(name, L))
                        for f in range(2):
                            for k in range(KT):
                                last = mm(ps(name)[:, f * SEQ:(f + 1) * SEQ], w[:, k, f * P:(f + 1) * P],
                                          hT[:, k, :], start=k == 0, stop=k == KT - 1)
                        done(last, name)
                    last_of_unit(last)

                for e in range(0, NE, 2):
                    gate_up(e)
                    gate_up(e + 1)
                    if e == 0:
                        pe.wait_ge(combine_ready, L + 1)
                        pe.wait_ge(*free("combT", L))
                        for t in range(TT):
                            last = tr(ps("combT")[0:NE, t * P:(t + 1) * P], rt[:, COMBINE, t, :], ident)
                        done(last, "combT")
                        pe.wait_ge(*taken("combT", L))
                        for b in range(NE // 2):
                            pe.wait_ge(*free(("comb", b), L))
                            for i in range(2):
                                x1 = 2 * b + i
                                last = mm(ps(("comb", b))[:, i * SEQ:(i + 1) * SEQ],
                                          ident[0:NE, x1:x1 + 1].to_broadcast([NE, P]), combs[0:NE, :],
                                          start=True, stop=True)
                            done(last, ("comb", b))
                        for t in range(TT):
                            for j in range(2):
                                pe.wait_ge(*free(("acc", t, j), L))
                    arrived(("down", e))
                    for i in range(2):
                        w = slot(("down", e))[:, i * 2048:(i + 1) * 2048].rearrange("p (k n) -> p k n", k=2)
                        pe.wait_ge(act_ready, L * NE + (e + i + 1))
                        for t in range(TT):
                            for j in range(2):
                                for k in range(2):
                                    last = mm(ps(("acc", t, j))[:, :],
                                              act_t[:, i, k * SEQ + t * P:k * SEQ + (t + 1) * P],
                                              w[:, k, j * HALF:(j + 1) * HALF],
                                              start=e + i + k == 0, stop=e + i + k == NE)
                                if e + i == NE - 1:
                                    done(last, ("acc", t, j))
                    last_of_unit(last)

                pe.wait_ge(*free("pT", L))
                for k in range(2):
                    for t in range(TT):
                        last = tr(ps("pT")[:, k * SEQ + t * P:k * SEQ + (t + 1) * P],
                                  prow[:, t, k * P:(k + 1) * P], ident)
                done(last, "pT")
                arrived(("ple_proj", 0))
                w = slot(("ple_proj", 0))[:, 0:2 * D].rearrange("p (k n) -> p k n", k=2)
                pe.wait_ge(*taken("pT", L))
                for t in range(TT):
                    for j in range(2):
                        name = ("proj", t, j)
                        pe.wait_ge(*free(name, L))
                        for k in range(2):
                            last = mm(ps(name)[:, :], pT[:, k, t * P:(t + 1) * P],
                                      w[:, k, j * HALF:(j + 1) * HALF], start=k == 0, stop=k == 1)
                        done(last, name)
                last_of_unit(last)
                transposes("hT3", h, lambda t: (h_ready, L * 6 + (t + 5)))
                pe.wait_ge(*taken(("hT3", 1, 1), L))
                tokens("pg0", ("ple_gate", 0), hT)
                tokens("pg1", ("ple_gate", 1), hT)

        @block.scalar
        def _(act):
            def ev(out_, name, L, func=ACT.Copy, in_=None, last=True, **kw):
                ins = nc.scalar.activation(out_, ps(name)[:, :] if in_ is None else in_, func, **kw)
                if last:
                    ins.then_inc(bank_free[JOB_AT[name][0]], 1)

            act.wait_ge(angles_ready, 1)
            nc.scalar.activation(sinT[:], ang[:, 2], ACT.Sin)
            nc.scalar.activation(cosT[:], ang[:, 3], ACT.Sin).then_inc(sines_done, 1)
            with act.Fori(0, DEPTH) as L:

                def evict_transposed(name, dst):
                    for t in range(TT):
                        for j in range(2):
                            act.wait_ge(*full((name, t, j), L))
                            ev(dst[:, 4 * j:4 * j + 4, t * P:(t + 1) * P], (name, t, j), L,
                               in_=ps((name, t, j)).rearrange("p (a b) -> p a b", a=4))

                def evict_pair(name, n, dst, func):
                    for t in range(TT):
                        act.wait_ge(*full((name, t), L))
                        ev(dst[:, t, n * HALF:(n + 1) * HALF], (name, t), L, func)

                def xbc(n):
                    for b in range(2):
                        act.wait_ge(*full((f"xbc{n}", b), L))
                        if n >= 2 and b == 0:
                            act.wait_ge(conv_done, L * 4 + (n - 1))
                        ev(xin[:, n % 2, 2 * b:2 * b + 2, 3:3 + SEQ], (f"xbc{n}", b), L,
                           in_=ps((f"xbc{n}", b)).rearrange("p (a b) -> p a b", a=2))

                def silu(n):
                    act.wait_ge(conv_done, L * 4 + (n + 1))
                    v = xconv[:, 4 * n:4 * n + 4, :]
                    nc.scalar.activation(v, v, ACT.Silu).then_inc(silu_done, 1)

                def exp_scores(r):
                    t, _ = ROUNDS[r]
                    act.wait_ge(scores_ready, L * 4 + (r + 1))
                    v = P0[:, :, :] if t == 0 else P1[:, :, CHUNK:SEQ]
                    nc.scalar.activation(amax[:, 3 + (r % 2), :], amax[:, 1 + (r % 2), :], ACT.Exp)
                    nc.scalar.activation(v, v, ACT.Exp).then_inc(exp_done, 1)

                def probs_values(r):
                    t, half = ROUNDS[r]
                    for b in range(2 if t == 0 else 4):
                        act.wait_ge(*full(("PT", r, b), L))
                        o = PTs[:, 0, b] if t == 0 else PTs[:, b // 2, b % 2]
                        ev(o.rearrange("p a b -> p (a b)"), ("PT", r, b), L)
                    for g in range(2):
                        act.wait_ge(*full(("PV", r, g), L))
                        v = ps(("PV", r, g))[0:HD, :].rearrange("p (a b c) -> p a b c", a=2, b=2)
                        f = 4 * half + 2 * g
                        for b in range(2):
                            ev(attT[b * HD:(b + 1) * HD, f:f + 2, t * P:(t + 1) * P], ("PV", r, g), L,
                               in_=v[:, :, b, :], last=b == 1)

                evict_transposed("hT1", hT)
                evict_pair("pu0", 0, xtok, ACT.Copy)
                evict_pair("pu1", 1, xtok, ACT.Copy)
                for t in range(TT):
                    for j in range(2):
                        act.wait_ge(*full(("qT", t, j), L))
                        ev(qT[:, 4 * j:4 * j + 4, t * P:(t + 1) * P], ("qT", t, j), L,
                           in_=ps(("qT", t, j)).rearrange("p (a b) -> p a b", a=4))
                    act.wait_ge(*full(("kT", t), L))
                    ev(kT[:, :, t * P:(t + 1) * P], ("kT", t), L,
                       in_=ps(("kT", t)).rearrange("p (a b) -> p a b", a=4))
                xbc(0)
                xbc(1)
                silu(0)
                xbc(2)
                silu(1)
                xbc(3)
                silu(2)
                silu(3)
                act.wait_ge(dt_pre, L + 1)
                nc.scalar.activation(sm[:, 2, :], sm[:, 1, :], ACT.Exp, scale=-1.0)
                nc.scalar.activation(sm[:, 3, 0:16], rows[:, 16:32], ACT.Exp).then_inc(dt_exp, 1)
                exp_scores(0)
                exp_scores(1)
                pooled = xdt[:, :, :].rearrange("p a b -> p (a b)")
                for j in range(4):
                    act.wait_ge(*full(("pooled", j), L))
                    ev(pooled[:, j * HALF:(j + 1) * HALF], ("pooled", j), L)
                for j in range(4):
                    act.wait_ge(*full(("mixed", j), L))
                    for i in range(2):
                        f = 2 * j + i
                        ev(poolT[:, f, :], ("mixed", j), L, in_=ps(("mixed", j))[:, i * SEQ:(i + 1) * SEQ],
                           scale=vecT[:, V_PS + f:V_PS + f + 1], last=i == 1)
                evict_pair("g_pool0", 0, G[:, 0], ACT.Sigmoid)
                probs_values(0)
                evict_pair("g_pool1", 1, G[:, 0], ACT.Sigmoid)
                probs_values(1)
                exp_scores(2)
                probs_values(2)
                exp_scores(3)
                probs_values(3)
                zs = qT[:, :, :].rearrange("p a b -> p (a b)").rearrange("p (t d) -> p t d", t=TT)
                evict_pair("z0", 0, zs, ACT.Silu)
                evict_pair("z1", 1, zs, ACT.Silu)
                act.wait_ge(*full("dsum", L))
                ev(dexp[:, :, :], "dsum", L, ACT.Exp,
                   in_=ps("dsum")[:, 0:32].rearrange("p (a b) -> p a b", a=2))
                for j in range(4):
                    act.wait_ge(*full(("xT", j), L))
                    ev(xtok[:, j // 2, (j % 2) * HALF:(j % 2 + 1) * HALF], ("xT", j), L)
                evict_pair("g_att0", 0, G[:, 1], ACT.Sigmoid)
                evict_pair("g_att1", 1, G[:, 1], ACT.Sigmoid)
                for n in range(len(SSD_ROUNDS)):
                    act.wait_ge(*full(("seg", n), L))
                    ev(E[:, n % 2, :, :].rearrange("p a b -> p (a b)"), ("seg", n), L, ACT.Exp)
                    if n == 3:
                        act.wait_ge(merge_step, L * 2 + 2)
                        evict_pair("g_ssd0", 0, G[:, 1], ACT.Sigmoid)
                    if n == 6:
                        evict_pair("g_ssd1", 1, G[:, 1], ACT.Sigmoid)
                act.wait_ge(gy_ms, L + 1)
                nc.scalar.activation(gss[:, 1], gss[:, 0], ACT.Sqrt).then_inc(gy_sqrt, 1)
                for t in range(TT):
                    for j in range(2):
                        act.wait_ge(*full(("yT", t, j), L))
                        for i in range(4):
                            f = 4 * j + i
                            ev(yT[:, f, t * P:(t + 1) * P], ("yT", t, j), L,
                               in_=ps(("yT", t, j))[:, i * P:(i + 1) * P],
                               scale=vecT[:, V_NW + f:V_NW + f + 1], last=i == 3)
                evict_transposed("mT", hT)

                def ln_sqrt(i):
                    for t in range(TT):
                        act.wait_ge(var_ready, L * 6 + (2 * i + t + 1))
                        nc.scalar.activation(rstd[:, 0, t:t + 1], mv[:, t, 1:2], ACT.Sqrt).then_inc(sqrt_done, 1)

                ln_sqrt(0)
                evict_transposed("hT2", hT)
                act.wait_ge(rexp_in, L * 2 + 1)
                nc.scalar.activation(rt[:, 3, :, 0:4], rt[:, 2, :, 0:4], ACT.Exp).then_inc(rexp_out, 1)
                act.wait_ge(rexp_in, L * 2 + 2)
                nc.scalar.activation(rt[:, 12, :, 0:1], rt[:, 11, :, 0:1], ACT.Exp).then_inc(rexp_out, 1)

                def hsilu(e):
                    act.wait_ge(*full(("hg", e), L))
                    if e >= 2:
                        act.wait_ge(act_ready, L * NE + (e - 1))
                    ev(act_s[:, e % 2, :], ("hg", e), L, ACT.Silu)

                hsilu(0)
                hsilu(1)
                act.wait_ge(*full("combT", L))
                ev(combs[0:NE, :], "combT", L, in_=ps("combT")[0:NE, 0:SEQ])
                for b in range(NE // 2):
                    act.wait_ge(*full(("comb", b), L))
                    ev(comb[:, 2 * b:2 * b + 2, :].rearrange("p a b -> p (a b)"), ("comb", b), L)
                for e in range(2, NE):
                    hsilu(e)
                act.wait_ge(*full("pT", L))
                ev(PTs[:, 0, 0, :, :].rearrange("p a b -> p (a b)"), "pT", L)
                for t in range(TT):
                    for j in range(2):
                        act.wait_ge(*full(("proj", t, j), L))
                        ev(xtok[:, t, j * HALF:(j + 1) * HALF], ("proj", t, j), L)
                ln_sqrt(1)
                evict_transposed("hT3", hT)
                evict_pair("pg0", 0, G[:, 0], ACT.Sigmoid)
                evict_pair("pg1", 1, G[:, 0], ACT.Sigmoid)
                ln_sqrt(2)

        @block.gpsimd
        def _(pool):
            with nc.allow_non_contiguous_dma(reason="256 positions, once"):
                pool.dma_start(posi[:], positions[0].rearrange("(t p) -> p t", p=P)).then_inc(pos_loaded, 16)
            with pool.Fori(0, DEPTH) as L:
                pool.wait_ge(params_free, L + 1)
                pool.sem_inc(passed_wait, 1)
                T = XBC_T
                loads = [
                    (vecrows[0:SSD_CONV * T, :], conv_w[L].rearrange("k (c p) -> (k c) p", p=P)),
                    (vecrows[V_CB:V_CB + T, :], conv_b[L].rearrange("(c p) -> c p", p=P)),
                    (vecrows[V_PS:V_PS + KT, :], pool_scale[L].rearrange("(c p) -> c p", p=P)),
                    (vecrows[V_NW:V_NW + KT, :], norm_w[L].rearrange("(c p) -> c p", p=P)),
                    (rows[:, 0:16], dt_bias[L].unsqueeze(0).broadcast_to([P, 16])),
                    (rows[:, 16:32], a_log[L].unsqueeze(0).broadcast_to([P, 16])),
                    (rows[:, 32:48], ssd_d[L].unsqueeze(0).broadcast_to([P, 16])),
                    (rows[:, 48:64], sinks[L].unsqueeze(0).broadcast_to([P, 16])),
                    (rows[:, 64:68], rg_b[L].unsqueeze(0).broadcast_to([P, 4])),
                    (rows[:, 68:84], re_b[L].unsqueeze(0).broadcast_to([P, 16])),
                    (rw[:, :, 0:4], rg_w[L].rearrange("(k p) n -> p k n", p=P)),
                    (rw[:, :, 4:20], re_w[L].rearrange("(k p) n -> p k n", p=P)),
                    (prow[:, :, :], p[L, 0].rearrange("(t p) n -> p t n", p=P)),
                ]
                assert 16 * len(loads) == PARAM_INC
                for d, s in loads:
                    pool.dma_start(d, s).then_inc(params_full, 16)

                def ln_params(i, g, b):
                    pool.wait_ge(lnp_free, L * 3 + (i + 1))
                    pool.sem_inc(passed_wait, 1)
                    for j, v in enumerate((g, b)):
                        pool.dma_start(lnp[:, j, :], v[L].unsqueeze(0).broadcast_to([P, D])).then_inc(lnp_full, 16)

                ln_params(0, ln1_g, ln1_b)
                pool.wait_ge(dA_ready, L + 1)
                for n, (g, c) in enumerate(SSD_ROUNDS):
                    if n >= 2:
                        pool.wait_ge(*full(("seg", n - 2), L))
                    nc.gpsimd.tensor_tensor(
                        segs[:, n % 2, :, :], after.unsqueeze(1).broadcast_to([P, SSD_R, P]),
                        dA[:, c, SSD_R * g:SSD_R * (g + 1)].unsqueeze(2).broadcast_to([P, SSD_R, P]),
                        ALU.mult).then_inc(seg_built, 1)
                ln_params(1, ln2_g, ln2_b)
                ln_params(2, ln3_g, ln3_b)

        @block.vector
        def _(dve):
            V = nc.vector
            steps = [0]

            def link(ins, base):
                steps[0] += 1
                ins.then_inc(dve_step, 1)
                dve.wait_ge(dve_step, base + steps[0])

            def frees(ins, name):
                ins.then_inc(bank_free[JOB_AT[name][0]], 1)

            V.memset(P1[:, :, 0:CHUNK], 0.0)
            dve.wait_ge(start_loads, 48)
            dve.wait_ge(pos_loaded, 16)
            link(V.tensor_copy(posf[:], posi[:]), 0)
            for t in range(TT):
                last = V.tensor_scalar(ang[:, 0, t, :], const("inv"), posf[:, t:t + 1], None, ALU.mult)
            link(last, 0)
            link(V.tensor_scalar(ang[:, 1], ang[:, 0], float(1 / (2 * np.pi)), None, ALU.mult), 0)
            link(V.tensor_scalar(ang[:, 1], ang[:, 1], ROUND, None, ALU.add), 0)
            link(V.tensor_scalar(ang[:, 1], ang[:, 1], -ROUND, None, ALU.add), 0)
            link(V.scalar_tensor_tensor(out=ang[:, 2], in0=ang[:, 1], scalar=-TWO_PI[0], in1=ang[:, 0],
                                        op0=ALU.mult, op1=ALU.add), 0)
            for part in TWO_PI[1:]:
                link(V.scalar_tensor_tensor(out=ang[:, 2], in0=ang[:, 1], scalar=-part, in1=ang[:, 2],
                                            op0=ALU.mult, op1=ALU.add), 0)
            link(V.tensor_scalar(ang[:, 2], ang[:, 2], PI_F, -PI_F, ALU.min, ALU.max), 0)
            link(V.tensor_scalar(ang[:, 3], ang[:, 2], float(np.pi / 2), None, ALU.add), 0)
            link(V.tensor_scalar(ang[:, 1], ang[:, 3], PI_F, float(-2 * np.pi), ALU.is_gt, ALU.mult), 0)
            link(V.tensor_tensor(ang[:, 3], ang[:, 3], ang[:, 1], ALU.add), 0)
            V.tensor_scalar(ang[:, 3], ang[:, 3], PI_F, -PI_F, ALU.min, ALU.max).then_inc(angles_ready, 1)
            dve.wait_ge(sines_done, 1)
            V.tensor_scalar(nsinT[:], sinT[:], -1.0, None, ALU.mult).then_inc(h_ready, 2)
            dve.sem_inc(params_free, 1)
            dve.sem_inc(lnp_free, 1)
            setup_steps = steps[0]
            with dve.Fori(0, DEPTH) as L:
                steps[0] = 0
                base = L * DVE_STEPS + setup_steps

                def lk(ins):
                    link(ins, base)

                def rope(name, t, dsts):
                    n = dsts[0].shape[1]
                    v = ps(name)[:, 0:n * HD].rearrange("p (h a d) -> p h a d", a=2, d=ROT)
                    A = tA[:, 0:n * HD].rearrange("p (h a d) -> p h a d", a=2, d=ROT)
                    B = tB[:, 0:n * HD].rearrange("p (h a d) -> p h a d", a=2, d=ROT)
                    c = cosT[:, t, :].unsqueeze(1).unsqueeze(1).broadcast_to([P, n, 2, ROT])
                    s = sinT[:, t, :].unsqueeze(1).broadcast_to([P, n, ROT])
                    ns = nsinT[:, t, :].unsqueeze(1).broadcast_to([P, n, ROT])
                    dve.wait_ge(*full(name, L))
                    V.tensor_tensor(A, v, c, ALU.mult)
                    V.tensor_tensor(B[:, :, 0, :], v[:, :, 1, :], ns, ALU.mult)
                    lk(V.tensor_tensor(B[:, :, 1, :], v[:, :, 0, :], s, ALU.mult))
                    for d in dsts:
                        last = V.tensor_tensor(d, tA[:, 0:n * HD].rearrange("p (h d) -> p h d", d=HD),
                                               tB[:, 0:n * HD].rearrange("p (h d) -> p h d", d=HD), ALU.add)
                    return last

                V.memset(xin[:, :, :, 0:3], 0.0)
                for n in range(2):
                    for t in range(TT):
                        rot = G[:, t, :, :].rearrange("p a b -> p (a b)")
                        d = rot[:, n * HALF:(n + 1) * HALF].rearrange("p (h d) -> p h d", d=HD)
                        name = (f"q{n}", t)
                        ins = rope(name, t, [d])
                        frees(ins, name)
                        steps[0] += 0
                        dve.wait_ge(*taken(name, L))
                for t in range(TT):
                    rot = G[:, t, :, :].rearrange("p a b -> p (a b)")
                    k2 = rot[:, D:D + 2 * KV_HEADS * HD].rearrange("p (h c d) -> p h c d", c=2, d=HD)
                    lk(rope(("kv", t), t, [k2[:, :, 0, :], k2[:, :, 1, :]]))
                    frees(V.tensor_copy(vv[:, t, :], ps(("kv", t))[:, KV_HEADS * HD:2 * KV_HEADS * HD]), ("kv", t))
                    dve.wait_ge(*taken(("kv", t), L))
                    dve.sem_inc(qrot_ready, 1)
                dve.wait_ge(*full("vec", L))
                frees(V.tensor_copy(vecT[:], ps("vec")[:, 0:VEC_ROWS]), "vec")
                dve.wait_ge(*taken("vec", L))

                def conv(n):
                    dve.wait_ge(*taken((f"xbc{n}", 1), L))
                    for k in (3, 2, 1, 0):
                        for i in range(4):
                            f = 4 * n + i
                            u = xin[:, n % 2, i, k:k + SEQ]
                            w = vecT[:, k * XBC_T + f:k * XBC_T + f + 1]
                            if k == 3:
                                last = V.tensor_scalar(xconv[:, f, :], u, w, vecT[:, V_CB + f:V_CB + f + 1],
                                                       ALU.mult, ALU.add)
                            else:
                                last = V.scalar_tensor_tensor(out=xconv[:, f, :], in0=u, scalar=w,
                                                              in1=xconv[:, f, :], op0=ALU.mult, op1=ALU.add)
                        if k:
                            lk(last)
                    last.then_inc(conv_done, 1)

                def shifted_scores(r):
                    t, half = ROUNDS[r]
                    per = 4 if t == 0 else 2
                    w = P if t == 0 else 192
                    mask = const("mask0") if t == 0 else const("mask1")
                    buf = P0[:, :, :] if t == 0 else P1[:, :, CHUNK:SEQ]
                    for b in range(8 // per):
                        dve.wait_ge(*full(("scores", r, b), L))
                        v = ps(("scores", r, b)).rearrange("p (h k) -> p h k", h=per)[:, :, 0:w]
                        o = (buf.rearrange("p (i c) k -> p c i k", c=2)[:, b] if t == 0 else
                             buf.rearrange("p (m i c) k -> p m c i k", m=2, c=2)[:, b // 2, b % 2])
                        frees(V.scalar_tensor_tensor(out=o, in0=v, scalar=HD ** -0.5,
                                                     in1=mask.unsqueeze(1).broadcast_to([P, per, w]),
                                                     op0=ALU.mult, op1=ALU.add), ("scores", r, b))
                    dve.wait_ge(*taken(("scores", r, 8 // per - 1), L))
                    lk(V.tensor_reduce(amax[:, 0, :], buf, AX.X, ALU.max))
                    sink = rows[:, 48 + 8 * half:56 + 8 * half]
                    lk(V.tensor_tensor(amax[:, 0, :], amax[:, 0, :], sink, ALU.max))
                    V.tensor_tensor(amax[:, 1 + (r % 2), :], sink, amax[:, 0, :], ALU.subtract)
                    V.tensor_tensor(buf, buf, amax[:, 0, :].unsqueeze(2).broadcast_to([P, 8, w]),
                                    ALU.subtract).then_inc(scores_ready, 1)

                def normalise(r):
                    t, _ = ROUNDS[r]
                    w = P if t == 0 else 192
                    buf = P0[:, :, :] if t == 0 else P1[:, :, CHUNK:SEQ]
                    dve.wait_ge(exp_done, L * 4 + (r + 1))
                    lk(V.tensor_reduce(amax[:, 5, :], buf, AX.X, ALU.add))
                    lk(V.tensor_tensor(amax[:, 5, :], amax[:, 5, :], amax[:, 3 + (r % 2), :], ALU.add))
                    lk(V.reciprocal(amax[:, 6, :], amax[:, 5, :]))
                    V.tensor_tensor(buf, buf, amax[:, 6, :].unsqueeze(2).broadcast_to([P, 8, w]),
                                    ALU.mult).then_inc(probs_ready, 1)

                dve.wait_ge(params_full, L * PARAM_INC + PARAM_INC)
                conv(0)
                shifted_scores(0)
                conv(1)
                conv(2)
                shifted_scores(1)
                conv(3)

                dve.wait_ge(*full("dt", L))
                frees(V.tensor_tensor(sm[:, 0, :].rearrange("p (t h) -> p t h", t=TT),
                                      ps("dt")[:, 0:32].rearrange("p (t h) -> p t h", t=TT),
                                      rows[:, 0:16].unsqueeze(1).broadcast_to([P, TT, 16]), ALU.add), "dt")
                dve.wait_ge(*taken("dt", L))
                V.scalar_tensor_tensor(out=sm[:, 1, :], in0=sm[:, 0, :], scalar=-1.0, in1=sm[:, 0, :],
                                       op0=ALU.mult, op1=ALU.max).then_inc(dt_pre, 1)
                V.tensor_scalar(sm[:, 4, :], sm[:, 0, :], 0.0, None, ALU.max)
                dve.wait_ge(dt_exp, L + 1)
                lk(V.tensor_scalar(sm[:, 5, :], sm[:, 2, :], 2.0, None, ALU.add))
                lk(V.reciprocal(sm[:, 6, :], sm[:, 5, :]))
                lk(V.tensor_tensor(sm[:, 7, :], sm[:, 6, :], sm[:, 2, :], ALU.mult))
                lk(V.tensor_tensor(sm[:, 8, :], sm[:, 7, :], sm[:, 7, :], ALU.mult))
                lk(V.tensor_scalar(sm[:, 9, :], sm[:, 8, :], 1.0 / 15, None, ALU.mult))
                for m in (13, 11, 9, 7, 5, 3):
                    lk(V.scalar_tensor_tensor(out=sm[:, 9, :], in0=sm[:, 9, :], scalar=1.0 / m, in1=sm[:, 8, :],
                                              op0=ALU.add, op1=ALU.mult))
                lk(V.scalar_tensor_tensor(out=sm[:, 9, :], in0=sm[:, 9, :], scalar=1.0, in1=sm[:, 7, :],
                                          op0=ALU.add, op1=ALU.mult))
                V.tensor_scalar(nega[:], sm[:, 3, 0:16], -1.0, None, ALU.mult)
                lk(V.scalar_tensor_tensor(out=dtv[:, :, :].rearrange("p a b -> p (a b)"), in0=sm[:, 9, :], scalar=2.0,
                                          in1=sm[:, 4, :], op0=ALU.mult, op1=ALU.add))
                V.tensor_tensor(dA[:, :, :], dtv[:, :, :], nega[:].unsqueeze(1).broadcast_to([P, TT, 16]),
                                ALU.mult).then_inc(dA_ready, 1)

                normalise(0)
                normalise(1)
                shifted_scores(2)
                shifted_scores(3)

                def gated(name, n, g):
                    for t in range(TT):
                        gate = G[:, g, t, n * HALF:(n + 1) * HALF]
                        dve.wait_ge(*full((name, t), L))
                        frees(V.tensor_tensor(gate, gate, ps((name, t))[:, :], ALU.mult), (name, t))

                dve.wait_ge(*taken(("g_pool1", 1), L))
                gated("b_pool0", 0, 0)
                gated("b_pool1", 1, 0)
                dve.wait_ge(*taken(("b_pool1", 1), L))
                dve.sem_inc(merge_step, 1)
                normalise(2)
                normalise(3)

                def heads(ap):
                    return ap.rearrange("p (h d) -> p h d", d=SSD_P)

                for t in range(TT):
                    dve.wait_ge(*taken(("xT", 2 * t + 1), L))
                    lk(V.tensor_tensor(heads(xdt[:, t, :]), heads(xtok[:, t, :]),
                                       dtv[:, t, :].unsqueeze(2).broadcast_to([P, 16, SSD_P]), ALU.mult))
                    lk(V.tensor_tensor(heads(xtok[:, t, :]), heads(xtok[:, t, :]),
                                       rows[:, 32:48].unsqueeze(2).broadcast_to([P, 16, SSD_P]), ALU.mult))
                V.tensor_tensor(heads(xde), heads(xdt[:, 0, :]),
                                dexp[:, 0, :].unsqueeze(2).broadcast_to([P, 16, SSD_P]),
                                ALU.mult).then_inc(xdt_ready, 1)

                dve.wait_ge(*taken(("g_att1", 1), L))
                gated("b_att0", 0, 1)
                gated("b_att1", 1, 1)
                dve.wait_ge(*taken(("b_att1", 1), L))
                V.tensor_tensor(G[:, 0].rearrange("p a b -> p (a b)"), G[:, 0].rearrange("p a b -> p (a b)"),
                                G[:, 1].rearrange("p a b -> p (a b)"), ALU.add).then_inc(merge_step, 1)

                def y(n):
                    g, c = SSD_ROUNDS[n]
                    name = ("y", n)
                    dst = xtok[:, c, g * GW:(g + 1) * GW]
                    dve.wait_ge(*full(name, L))
                    if c == 1:
                        V.tensor_tensor(heads(tA[:, 0:GW]), heads(ps(name)[:, GW:2 * GW]),
                                        dexp[:, 1, SSD_R * g:SSD_R * (g + 1)].unsqueeze(2)
                                        .broadcast_to([P, SSD_R, SSD_P]), ALU.mult)
                    frees(V.tensor_tensor(dst, dst, ps(name)[:, 0:GW], ALU.add), name)
                    if c == 1:
                        dve.wait_ge(*taken(name, L))
                        lk(V.tensor_tensor(dst, dst, tA[:, 0:GW], ALU.add))

                for n, (g, c) in enumerate(SSD_ROUNDS):
                    if c == 0:
                        dve.wait_ge(*full(("cb", g), L))
                        V.tensor_tensor(cbm[:, g % 2, 0:2, :], ps(("cb", g))[:, 0:2 * P].rearrange("p (a b) -> p a b", a=2),
                                        upto.unsqueeze(1).broadcast_to([P, 2, P]), ALU.mult)
                        frees(V.tensor_copy(cbm[:, g % 2, 2, :], ps(("cb", g))[:, 2 * P:3 * P]), ("cb", g))
                        dve.wait_ge(*taken(("cb", g), L))
                    dve.wait_ge(*taken(("seg", n), L))
                    V.tensor_tensor(E[:, n % 2, :, :], E[:, n % 2, :, :],
                                    cbm[:, g % 2, c, :].unsqueeze(1).broadcast_to([P, SSD_R, P]),
                                    ALU.mult).then_inc(decay_ready, 1)
                    if n >= 1:
                        y(n - 1)
                y(len(SSD_ROUNDS) - 1)

                zs = qT[:, :, :].rearrange("p a b -> p (a b)").rearrange("p (t d) -> p t d", t=TT)
                sq = xdt
                dve.wait_ge(*taken(("z1", 1), L))
                for t in range(TT):
                    last = V.tensor_tensor(xtok[:, t, :], xtok[:, t, :], zs[:, t, :], ALU.mult)
                lk(last)
                for t in range(TT):
                    last = V.tensor_tensor(sq[:, t, :], xtok[:, t, :], xtok[:, t, :], ALU.mult)
                lk(last)
                lk(V.tensor_reduce(gss[:, 2], sq[:, :, :].rearrange("p t (g d) -> p t g d", g=SSD_GROUPS), AX.X, ALU.add))
                V.tensor_scalar(gss[:, 0], gss[:, 2], 1.0 / GW, EPS, ALU.mult, ALU.add).then_inc(gy_ms, 1)
                dve.wait_ge(gy_sqrt, L + 1)
                lk(V.reciprocal(gss[:, 2], gss[:, 1]))
                for t in range(TT):
                    v = xtok[:, t, :].rearrange("p (g d) -> p g d", g=SSD_GROUPS)
                    V.tensor_tensor(v, v, gss[:, 2, t, :].unsqueeze(2).broadcast_to([P, SSD_GROUPS, GW]),
                                    ALU.mult).then_inc(ssd_ready, 1)
                dve.wait_ge(*taken(("g_ssd1", 1), L))
                gated("b_ssd0", 0, 1)
                gated("b_ssd1", 1, 1)
                dve.wait_ge(*taken(("b_ssd1", 1), L))
                for t in range(TT):
                    V.tensor_tensor(G[:, 0, t, :], G[:, 0, t, :], G[:, 1, t, :], ALU.add).then_inc(merged_ready, 1)

                def layer_norm(i, names):
                    for t in range(TT):
                        for j in range(2):
                            last = V.bn_stats(stats[:, t, j, :], h[:, t, j * HALF:(j + 1) * HALF])
                        lk(last)
                        dve.sem_inc(passed_wait, 1)
                        lk(V.bn_aggr(mv[:, t, :], stats[:, t, :, :].rearrange("p a b -> p (a b)")))
                        V.tensor_scalar(mv[:, t, 1:2], mv[:, t, 1:2], EPS, None, ALU.add).then_inc(var_ready, 1)
                    dve.wait_ge(lnp_full, L * 96 + 32 * (i + 1))
                    for t in range(TT):
                        dve.wait_ge(sqrt_done, L * 6 + (2 * i + t + 1))
                        V.reciprocal(rstd[:, 1, t:t + 1], rstd[:, 0, t:t + 1])
                        lk(V.scalar_tensor_tensor(out=h[:, t, :], in0=h[:, t, :], scalar=mv[:, t, 0:1],
                                                  in1=lnp[:, 0, :], op0=ALU.subtract, op1=ALU.mult))
                        V.scalar_tensor_tensor(out=h[:, t, :], in0=h[:, t, :], scalar=rstd[:, 1, t:t + 1],
                                               in1=lnp[:, 1, :], op0=ALU.mult, op1=ALU.add).then_inc(h_ready, 1)
                    dve.wait_ge(h_ready, L * 6 + (2 * i + 4))
                    dve.sem_inc(lnp_free, 1)

                def residual(name, t, j):
                    dve.wait_ge(*full(name, L))
                    d = h[:, t, j * HALF:(j + 1) * HALF]
                    frees(V.scalar_tensor_tensor(out=d, in0=d, scalar=ALPHA, in1=ps(name)[:, :],
                                                 op0=ALU.mult, op1=ALU.add), name)

                for j in range(2):
                    for t in range(TT):
                        residual((f"out{j}", t), t, j)
                dve.wait_ge(*taken(("out1", 1), L))
                layer_norm(0, None)

                R = [rt[:, i] for i in range(24)]
                dve.wait_ge(*full("router", L))
                lg = ps("router")[:, 0:40].rearrange("p (t n) -> p t n", t=TT)
                V.tensor_tensor(R[0][:, :, 0:4], lg[:, :, 0:4], rows[:, 64:68].unsqueeze(1).broadcast_to([P, TT, 4]), ALU.add)
                frees(V.tensor_tensor(R[1], lg[:, :, 4:20], rows[:, 68:84].unsqueeze(1).broadcast_to([P, TT, 16]),
                                      ALU.add), "router")
                dve.wait_ge(*taken("router", L))
                dve.sem_inc(params_free, 1)

                def bc(ap, n):
                    return ap.broadcast_to([P, TT, n])

                def first_max(src, m, tmp, hot):
                    lk(V.tensor_tensor(tmp[:, :, 0:4], src, bc(m, 4), ALU.is_equal))
                    lk(V.tensor_tensor(tmp[:, :, 0:4], tmp[:, :, 0:4],
                                       weight4.unsqueeze(1).broadcast_to([P, TT, 4]), ALU.mult))
                    lk(V.tensor_reduce(tmp[:, :, 4:5], tmp[:, :, 0:4], AX.X, ALU.max))
                    lk(V.tensor_tensor(hot, tmp[:, :, 0:4], bc(tmp[:, :, 4:5], 4), ALU.is_equal))

                gmax = R[4][:, :, 0:1]
                lk(V.tensor_reduce(gmax, R[0][:, :, 0:4], AX.X, ALU.max))
                V.tensor_tensor(R[2][:, :, 0:4], R[0][:, :, 0:4], bc(gmax, 4), ALU.subtract).then_inc(rexp_in, 1)
                first_max(R[0][:, :, 0:4], gmax, R[5], R[6][:, :, 0:4])
                gl = R[7].rearrange("p t (g e) -> p t g e", g=MOE_G)
                lk(V.tensor_tensor(gl, R[1].rearrange("p t (g e) -> p t g e", g=MOE_G),
                                   R[6][:, :, 0:4].unsqueeze(3).broadcast_to([P, TT, MOE_G, MOE_E]), ALU.mult))
                es = R[8][:, :, 0:4]
                lk(V.tensor_reduce(es, R[7].rearrange("p t (g e) -> p t e g", g=MOE_G), AX.X, ALU.add))
                m1, m2 = R[9][:, :, 0:1], R[10][:, :, 0:1]
                lk(V.tensor_reduce(m1, es, AX.X, ALU.max))
                first_max(es, m1, R[5], R[13][:, :, 0:4])
                lk(V.scalar_tensor_tensor(out=R[14][:, :, 0:4], in0=R[13][:, :, 0:4], scalar=NEG, in1=es,
                                          op0=ALU.mult, op1=ALU.add))
                lk(V.tensor_reduce(m2, R[14][:, :, 0:4], AX.X, ALU.max))
                V.tensor_tensor(R[11][:, :, 0:1], m2, m1, ALU.subtract).then_inc(rexp_in, 1)
                first_max(R[14][:, :, 0:4], m2, R[5], R[15][:, :, 0:4])
                dve.wait_ge(rexp_out, L * 2 + 2)
                lk(V.tensor_reduce(R[16][:, :, 0:1], R[3][:, :, 0:4], AX.X, ALU.add))
                lk(V.reciprocal(R[16][:, :, 1:2], R[16][:, :, 0:1]))
                lk(V.tensor_scalar(R[17][:, :, 0:1], R[12][:, :, 0:1], 1.0, None, ALU.add))
                lk(V.reciprocal(R[17][:, :, 1:2], R[17][:, :, 0:1]))
                lk(V.tensor_tensor(R[17][:, :, 2:3], R[17][:, :, 1:2], R[16][:, :, 1:2], ALU.mult))
                lk(V.tensor_tensor(R[17][:, :, 3:4], R[17][:, :, 2:3], R[12][:, :, 0:1], ALU.mult))
                V.tensor_tensor(R[18][:, :, 0:4], R[13][:, :, 0:4], bc(R[17][:, :, 2:3], 4), ALU.mult)
                lk(V.tensor_tensor(R[19][:, :, 0:4], R[15][:, :, 0:4], bc(R[17][:, :, 3:4], 4), ALU.mult))
                lk(V.tensor_tensor(R[18][:, :, 0:4], R[18][:, :, 0:4], R[19][:, :, 0:4], ALU.add))
                for t in range(TT):
                    last = V.tensor_tensor(rt[:, COMBINE, t, :].rearrange("p (g e) -> p g e", g=MOE_G),
                                           R[6][:, t, 0:4].unsqueeze(2).broadcast_to([P, MOE_G, MOE_E]),
                                           R[18][:, t, 0:4].unsqueeze(1).broadcast_to([P, MOE_G, MOE_E]), ALU.mult)
                last.then_inc(combine_ready, 1)

                for e in range(NE):
                    u = act_t[:, e % 2, :]
                    dve.wait_ge(*taken(("hg", e), L))
                    dve.wait_ge(*full(("hu", e), L))
                    frees(V.tensor_tensor(u, act_s[:, e % 2, :], ps(("hu", e))[:, :], ALU.mult), ("hu", e))
                    dve.wait_ge(*taken(("hu", e), L))
                    dve.wait_ge(*taken(("comb", e // 2), L))
                    u2 = u.rearrange("p (f s) -> p f s", f=2)
                    V.tensor_tensor(u2, u2, comb[:, e, :].unsqueeze(1).broadcast_to([P, 2, SEQ]),
                                    ALU.mult).then_inc(act_ready, 1)
                for t in range(TT):
                    for j in range(2):
                        residual(("acc", t, j), t, j)
                dve.wait_ge(*taken(("acc", 1, 1), L))
                layer_norm(1, None)

                for j in range(2):
                    for t in range(TT):
                        name = (f"pg{j}", t)
                        dve.wait_ge(*taken(name, L))
                        g = G[:, 0, t, j * HALF:(j + 1) * HALF]
                        dve.wait_ge(*taken(("proj", t, j), L))
                        lk(V.tensor_tensor(g, g, xtok[:, t, j * HALF:(j + 1) * HALF], ALU.mult))
                        d = h[:, t, j * HALF:(j + 1) * HALF]
                        lk(V.scalar_tensor_tensor(out=d, in0=d, scalar=ALPHA, in1=g, op0=ALU.mult, op1=ALU.add))
                layer_norm(2, None)
                assert steps[0] == DVE_STEPS, f"DVE_STEPS = {steps[0]}"


_INS = ["x", "p", "positions", "w_in", "ssd_conv_w", "ssd_conv_b", "ssd_dt_bias", "ssd_a_log", "ssd_d",
        "ssd_norm_w", "attn_sinks", "pool_w", "pool_scale", "w_branch", "w_out", "ln1_g", "ln1_b",
        "router_group_w", "router_group_b", "router_expert_w", "router_expert_b", "exp_w_gate",
        "exp_w_up", "exp_w_down", "ln2_g", "ln2_b", "ple_w_proj", "ple_w_gate", "ln3_g", "ln3_b"]


def kernel(**inputs):
    import concourse.bacc as bacc
    from concourse.bass_utils import run_bass_kernel_spmd

    nc = bacc.Bacc("TRN2", target_bir_lowering=False, num_devices=1)
    arrays, args = {}, []
    for name in _INS + ["consts"]:
        a = shape_constants() if name == "consts" else np.ascontiguousarray(inputs[name])
        arrays[f"in_{name}"] = a
        args.append(nc.dram_tensor(f"in_{name}", a.shape, mybir.dt.from_np(a.dtype), kind="ExternalInput").ap())
    args.append(nc.dram_tensor("out_h", (1, SEQ, D), F32, kind="ExternalOutput").ap())
    program(nc, *args)
    return run_bass_kernel_spmd(nc, [arrays], core_ids=[0]).results[0]["out_h"]
```

```python
from contextlib import ExitStack

import numpy as np

import concourse.bass as bass
from concourse import mybir

F32 = mybir.dt.float32
I32 = mybir.dt.int32
ALU = mybir.AluOpType
ACT = mybir.ActivationFunctionType
AX = mybir.AxisListType

P = 128
DEPTH, SEQ, D = 2, 256, 1024
TT = SEQ // P
KT = D // P
HALF = 512
PLE = 256
SSD_HEADS, SSD_P, SSD_GROUPS, SSD_N, SSD_CONV = 16, 64, 4, 128, 4
SSD_R = SSD_HEADS // SSD_GROUPS
GW = SSD_R * SSD_P
XBC = D + 2 * SSD_GROUPS * SSD_N
XBC_T = XBC // P
Q_HEADS, KV_HEADS, HD = 16, 4, 64
ROT = HD // 2
CHUNK = 64
POOL_WINDOWS = (2, 4, 8, 16)
MOE_G, MOE_E = 4, 4
NE = MOE_G * MOE_E
HID = 256
ALPHA = (2.0 * DEPTH) ** 0.25
EPS = 1e-5
NEG = -1e30
CAP = 96

COL_Z, COL_XBC = 0, D
COL_DT = COL_XBC + XBC
COL_Q = COL_DT + SSD_HEADS
COL_KV = COL_Q + Q_HEADS * HD
COL_PU = COL_KV + 2 * KV_HEADS * HD
COL_GATE = COL_PU + D

UNITS = (
    [("q", 0), ("q", 1), ("kv", 0), ("pu", 0), ("pu", 1)]
    + [("xbc", 0), ("xbc", 1), ("xbc", 2), ("pool_w", 0), ("xbc", 3), ("dt", 0)]
    + [("gate", 4), ("gate", 5), ("branch", 4), ("branch", 5), ("z", 0), ("z", 1)]
    + [("gate", 2), ("gate", 3), ("branch", 2), ("branch", 3)]
    + [("gate", 0), ("gate", 1), ("branch", 0), ("branch", 1), ("out", 0), ("out", 1)]
    + [("ple_proj", 0)]
    + [x for e in range(0, NE, 2) for x in (("gu", e), ("gu", e + 1), ("down", e))]
    + [("ple_gate", 0), ("ple_gate", 1)]
)
RING = 3
UNIT_W = 8 * HALF
NU = len(UNITS)
assert NU % RING == 0
UNIT_AT = {u: i for i, u in enumerate(UNITS)}
UNIT_DMAS = 2

ROUNDS = [(0, 0), (1, 0), (0, 1), (1, 1)]
SSD_ROUNDS = [(g, c) for g in range(SSD_GROUPS) for c in range(TT)]

SSD_FILL = {1: ("z1", ("z", 1), 1), 3: ("g_att0", ("gate", 2), 0), 5: ("g_att1", ("gate", 3), 1)}


def job_table():
    jobs = []

    def job(name, bank):
        jobs.append((name, bank))

    def pair(name, n):
        for t in range(TT):
            job((name, t), 2 * (n % 2) + t)

    def transposes(name):
        for t in range(TT):
            for j in range(2):
                job((name, t, j), 4 + 2 * t + j)

    transposes("hT1")
    pair("q0", 0)
    pair("q1", 1)
    pair("kv", 0)
    pair("pu0", 1)
    pair("pu1", 0)
    job("vec", 4)
    for t in range(TT):
        job(("qT", t, 0), 5)
        job(("qT", t, 1), 6)
        job(("kT", t), 7)
    pair("xbc0", 1)
    job(("scores", 0, 0), 4)
    job(("scores", 0, 1), 5)
    pair("xbc1", 0)
    for j in range(4):
        job(("pooled", j), 4 + j)
    pair("xbc2", 1)
    for j in range(4):
        job(("mixed", j), 4 + j)
    for b in range(4):
        job(("scores", 1, b), 4 + b)
    pair("xbc3", 0)
    job("dt", 2)
    for r, fill in enumerate(("g_pool0", "g_pool1", "b_pool0", "z0")):
        if r == 3:
            pair("b_pool1", 1)
        pair(fill, (0, 1, 0, 0)[r])
        nb = 2 if r % 2 == 0 else 4
        for b in range(nb):
            job(("PT", r, b), 4 + b)
        for g in range(2):
            job(("PV", r, g), 4 + 2 * (r % 2 == 0) + g)
        if r + 2 < 4:
            for b in range(nb):
                job(("scores", r + 2, b), 4 + b)
    job("dsum", 4)
    for j in range(4):
        job(("xT", j), 4 + j)
    for n, (g, c) in enumerate(SSD_ROUNDS):
        if n in SSD_FILL:
            pair(SSD_FILL[n][0], SSD_FILL[n][2])
        if c == 0:
            job(("cb", g), 4)
        job(("seg", n), 5)
        if n >= 1:
            job(("y", n - 1), 6 + (n - 1) % 2)
    job(("y", len(SSD_ROUNDS) - 1), 7)
    pair("b_att0", 0)
    pair("b_att1", 1)
    pair("g_ssd0", 0)
    pair("g_ssd1", 1)
    transposes("yT")
    pair("b_ssd0", 0)
    pair("b_ssd1", 1)
    transposes("mT")
    pair("out0", 0)
    pair("out1", 1)
    transposes("hT2")
    job("router", 4)
    job("pT", 0)
    for t in range(TT):
        for j in range(2):
            job(("proj", t, j), [1, 2, 3, 0][2 * t + j])
    job("rank", 5)
    jobs.append(("sparse", None))
    for d in range(KT):
        job(("sorted", d), 4 + d % 4)
    for e in range(NE):
        job(("hgu", e), e % 2)
        if e == 1:
            for g in range(MOE_G):
                job(("weight", g), 2 + g % 2)
            for g in range(MOE_G):
                job(("back", g), 2 + g % 2)
        if e % MOE_E == MOE_E - 1:
            for j in range(2):
                job(("yg", e // MOE_E, j), 2 + j)
    jobs.append(("dense", None))
    for e in range(NE):
        job(("hg", e), 2 * (e % 2))
        job(("hu", e), 2 * (e % 2) + 1)
        if e == 1:
            for b in range(NE // 2):
                job(("comb", b), 4 + b % 4)
    jobs.append(("both", None))
    for t in range(TT):
        for j in range(2):
            job(("acc", t, j), 4 + 2 * t + j)
    transposes("hT3")
    pair("pg0", 1)
    pair("pg1", 0)
    return jobs


JOBS = job_table()
NBANK = 8
JOB_AT, BANK_JOBS = {}, [0] * NBANK
for _name, _bank in JOBS:
    if _bank is None:
        if _name == "sparse":
            _before = list(BANK_JOBS)
        elif _name == "dense":
            _after, BANK_JOBS = BANK_JOBS, _before
        else:
            assert BANK_JOBS == _after
        continue
    assert _name not in JOB_AT, _name
    JOB_AT[_name] = (_bank, BANK_JOBS[_bank])
    BANK_JOBS[_bank] += 1

CONST_COLS = {}
_at = 0
for _n, _w in (("ident", P), ("upto", P), ("after", P), ("mask0", P), ("mask1", 192),
               ("band0", 4 * SEQ), ("band1", 4 * P), ("inv", ROT), ("weight4", 4), ("iota", CAP)):
    CONST_COLS[_n] = (_at, _w)
    _at += _w
NCONST = _at


def shape_constants():
    a, b = np.arange(P)[:, None], np.arange(P)[None, :]
    c = {}
    c["ident"] = a == b
    c["upto"] = a <= b
    c["after"] = a > b
    own = a // CHUNK
    c["mask0"] = np.where((own == 0) & (b // CHUNK == 1), NEG, 0.0)
    k = np.arange(192)[None, :] // CHUNK
    c["mask1"] = np.where(k - own * 1 == 2, NEG, 0.0) + np.where((own == 1) & (k == 0), NEG, 0.0)
    t, s = np.arange(P)[:, None], np.arange(SEQ)[None, :]
    band0, band1 = [], []
    for w in POOL_WINDOWS:
        inside = (t <= s) & (t > s - w)
        band0.append(inside / np.minimum(s + 1, w) - (t == s))
        band1.append(((t <= b) & (t > b - w)) / w - (t == b))
    c["band0"] = np.concatenate(band0, 1)
    c["band1"] = np.concatenate(band1, 1)
    inv = np.float32(10000.0) ** (-np.arange(0, HD, 2, dtype=np.float32) / np.float32(HD))
    c["inv"] = np.broadcast_to(inv[None, :], (P, ROT))
    c["weight4"] = np.broadcast_to(np.array([[4, 3, 2, 1]]), (P, 4))
    c["iota"] = np.broadcast_to(np.arange(CAP)[None, :], (P, CAP))
    out = np.zeros((P, NCONST), np.float32)
    for n, (o, w) in CONST_COLS.items():
        out[:, o:o + w] = c[n]
    return out


VEC_ROWS = SSD_CONV * XBC_T + XBC_T + KT + KT
V_CB = SSD_CONV * XBC_T
V_PS = V_CB + XBC_T
V_NW = V_PS + KT
ROWS = {"dt_bias": (0, 16), "a_log": (16, 16), "d": (32, 16), "sinks": (48, 16), "rb": (64, 20)}
RROW = 84

PARAM_INC = 13 * 16
ROUND = float(3 * 2 ** 22)
TWO_PI = (6.28125, 0.0019350051879882812, 3.019915981956753e-07)
PI_F = 3.1415925
COMBINE = 20
DVE_STEPS = 119


def program(nc, x, p, positions, w_in, conv_w, conv_b, dt_bias, a_log, ssd_d, norm_w, sinks, pool_w,
            pool_scale, w_branch, w_out, ln1_g, ln1_b, rg_w, rg_b, re_w, re_b, w_gate, w_up, w_down,
            ln2_g, ln2_b, ple_proj, ple_gate, ln3_g, ln3_b, consts, out):
    with ExitStack() as ctx:
        def sb(name, shape, dt=F32):
            return ctx.enter_context(nc.sbuf_tensor(name, [P] + shape, dt))

        def sem(name):
            return ctx.enter_context(nc.semaphore(name))

        ring = sb("ring", [RING, UNIT_W])
        cst = sb("cst", [NCONST])
        h = sb("h", [TT, D])
        hT = sb("hT", [KT, SEQ])
        G = sb("G", [2, TT, D])
        xin = sb("xin", [2, 4, 3 + SEQ])
        poolT = sb("poolT", [KT, SEQ])
        xconv = sb("xconv", [XBC_T, SEQ])
        xtok = sb("xtok", [TT, D])
        xdt = sb("xdt", [TT, D])
        qkT = sb("qkT", [KT + KV_HEADS, SEQ])
        qT = qkT[:, 0:KT, :]
        kT = qkT[:, KT:KT + KV_HEADS, :]
        vv = sb("vv", [TT, KV_HEADS * HD])
        P0 = sb("P0", [8, P])
        P1 = sb("P1", [8, 2 * P])
        PTs = sb("PTs", [2, 2, 4, P])
        segs = sb("segs", [2, SSD_R, P])
        E = sb("E", [2, SSD_R, P])
        cbm = sb("cbm", [2, 3, P])
        lnp = sb("lnp", [2, D])
        tA = sb("tA", [HALF])
        tB = sb("tB", [HALF])
        attT = xin[:, :, :, :].rearrange("p a b c -> p (a b c)")[:, 0:D * TT].rearrange(
            "p (f s) -> p f s", f=KT)
        xde = P0[:, :, :].rearrange("p a b -> p (a b)")
        pT = PTs[:, 0, 0, :, :].rearrange("p a b -> p (a b)").rearrange("p (k s) -> p k s", k=2)
        act_s = segs[:, :, :].rearrange("p a b c -> p a (b c)")
        act_t = E[:, :, :].rearrange("p a b c -> p a (b c)")
        yT = xconv[:, 0:KT, :]
        NS = MOE_G * CAP
        hS = qkT[:, :, :].rearrange("p a b -> p (a b)")[:, 0:KT * NS].rearrange("p (k s) -> p k s", k=KT)
        sel = xdt[:, :, :].rearrange("p a b -> p (a b)")[:, 0:TT * NS].rearrange("p (t s) -> p t s", t=TT)
        selT = xdt[:, :, :].rearrange("p a b -> p (a b)")[:, TT * NS:TT * NS + MOE_G * SEQ].rearrange(
            "p (g s) -> p g s", g=MOE_G)
        yg = poolT[:, :, :].rearrange("p a b -> p (a b)").rearrange("p (i d) -> p i d", i=2)
        wS = xconv[:, :, :].rearrange("p a b -> p (a b)")[:, 0:NE * CAP].rearrange("p (e s) -> p e s", e=NE)
        comb = xconv
        vecrows = sb("vecrows", [P])
        vecT = sb("vecT", [VEC_ROWS])
        rows = sb("rows", [RROW])
        rw = sb("rw", [KT, 20])
        prow = sb("prow", [TT, PLE])
        posi = sb("posi", [TT], I32)
        posf = sb("posf", [TT])
        cosT = sb("cosT", [TT, ROT])
        sinT = sb("sinT", [TT, ROT])
        nsinT = sb("nsinT", [TT, ROT])
        ang = sb("ang", [4, TT, ROT])
        sm = sb("sm", [12, TT * SSD_HEADS])
        dtv = sb("dtv", [TT, SSD_HEADS])
        dA = sb("dA", [TT, SSD_HEADS])
        nega = sb("nega", [SSD_HEADS])
        dexp = sb("dexp", [2, SSD_HEADS])
        amax = sb("amax", [8, 8])
        gss = sb("gss", [3, TT, SSD_GROUPS])
        stats = sb("stats", [TT, 2, 6])
        mv = sb("mv", [TT, 2])
        overflow = sb("overflow", [1], I32)
        rstd = sb("rstd", [2, TT])
        rt = sb("rt", [24, TT, 16])
        bank = [ctx.enter_context(nc.psum_tensor(f"bank{i}", [P, HALF], F32)) for i in range(NBANK)]

        def const(name):
            o, w = CONST_COLS[name]
            return cst[:, o:o + w]

        ident, upto, after = const("ident"), const("upto"), const("after")
        band0 = const("band0").rearrange("p (w s) -> p w s", w=4)
        weight4 = const("weight4")
        ones = weight4[:, 3:4].to_broadcast([P, P])
        band1 = const("band1").rearrange("p (w s) -> p w s", w=4)

        unit_full = [sem(f"unit_full{s}") for s in range(RING)]
        unit_free = sem("unit_free")
        bank_full = [sem(f"bank_full{b}") for b in range(NBANK)]
        bank_free = [sem(f"bank_free{b}") for b in range(NBANK)]
        start_loads = [sem("ident_x0_loaded"), sem("x1_loaded")]
        const_loaded = sem("const_loaded")
        dve_step = sem("dve_step")
        pos_loaded = sem("pos_loaded")
        sines_done = sem("sines_done")
        angles_ready = sem("angles_ready")
        params_full = sem("params_full")
        params_free = sem("params_free")
        lnp_full = sem("lnp_full")
        lnp_free = sem("lnp_free")
        h_ready = sem("h_ready")
        qrot_ready = sem("qrot_ready")
        conv_done = sem("conv_done")
        silu_done = sem("silu_done")
        probs_ready = sem("probs_ready")
        scores_ready = sem("scores_ready")
        exp_done = sem("exp_done")
        dt_pre = sem("dt_pre")
        dt_exp = sem("dt_exp")
        dA_ready = sem("dA_ready")
        dsum_exp = sem("dsum_exp")
        xdt_ready = sem("xdt_ready")
        seg_built = sem("seg_built")
        seg_exp = sem("seg_exp")
        decay_ready = sem("decay_ready")
        merge_step = sem("merge_step")
        gy_ms = sem("gy_ms")
        gy_sqrt = sem("gy_sqrt")
        ssd_ready = sem("ssd_ready")
        merged_ready = sem("merged_ready")
        var_ready = sem("var_ready")
        sqrt_done = sem("sqrt_done")
        rexp_in = sem("rexp_in")
        rexp_out = sem("rexp_out")
        combine_ready = sem("combine_ready")
        hsilu_done = sem("hsilu_done")
        act_ready = sem("act_ready")
        group_ready = sem("group_ready")
        flag_ready = sem("flag_ready")
        sel_ready = sem("sel_ready")
        silu_s = sem("silu_s")
        stored = sem("stored")
        passed_wait = sem("passed_wait")

        def full(name, L):
            b, k = JOB_AT[name]
            return bank_full[b], L * BANK_JOBS[b] + (k + 1)

        def free(name, L):
            b, k = JOB_AT[name]
            return bank_free[b], L * BANK_JOBS[b] + (k + 1)

        def taken(name, L):
            b, k = JOB_AT[name]
            return bank_free[b], L * BANK_JOBS[b] + (k + 2)

        def ps(name):
            return bank[JOB_AT[name][0]]

        def slot(unit):
            return ring[:, UNIT_AT[unit] % RING, :]

        block = ctx.enter_context(nc.Block())

        @block.sync
        def _(sp):
            sp.dma_start(cst[:, 0:P], consts[:, 0:P]).then_inc(start_loads[0], 16)
            for t in range(TT):
                sp.dma_start(h[:, t, :], x[0, t * P:(t + 1) * P, :]).then_inc(start_loads[t], 16)
            with sp.Fori(0, DEPTH) as L:
                for u, (kind, n) in enumerate(UNITS):
                    dst = ring[:, u % RING, :]
                    k8 = dst.rearrange("p (k n) -> p k n", k=KT)
                    sp.wait_ge(unit_free, L * NU + (u + 1))
                    sp.sem_inc(passed_wait, 1)
                    pairs = []
                    if kind in ("q", "kv", "pu", "xbc", "gate", "z", "dt"):
                        col = {"q": COL_Q, "kv": COL_KV, "pu": COL_PU, "xbc": COL_XBC,
                               "gate": COL_GATE, "z": COL_Z, "dt": COL_DT}[kind] + n * HALF
                        w = SSD_HEADS if kind == "dt" else HALF
                        src = w_in[L].rearrange("(k p) n -> p k n", p=P)[:, :, col:col + w]
                        pairs = [(k8[:, 0:4, 0:w], src[:, 0:4]), (k8[:, 4:8, 0:w], src[:, 4:8])]
                    elif kind in ("branch", "out", "ple_gate"):
                        m = {"branch": w_branch, "out": w_out, "ple_gate": ple_gate}[kind]
                        m = m[L, n // 2] if kind == "branch" else m[L]
                        c = (n % 2) * HALF
                        src = m.rearrange("(k p) n -> p k n", p=P)[:, :, c:c + HALF]
                        pairs = [(k8[:, 0:4, :], src[:, 0:4]), (k8[:, 4:8, :], src[:, 4:8])]
                    elif kind == "gu":
                        for i, m in enumerate((w_gate, w_up)):
                            pairs.append((dst[:, i * 2048:(i + 1) * 2048].rearrange("p (k n) -> p k n", k=KT),
                                          m[L, n // 4, n % 4].rearrange("(k p) n -> p k n", p=P)))
                    elif kind == "down":
                        for i in range(2):
                            e = n + i
                            pairs.append((dst[:, i * 2048:(i + 1) * 2048].rearrange("p (k n) -> p k n", k=2),
                                          w_down[L, e // 4, e % 4].rearrange("(k p) n -> p k n", p=P)))
                    elif kind == "pool_w":
                        for i in range(2):
                            pairs.append((dst[:, i * 1024:(i + 1) * 1024].rearrange("p (g k n) -> p g k n", g=2, k=2),
                                          pool_w[L, 2 * i:2 * i + 2].rearrange("g (k p) n -> p g k n", p=P)))
                    elif kind == "ple_proj":
                        for i in range(2):
                            pairs.append((dst[:, i * D:(i + 1) * D], ple_proj[L, i * P:(i + 1) * P, :]))
                    for d, s in pairs:
                        sp.dma_start(d, s).then_inc(unit_full[u % RING], 16)
            for t in range(TT):
                sp.wait_ge(h_ready, 6 * DEPTH + 1 + t)
                sp.dma_start(out[0, t * P:(t + 1) * P, :], h[:, t, :]).then_inc(stored, 16)
            sp.wait_ge(stored, 32)

        @block.tensor
        def _(pe):
            mm, tr = nc.tensor.matmul, nc.tensor.transpose

            def done(ins, name):
                ins.then_inc(bank_full[JOB_AT[name][0]], 1)

            pe.sem_inc(unit_free, RING - 1)
            for b in range(NBANK):
                pe.sem_inc(bank_free[b], 1)
            pe.wait_ge(start_loads[0], 32)
            pe.wait_ge(start_loads[1], 16)
            with pe.Fori(0, DEPTH) as L:

                def arrived(unit):
                    u = UNIT_AT[unit]
                    pe.wait_ge(unit_full[u % RING], L * (NU // RING * 32) + 32 * (u // RING + 1))

                def transposes(name, t, src, ready):
                    pe.wait_ge(*ready)
                    for j in range(2):
                        pe.wait_ge(*free((name, t, j), L))
                        for i in range(4):
                            f = (4 * j + i) * P
                            last = tr(ps((name, t, j))[:, i * P:(i + 1) * P], src[:, t, f:f + P], ident)
                        done(last, (name, t, j))

                def token_tile(name, unit, t, lhs, starts=False):
                    w = slot(unit).rearrange("p (k n) -> p k n", k=KT)
                    pe.wait_ge(*free((name, t), L))
                    for k in range(KT):
                        last = mm(ps((name, t))[:, :], lhs[:, k, t * P:(t + 1) * P], w[:, k, :],
                                  start=k == 0, stop=k == KT - 1)
                        if k == 0 and starts:
                            last.then_inc(unit_free, 1)
                    done(last, (name, t))

                def tokens(name, unit, lhs):
                    arrived(unit)
                    for t in range(TT):
                        token_tile(name, unit, t, lhs, starts=t == 0)

                def token_pair(a, b, unit_a, unit_b, lhs, before):
                    for t in range(TT):
                        before(t)
                        if t == 0:
                            arrived(unit_a)
                        token_tile(a, unit_a, t, lhs, starts=t == 0)
                        if t == 0:
                            arrived(unit_b)
                        token_tile(b, unit_b, t, lhs, starts=t == 1)

                def features(name, unit):
                    arrived(unit)
                    w = slot(unit).rearrange("p (k n) -> p k n", k=KT)
                    for b in range(2):
                        pe.wait_ge(*free((name, b), L))
                        for i in range(2):
                            f = (2 * b + i) * P
                            for k in range(KT):
                                last = mm(ps((name, b))[:, i * SEQ:(i + 1) * SEQ], w[:, k, f:f + P],
                                          hT[:, k, :], start=k == 0, stop=k == KT - 1)
                                if b + i + k == 0:
                                    last.then_inc(unit_free, 1)
                        done(last, (name, b))

                def qk_transposes(t):
                    pe.wait_ge(qrot_ready, L * TT + (t + 1))
                    rot = G[:, t, :, :].rearrange("p a b -> p (a b)")
                    for n, name in enumerate((("qT", t, 0), ("qT", t, 1), ("kT", t))):
                        pe.wait_ge(*free(name, L))
                        for i in range(4):
                            last = tr(ps(name)[:, i * P:(i + 1) * P],
                                      rot[:, (4 * n + i) * P:(4 * n + i + 1) * P], ident)
                        done(last, name)

                def scores(r):
                    t, half = ROUNDS[r]
                    per = 4 if t == 0 else 2
                    pe.wait_ge(*taken(("kT", 1), L))
                    for b in range(8 // per):
                        pe.wait_ge(*free(("scores", r, b), L))
                        for i in range(per):
                            head = 8 * half + (2 * i + b if t == 0 else 4 * (b // 2) + 2 * i + b % 2)
                            q0 = HD * (head % 2)
                            if t == 0:
                                o = ps(("scores", r, b))[:, i * P:(i + 1) * P]
                                keys = slice(0, P)
                            else:
                                o = ps(("scores", r, b))[:, i * 256:i * 256 + 192]
                                keys = slice(CHUNK, SEQ)
                            last = mm(o, qT[q0:q0 + HD, head // 2, t * P:(t + 1) * P],
                                      kT[q0:q0 + HD, head // 4, keys], start=True, stop=True)
                        done(last, ("scores", r, b))

                def probs_transposes(r):
                    t, half = ROUNDS[r]
                    pe.wait_ge(probs_ready, L * 4 + (r + 1))
                    for b in range(2 if t == 0 else 4):
                        name = ("PT", r, b)
                        pe.wait_ge(*free(name, L))
                        for i in range(4):
                            src = P0[:, 4 * b + i, :] if t == 0 else \
                                P1[:, 4 * (b // 2) + i, (b % 2) * P:(b % 2 + 1) * P]
                            last = tr(ps(name)[:, i * P:(i + 1) * P], src, ident)
                        done(last, name)

                def values(r):
                    t, half = ROUNDS[r]
                    for g in range(2):
                        name = ("PV", r, g)
                        kv = 2 * half + g
                        pe.wait_ge(*free(name, L))
                        for kb in range(t + 1):
                            b = g if t == 0 else 2 * g + kb
                            pe.wait_ge(*taken(("PT", r, b), L))
                            last = mm(ps(name)[0:HD, :], vv[:, kb, kv * HD:(kv + 1) * HD],
                                      PTs[:, b // 2, b % 2, :, :].rearrange("p a b -> p (a b)") if t else
                                      PTs[:, 0, b, :, :].rearrange("p a b -> p (a b)"),
                                      start=kb == 0, stop=kb == t)
                        done(last, name)

                def h_transposed(name, t, i):
                    transposes(name, t, h, (h_ready, L * 6 + (2 * i + t + 1)))

                def q_tile(t):
                    h_transposed("hT1", t, 0)
                    pe.wait_ge(*taken(("hT1", t, 1), L))

                token_pair("q0", "q1", ("q", 0), ("q", 1), hT, q_tile)
                tokens("kv", ("kv", 0), hT)
                tokens("pu0", ("pu", 0), hT)
                tokens("pu1", ("pu", 1), hT)

                pe.wait_ge(params_full, L * PARAM_INC + PARAM_INC)
                pe.wait_ge(*free("vec", L))
                done(tr(ps("vec")[:, 0:VEC_ROWS], vecrows[0:VEC_ROWS, :], ident[0:VEC_ROWS, 0:VEC_ROWS]), "vec")
                for t in range(TT):
                    qk_transposes(t)
                features("xbc0", ("xbc", 0))
                scores(0)
                features("xbc1", ("xbc", 1))

                pe.wait_ge(const_loaded, 16)
                pe.wait_ge(*taken(("pu1", 1), L))
                for j in range(4):
                    pe.wait_ge(*free(("pooled", j), L))
                    for i in range(2):
                        f = 2 * j + i
                        o = ps(("pooled", j))[:, i * SEQ:(i + 1) * SEQ]
                        mm(o[:, 0:P], xtok[:, 0, f * P:(f + 1) * P], band0[:, j, 0:P], start=True, stop=True)
                        mm(o[:, P:SEQ], xtok[:, 0, f * P:(f + 1) * P], band0[:, j, P:SEQ], start=True, stop=False)
                        last = mm(o[:, P:SEQ], xtok[:, 1, f * P:(f + 1) * P], band1[:, j, :],
                                  start=False, stop=True)
                    done(last, ("pooled", j))
                features("xbc2", ("xbc", 2))
                arrived(("pool_w", 0))
                w = slot(("pool_w", 0))[:, 0:2048].rearrange("p (g k n) -> p g k n", g=4, k=2)
                pooled = xdt[:, :, :].rearrange("p a b -> p (a b)").rearrange("p (f s) -> p f s", f=KT)
                for j in range(4):
                    pe.wait_ge(*taken(("pooled", j), L))
                    pe.wait_ge(*free(("mixed", j), L))
                    for i in range(2):
                        for k in range(2):
                            last = mm(ps(("mixed", j))[:, i * SEQ:(i + 1) * SEQ], w[:, j, k, i * P:(i + 1) * P],
                                      pooled[:, 2 * j + k, :], start=k == 0, stop=k == 1)
                            if i + j + k == 0:
                                last.then_inc(unit_free, 1)
                    done(last, ("mixed", j))
                scores(1)
                features("xbc3", ("xbc", 3))

                arrived(("dt", 0))
                pe.wait_ge(*free("dt", L))
                w = slot(("dt", 0)).rearrange("p (k n) -> p k n", k=KT)
                for t in range(TT):
                    for k in range(KT):
                        last = mm(ps("dt")[:, t * 16:(t + 1) * 16], hT[:, k, t * P:(t + 1) * P],
                                  w[:, k, 0:SSD_HEADS], start=k == 0, stop=k == KT - 1)
                        if t + k == 0:
                            last.then_inc(unit_free, 1)
                done(last, "dt")

                tokens("g_pool0", ("gate", 4), hT)
                probs_transposes(0)
                values(0)
                scores(2)
                tokens("g_pool1", ("gate", 5), hT)
                probs_transposes(1)
                values(1)
                scores(3)
                pe.wait_ge(*taken(("mixed", 3), L))
                tokens("b_pool0", ("branch", 4), poolT)
                probs_transposes(2)
                values(2)
                tokens("b_pool1", ("branch", 5), poolT)
                tokens("z0", ("z", 0), hT)
                probs_transposes(3)
                values(3)

                pe.wait_ge(dA_ready, L + 1)
                pe.wait_ge(*free("dsum", L))
                mm(ps("dsum")[:, 0:16], after, dA[:, 0, :], start=True, stop=True)
                done(mm(ps("dsum")[:, 16:32], upto, dA[:, 1, :], start=True, stop=True), "dsum")
                pe.wait_ge(silu_done, L * 4 + 4)
                for j in range(4):
                    t, half = j // 2, j % 2
                    pe.wait_ge(*free(("xT", j), L))
                    for i in range(4):
                        last = tr(ps(("xT", j))[:, i * P:(i + 1) * P],
                                  xconv[:, 4 * half + i, t * P:(t + 1) * P], ident)
                    done(last, ("xT", j))

                def y(n):
                    g, c = SSD_ROUNDS[n]
                    pe.wait_ge(decay_ready, L * 8 + (n + 1))
                    pe.wait_ge(*free(("y", n), L))
                    for r in range(SSD_R):
                        hd = SSD_R * g + r
                        last = mm(ps(("y", n))[:, r * SSD_P:(r + 1) * SSD_P], E[:, n % 2, r, :],
                                  xdt[:, c, hd * SSD_P:(hd + 1) * SSD_P], start=True, stop=True)
                    if c == 1:
                        last = mm(ps(("y", n))[:, GW:2 * GW], cbm[:, g % 2, 2, :],
                                  xde[:, g * GW:(g + 1) * GW], start=True, stop=True)
                    done(last, ("y", n))

                for n, (g, c) in enumerate(SSD_ROUNDS):
                    if n in SSD_FILL:
                        tokens(SSD_FILL[n][0], SSD_FILL[n][1], hT)
                    if c == 0:
                        pe.wait_ge(*free(("cb", g), L))
                        for i, (s, l) in enumerate(((0, 0), (1, 1), (0, 1))):
                            last = mm(ps(("cb", g))[:, i * P:(i + 1) * P], xconv[:, 8 + g, s * P:(s + 1) * P],
                                      xconv[:, 12 + g, l * P:(l + 1) * P], start=True, stop=True)
                        done(last, ("cb", g))
                    pe.wait_ge(seg_built, L * 8 + (n + 1))
                    pe.wait_ge(*free(("seg", n), L))
                    for r in range(SSD_R):
                        last = mm(ps(("seg", n))[:, r * P:(r + 1) * P], segs[:, n % 2, r, :], upto,
                                  start=True, stop=True)
                    done(last, ("seg", n))
                    if n == 1:
                        pe.wait_ge(xdt_ready, L + 1)
                    if n >= 1:
                        y(n - 1)
                y(len(SSD_ROUNDS) - 1)
                pe.wait_ge(*taken(("PV", 3, 1), L))
                tokens("b_att0", ("branch", 2), attT)
                tokens("b_att1", ("branch", 3), attT)
                tokens("g_ssd0", ("gate", 0), hT)
                tokens("g_ssd1", ("gate", 1), hT)
                for t in range(TT):
                    transposes("yT", t, xtok, (ssd_ready, L * TT + (t + 1)))
                token_pair("b_ssd0", "b_ssd1", ("branch", 0), ("branch", 1), yT,
                           lambda t: pe.wait_ge(*taken(("yT", t, 1), L)))

                def merged_tile(t):
                    transposes("mT", t, G[:, 0, :, :], (merged_ready, L * TT + (t + 1)))
                    pe.wait_ge(*taken(("mT", t, 1), L))

                token_pair("out0", "out1", ("out", 0), ("out", 1), hT, merged_tile)

                pe.wait_ge(*free("pT", L))
                for k in range(2):
                    for t in range(TT):
                        last = tr(ps("pT")[:, k * SEQ + t * P:k * SEQ + (t + 1) * P],
                                  prow[:, t, k * P:(k + 1) * P], ident)
                done(last, "pT")
                arrived(("ple_proj", 0))
                wp = slot(("ple_proj", 0))[:, 0:2 * D].rearrange("p (k n) -> p k n", k=2)

                def projection(t):
                    for j in range(2):
                        name = ("proj", t, j)
                        pe.wait_ge(*free(name, L))
                        for k in range(2):
                            last = mm(ps(name)[:, :], pT[:, k, t * P:(t + 1) * P],
                                      wp[:, k, j * HALF:(j + 1) * HALF], start=k == 0, stop=k == 1)
                            if t + j + k == 0:
                                last.then_inc(unit_free, 1)
                        done(last, name)

                h_transposed("hT2", 0, 1)
                pe.wait_ge(*taken("pT", L))
                projection(0)
                h_transposed("hT2", 1, 1)
                pe.wait_ge(*taken(("hT2", 1, 1), L))
                pe.wait_ge(*free("router", L))
                for t in range(TT):
                    for k in range(KT):
                        last = mm(ps("router")[:, t * 20:(t + 1) * 20], hT[:, k, t * P:(t + 1) * P],
                                  rw[:, k, :], start=k == 0, stop=k == KT - 1)
                done(last, "router")
                projection(1)
                pe.wait_ge(group_ready, L + 1)
                pe.wait_ge(*free("rank", L))
                hot = rt[:, 6, :, 0:MOE_G]
                mm(ps("rank")[:, 0:4], upto, hot[:, 0, :], start=True, stop=True)
                mm(ps("rank")[:, 4:8], upto, hot[:, 1, :], start=True, stop=False)
                mm(ps("rank")[:, 4:8], ones, hot[:, 0, :], start=False, stop=True)
                mm(ps("rank")[:, 8:12], ones, hot[:, 0, :], start=True, stop=False)
                done(mm(ps("rank")[:, 8:12], ones, hot[:, 1, :], start=False, stop=True), "rank")

                def gate_up(e, parts, cols):
                    arrived(("gu", e))
                    n = cols.shape[-1]
                    for i, (name, at) in enumerate(parts):
                        w = slot(("gu", e))[:, i * 2048:(i + 1) * 2048].rearrange("p (k n) -> p k n", k=KT)
                        if i == 0 or name != parts[0][0]:
                            pe.wait_ge(*free(name, L))
                        for f in range(2):
                            for k in range(KT):
                                last = mm(ps(name)[:, at + f * n:at + (f + 1) * n], w[:, k, f * P:(f + 1) * P],
                                          cols[:, k, :], start=k == 0, stop=k == KT - 1)
                                if i + f + k == 0:
                                    last.then_inc(unit_free, 1)
                        if i == 1 or name != parts[1][0]:
                            done(last, name)

                def free_acc():
                    for t in range(TT):
                        for j in range(2):
                            pe.wait_ge(*free(("acc", t, j), L))

                pe.wait_ge(flag_ready, L + 1)
                pe.sem_inc(passed_wait, 1)
                with pe.If(pe.value_load(overflow[0:1, 0:1], min_val=0, max_val=1) == 0):
                    pe.wait_ge(sel_ready, L + 1)
                    for d in range(KT):
                        name = ("sorted", d)
                        pe.wait_ge(*free(name, L))
                        for t in range(TT):
                            last = mm(ps(name)[:, 0:NS], h[:, t, d * P:(d + 1) * P], sel[:, t, :],
                                      start=t == 0, stop=t == 1)
                        done(last, name)
                    pe.wait_ge(*taken(("sorted", KT - 1), L))

                    def back(g):
                        pe.wait_ge(*taken(("yg", g, 1), L))
                        if g == 0:
                            free_acc()
                        for t in range(TT):
                            for j in range(2):
                                last = mm(ps(("acc", t, j))[:, :], selT[0:CAP, g, t * P:(t + 1) * P],
                                          yg[0:CAP, g % 2, j * HALF:(j + 1) * HALF],
                                          start=g == 0, stop=g == MOE_G - 1)
                                if g == MOE_G - 1:
                                    done(last, ("acc", t, j))

                    for e in range(NE):
                        g = e // MOE_E
                        gate_up(e, [(("hgu", e), 0), (("hgu", e), 2 * CAP)], hS[:, :, g * CAP:(g + 1) * CAP])
                        if e == 1:
                            pe.wait_ge(combine_ready, L + 1)
                            for gg in range(MOE_G):
                                pe.wait_ge(*free(("weight", gg), L))
                                for i in range(MOE_E):
                                    x1 = MOE_E * gg + i
                                    for t in range(TT):
                                        last = mm(ps(("weight", gg))[:, i * CAP:(i + 1) * CAP],
                                                  rt[:, COMBINE, t, x1:x1 + 1].to_broadcast([P, P]),
                                                  sel[:, t, gg * CAP:(gg + 1) * CAP], start=t == 0, stop=t == 1)
                                done(last, ("weight", gg))
                            for gg in range(MOE_G):
                                pe.wait_ge(*free(("back", gg), L))
                                for t in range(TT):
                                    last = tr(ps(("back", gg))[0:CAP, t * P:(t + 1) * P],
                                              sel[:, t, gg * CAP:(gg + 1) * CAP], ident)
                                done(last, ("back", gg))
                        if e % MOE_E == 1 and g >= 1:
                            back(g - 1)
                        if e % 2 == 0:
                            continue
                        arrived(("down", e - 1))
                        for i in range(2):
                            w = slot(("down", e - 1))[:, i * 2048:(i + 1) * 2048].rearrange("p (k n) -> p k n", k=2)
                            pe.wait_ge(act_ready, L * NE + (e + i))
                            for j in range(2):
                                if e % MOE_E == 1 and i == 0:
                                    pe.wait_ge(*free(("yg", g, j), L))
                                for k in range(2):
                                    last = mm(ps(("yg", g, j))[0:CAP, :], act_t[:, i, k * CAP:(k + 1) * CAP],
                                              w[:, k, j * HALF:(j + 1) * HALF],
                                              start=e % MOE_E + i + k == 1, stop=e % MOE_E + i + k == MOE_E + 1)
                                    if i + j + k == 0:
                                        last.then_inc(unit_free, 1)
                                if e % MOE_E == MOE_E - 1 and i == 1:
                                    done(last, ("yg", g, j))
                    back(MOE_G - 1)
                with pe.Else():
                    for e in range(0, NE, 2):
                        gate_up(e, [(("hg", e), 0), (("hu", e), 0)], hT)
                        gate_up(e + 1, [(("hg", e + 1), 0), (("hu", e + 1), 0)], hT)
                        if e == 0:
                            pe.wait_ge(combine_ready, L + 1)
                            for b in range(NE // 2):
                                pe.wait_ge(*free(("comb", b), L))
                                for i in range(2):
                                    x1 = 2 * b + i
                                    for t in range(TT):
                                        last = mm(ps(("comb", b))[:, i * SEQ + t * P:i * SEQ + (t + 1) * P],
                                                  rt[:, COMBINE, t, x1:x1 + 1].to_broadcast([P, P]), ident,
                                                  start=True, stop=True)
                                done(last, ("comb", b))
                            free_acc()
                        arrived(("down", e))
                        for i in range(2):
                            w = slot(("down", e))[:, i * 2048:(i + 1) * 2048].rearrange("p (k n) -> p k n", k=2)
                            pe.wait_ge(act_ready, L * NE + (e + i + 1))
                            for t in range(TT):
                                for j in range(2):
                                    for k in range(2):
                                        last = mm(ps(("acc", t, j))[:, :],
                                                  act_t[:, i, k * SEQ + t * P:k * SEQ + (t + 1) * P],
                                                  w[:, k, j * HALF:(j + 1) * HALF],
                                                  start=e + i + k == 0, stop=e + i + k == NE)
                                        if i + t + j + k == 0:
                                            last.then_inc(unit_free, 1)
                                    if e + i == NE - 1:
                                        done(last, ("acc", t, j))

                def embedding_tile(t):
                    h_transposed("hT3", t, 2)
                    pe.wait_ge(*taken(("hT3", t, 1), L))

                token_pair("pg0", "pg1", ("ple_gate", 0), ("ple_gate", 1), hT, embedding_tile)

        @block.scalar
        def _(act):
            def ev(out_, name, L, func=ACT.Copy, in_=None, last=True, **kw):
                ins = nc.scalar.activation(out_, ps(name)[:, :] if in_ is None else in_, func, **kw)
                if last:
                    ins.then_inc(bank_free[JOB_AT[name][0]], 1)

            act.dma_start(cst[:, P:NCONST], consts[:, P:NCONST]).then_inc(const_loaded, 16)
            act.wait_ge(angles_ready, 1)
            nc.scalar.activation(sinT[:], ang[:, 2], ACT.Sin)
            nc.scalar.activation(cosT[:], ang[:, 3], ACT.Sin).then_inc(sines_done, 1)
            with act.Fori(0, DEPTH) as L:

                def evict_transposed(name, dst):
                    for t in range(TT):
                        for j in range(2):
                            act.wait_ge(*full((name, t, j), L))
                            ev(dst[:, 4 * j:4 * j + 4, t * P:(t + 1) * P], (name, t, j), L,
                               in_=ps((name, t, j)).rearrange("p (a b) -> p a b", a=4))

                def evict_pair(name, n, dst, func):
                    for t in range(TT):
                        act.wait_ge(*full((name, t), L))
                        ev(dst[:, t, n * HALF:(n + 1) * HALF], (name, t), L, func)

                def xbc(n):
                    for b in range(2):
                        act.wait_ge(*full((f"xbc{n}", b), L))
                        if n >= 2 and b == 0:
                            act.wait_ge(conv_done, L * 4 + (n - 1))
                        ev(xin[:, n % 2, 2 * b:2 * b + 2, 3:3 + SEQ], (f"xbc{n}", b), L,
                           in_=ps((f"xbc{n}", b)).rearrange("p (a b) -> p a b", a=2))

                def silu(n):
                    act.wait_ge(conv_done, L * 4 + (n + 1))
                    v = xconv[:, 4 * n:4 * n + 4, :]
                    nc.scalar.activation(v, v, ACT.Silu).then_inc(silu_done, 1)

                def exp_scores(r):
                    t, _ = ROUNDS[r]
                    act.wait_ge(scores_ready, L * 4 + (r + 1))
                    v = P0[:, :, :] if t == 0 else P1[:, :, CHUNK:SEQ]
                    nc.scalar.activation(amax[:, 3 + (r % 2), :], amax[:, 1 + (r % 2), :], ACT.Exp)
                    nc.scalar.activation(v, v, ACT.Exp).then_inc(exp_done, 1)

                def probs_values(r):
                    t, half = ROUNDS[r]
                    for b in range(2 if t == 0 else 4):
                        act.wait_ge(*full(("PT", r, b), L))
                        o = PTs[:, 0, b] if t == 0 else PTs[:, b // 2, b % 2]
                        ev(o.rearrange("p a b -> p (a b)"), ("PT", r, b), L)
                    for g in range(2):
                        act.wait_ge(*full(("PV", r, g), L))
                        v = ps(("PV", r, g))[0:HD, :].rearrange("p (a b c) -> p a b c", a=2, b=2)
                        f = 4 * half + 2 * g
                        for b in range(2):
                            ev(attT[b * HD:(b + 1) * HD, f:f + 2, t * P:(t + 1) * P], ("PV", r, g), L,
                               in_=v[:, :, b, :], last=b == 1)

                evict_transposed("hT1", hT)
                evict_pair("pu0", 0, xtok, ACT.Copy)
                evict_pair("pu1", 1, xtok, ACT.Copy)
                for t in range(TT):
                    for j in range(2):
                        act.wait_ge(*full(("qT", t, j), L))
                        ev(qT[:, 4 * j:4 * j + 4, t * P:(t + 1) * P], ("qT", t, j), L,
                           in_=ps(("qT", t, j)).rearrange("p (a b) -> p a b", a=4))
                    act.wait_ge(*full(("kT", t), L))
                    ev(kT[:, :, t * P:(t + 1) * P], ("kT", t), L,
                       in_=ps(("kT", t)).rearrange("p (a b) -> p a b", a=4))
                xbc(0)
                xbc(1)
                silu(0)
                pooled = xdt[:, :, :].rearrange("p a b -> p (a b)")
                for j in range(4):
                    act.wait_ge(*full(("pooled", j), L))
                    ev(pooled[:, j * HALF:(j + 1) * HALF], ("pooled", j), L)
                xbc(2)
                silu(1)
                for j in range(4):
                    act.wait_ge(*full(("mixed", j), L))
                    for i in range(2):
                        f = 2 * j + i
                        ev(poolT[:, f, :], ("mixed", j), L, in_=ps(("mixed", j))[:, i * SEQ:(i + 1) * SEQ],
                           scale=vecT[:, V_PS + f:V_PS + f + 1], last=i == 1)
                xbc(3)
                silu(2)
                silu(3)
                act.wait_ge(dt_pre, L + 1)
                nc.scalar.activation(sm[:, 2, :], sm[:, 1, :], ACT.Exp, scale=-1.0)
                nc.scalar.activation(sm[:, 3, 0:16], rows[:, 16:32], ACT.Exp).then_inc(dt_exp, 1)
                exp_scores(0)
                exp_scores(1)
                evict_pair("g_pool0", 0, G[:, 0], ACT.Sigmoid)
                probs_values(0)
                evict_pair("g_pool1", 1, G[:, 0], ACT.Sigmoid)
                probs_values(1)
                exp_scores(2)
                exp_scores(3)
                probs_values(2)
                zs = qT.rearrange("p a b -> p (a b)").rearrange("p (t d) -> p t d", t=TT)
                evict_pair("z0", 0, zs, ACT.Silu)
                probs_values(3)
                act.wait_ge(*full("dsum", L))
                ev(dexp[:, :, :], "dsum", L, ACT.Exp,
                   in_=ps("dsum")[:, 0:32].rearrange("p (a b) -> p a b", a=2))
                for j in range(4):
                    act.wait_ge(*full(("xT", j), L))
                    ev(xtok[:, j // 2, (j % 2) * HALF:(j % 2 + 1) * HALF], ("xT", j), L)
                for n in range(len(SSD_ROUNDS)):
                    if n == 1:
                        evict_pair("z1", 1, zs, ACT.Silu)
                    if n in (3, 5):
                        evict_pair(f"g_att{n // 2 - 1}", n // 2 - 1, G[:, 1], ACT.Sigmoid)
                    act.wait_ge(*full(("seg", n), L))
                    ev(E[:, n % 2, :, :].rearrange("p a b -> p (a b)"), ("seg", n), L, ACT.Exp)
                act.wait_ge(gy_ms, L + 1)
                nc.scalar.activation(gss[:, 1], gss[:, 0], ACT.Sqrt).then_inc(gy_sqrt, 1)
                act.wait_ge(merge_step, L * 2 + 2)
                evict_pair("g_ssd0", 0, G[:, 1], ACT.Sigmoid)
                evict_pair("g_ssd1", 1, G[:, 1], ACT.Sigmoid)
                for t in range(TT):
                    for j in range(2):
                        act.wait_ge(*full(("yT", t, j), L))
                        for i in range(4):
                            f = 4 * j + i
                            ev(yT[:, f, t * P:(t + 1) * P], ("yT", t, j), L,
                               in_=ps(("yT", t, j))[:, i * P:(i + 1) * P],
                               scale=vecT[:, V_NW + f:V_NW + f + 1], last=i == 3)
                evict_transposed("mT", hT)

                def ln_sqrt(i, t):
                    act.wait_ge(var_ready, L * 6 + (2 * i + t + 1))
                    nc.scalar.activation(rstd[:, 0, t:t + 1], mv[:, t, 1:2], ACT.Sqrt).then_inc(sqrt_done, 1)

                ln_sqrt(0, 0)
                act.wait_ge(*full("pT", L))
                ev(PTs[:, 0, 0, :, :].rearrange("p a b -> p (a b)"), "pT", L)
                ln_sqrt(0, 1)
                evict_transposed("hT2", hT)
                act.wait_ge(rexp_in, L * 2 + 1)
                nc.scalar.activation(rt[:, 3, :, 0:4], rt[:, 2, :, 0:4], ACT.Exp).then_inc(rexp_out, 1)
                act.wait_ge(rexp_in, L * 2 + 2)
                nc.scalar.activation(rt[:, 12, :, 0:1], rt[:, 11, :, 0:1], ACT.Exp).then_inc(rexp_out, 1)
                for t in range(TT):
                    for j in range(2):
                        act.wait_ge(*full(("proj", t, j), L))
                        ev(xtok[:, t, j * HALF:(j + 1) * HALF], ("proj", t, j), L)

                def act_s_free(e):
                    if e >= 2:
                        act.wait_ge(act_ready, L * NE + (e - 1))

                act.wait_ge(flag_ready, L + 1)
                act.sem_inc(passed_wait, 1)
                with act.If(act.value_load(overflow[0:1, 0:1], min_val=0, max_val=1) == 0):
                    for d in range(KT):
                        act.wait_ge(*full(("sorted", d), L))
                        ev(hS[:, d, :], ("sorted", d), L, in_=ps(("sorted", d))[:, 0:NS])
                    for e in range(NE):
                        act.wait_ge(*full(("hgu", e), L))
                        act_s_free(e)
                        nc.scalar.activation(act_s[:, e % 2, 0:2 * CAP], ps(("hgu", e))[:, 0:2 * CAP],
                                             ACT.Silu).then_inc(silu_s, 1)
                        if e == 1:
                            for g in range(MOE_G):
                                act.wait_ge(*full(("weight", g), L))
                                ev(wS[:, MOE_E * g:MOE_E * (g + 1), :].rearrange("p a b -> p (a b)"),
                                   ("weight", g), L, in_=ps(("weight", g))[:, 0:MOE_E * CAP])
                            for g in range(MOE_G):
                                act.wait_ge(*full(("back", g), L))
                                ev(selT[0:CAP, g, :], ("back", g), L, in_=ps(("back", g))[0:CAP, 0:SEQ])
                        if e % MOE_E == MOE_E - 1:
                            g = e // MOE_E
                            for j in range(2):
                                act.wait_ge(*full(("yg", g, j), L))
                                ev(yg[0:CAP, g % 2, j * HALF:(j + 1) * HALF], ("yg", g, j), L,
                                   in_=ps(("yg", g, j))[0:CAP, :])
                with act.Else():
                    for e in range(NE):
                        act.wait_ge(*full(("hg", e), L))
                        act_s_free(e)
                        ev(act_s[:, e % 2, :], ("hg", e), L, ACT.Silu)
                        if e == 1:
                            for b in range(NE // 2):
                                act.wait_ge(*full(("comb", b), L))
                                ev(comb[:, 2 * b:2 * b + 2, :].rearrange("p a b -> p (a b)"), ("comb", b), L)
                    act.sem_inc(silu_s, NE)
                ln_sqrt(1, 0)
                ln_sqrt(1, 1)
                evict_transposed("hT3", hT)
                for t in range(TT):
                    for j in range(2):
                        act.wait_ge(*full((f"pg{j}", t), L))
                        ev(G[:, 0, t, j * HALF:(j + 1) * HALF], (f"pg{j}", t), L, ACT.Sigmoid)
                ln_sqrt(2, 0)
                ln_sqrt(2, 1)

        @block.gpsimd
        def _(pool):
            with nc.allow_non_contiguous_dma(reason="256 positions, once"):
                pool.dma_start(posi[:], positions[0].rearrange("(t p) -> p t", p=P)).then_inc(pos_loaded, 16)
            with pool.Fori(0, DEPTH) as L:
                pool.wait_ge(params_free, L + 1)
                pool.sem_inc(passed_wait, 1)
                T = XBC_T
                loads = [
                    (vecrows[0:SSD_CONV * T, :], conv_w[L].rearrange("k (c p) -> (k c) p", p=P)),
                    (vecrows[V_CB:V_CB + T, :], conv_b[L].rearrange("(c p) -> c p", p=P)),
                    (vecrows[V_PS:V_PS + KT, :], pool_scale[L].rearrange("(c p) -> c p", p=P)),
                    (vecrows[V_NW:V_NW + KT, :], norm_w[L].rearrange("(c p) -> c p", p=P)),
                    (rows[:, 0:16], dt_bias[L].unsqueeze(0).broadcast_to([P, 16])),
                    (rows[:, 16:32], a_log[L].unsqueeze(0).broadcast_to([P, 16])),
                    (rows[:, 32:48], ssd_d[L].unsqueeze(0).broadcast_to([P, 16])),
                    (rows[:, 48:64], sinks[L].unsqueeze(0).broadcast_to([P, 16])),
                    (rows[:, 64:68], rg_b[L].unsqueeze(0).broadcast_to([P, 4])),
                    (rows[:, 68:84], re_b[L].unsqueeze(0).broadcast_to([P, 16])),
                    (rw[:, :, 0:4], rg_w[L].rearrange("(k p) n -> p k n", p=P)),
                    (rw[:, :, 4:20], re_w[L].rearrange("(k p) n -> p k n", p=P)),
                    (prow[:, :, :], p[L, 0].rearrange("(t p) n -> p t n", p=P)),
                ]
                assert 16 * len(loads) == PARAM_INC
                for d, s in loads:
                    pool.dma_start(d, s).then_inc(params_full, 16)

                def ln_params(i, g, b):
                    pool.wait_ge(lnp_free, L * 3 + (i + 1))
                    pool.sem_inc(passed_wait, 1)
                    for j, v in enumerate((g, b)):
                        pool.dma_start(lnp[:, j, :], v[L].unsqueeze(0).broadcast_to([P, D])).then_inc(lnp_full, 16)

                ln_params(0, ln1_g, ln1_b)
                pool.wait_ge(dA_ready, L + 1)
                for n, (g, c) in enumerate(SSD_ROUNDS):
                    if n >= 2:
                        pool.wait_ge(*full(("seg", n - 2), L))
                    nc.gpsimd.tensor_tensor(
                        segs[:, n % 2, :, :], after.unsqueeze(1).broadcast_to([P, SSD_R, P]),
                        dA[:, c, SSD_R * g:SSD_R * (g + 1)].unsqueeze(2).broadcast_to([P, SSD_R, P]),
                        ALU.mult).then_inc(seg_built, 1)
                ln_params(1, ln2_g, ln2_b)
                ln_params(2, ln3_g, ln3_b)

        @block.vector
        def _(dve):
            V = nc.vector
            steps = [0]

            def link(ins, base):
                steps[0] += 1
                ins.then_inc(dve_step, 1)
                dve.wait_ge(dve_step, base + steps[0])

            def frees(ins, name):
                ins.then_inc(bank_free[JOB_AT[name][0]], 1)

            V.memset(P1[:, :, 0:CHUNK], 0.0).then_inc(h_ready, 2)
            for t in range(TT):
                dve.wait_ge(start_loads[t], 32 - 16 * t)
            dve.wait_ge(const_loaded, 16)
            dve.wait_ge(pos_loaded, 16)
            link(V.tensor_copy(posf[:], posi[:]), 0)
            for t in range(TT):
                last = V.tensor_scalar(ang[:, 0, t, :], const("inv"), posf[:, t:t + 1], None, ALU.mult)
            link(last, 0)
            link(V.tensor_scalar(ang[:, 1], ang[:, 0], float(1 / (2 * np.pi)), None, ALU.mult), 0)
            link(V.tensor_scalar(ang[:, 1], ang[:, 1], ROUND, None, ALU.add), 0)
            link(V.tensor_scalar(ang[:, 1], ang[:, 1], -ROUND, None, ALU.add), 0)
            link(V.scalar_tensor_tensor(out=ang[:, 2], in0=ang[:, 1], scalar=-TWO_PI[0], in1=ang[:, 0],
                                        op0=ALU.mult, op1=ALU.add), 0)
            for part in TWO_PI[1:]:
                link(V.scalar_tensor_tensor(out=ang[:, 2], in0=ang[:, 1], scalar=-part, in1=ang[:, 2],
                                            op0=ALU.mult, op1=ALU.add), 0)
            link(V.tensor_scalar(ang[:, 2], ang[:, 2], PI_F, -PI_F, ALU.min, ALU.max), 0)
            link(V.tensor_scalar(ang[:, 3], ang[:, 2], float(np.pi / 2), None, ALU.add), 0)
            link(V.tensor_scalar(ang[:, 1], ang[:, 3], PI_F, float(-2 * np.pi), ALU.is_gt, ALU.mult), 0)
            link(V.tensor_tensor(ang[:, 3], ang[:, 3], ang[:, 1], ALU.add), 0)
            V.tensor_scalar(ang[:, 3], ang[:, 3], PI_F, -PI_F, ALU.min, ALU.max).then_inc(angles_ready, 1)
            dve.wait_ge(sines_done, 1)
            link(V.tensor_scalar(nsinT[:], sinT[:], -1.0, None, ALU.mult), 0)
            dve.sem_inc(params_free, 1)
            dve.sem_inc(lnp_free, 1)
            setup_steps = steps[0]
            with dve.Fori(0, DEPTH) as L:
                steps[0] = 0
                base = L * DVE_STEPS + setup_steps

                def lk(ins):
                    link(ins, base)

                def rope(name, t, dsts):
                    n = dsts[0].shape[1]
                    v = ps(name)[:, 0:n * HD].rearrange("p (h a d) -> p h a d", a=2, d=ROT)
                    A = tA[:, 0:n * HD].rearrange("p (h a d) -> p h a d", a=2, d=ROT)
                    B = tB[:, 0:n * HD].rearrange("p (h a d) -> p h a d", a=2, d=ROT)
                    c = cosT[:, t, :].unsqueeze(1).unsqueeze(1).broadcast_to([P, n, 2, ROT])
                    s = sinT[:, t, :].unsqueeze(1).broadcast_to([P, n, ROT])
                    ns = nsinT[:, t, :].unsqueeze(1).broadcast_to([P, n, ROT])
                    dve.wait_ge(*full(name, L))
                    V.tensor_tensor(A, v, c, ALU.mult)
                    V.tensor_tensor(B[:, :, 0, :], v[:, :, 1, :], ns, ALU.mult)
                    lk(V.tensor_tensor(B[:, :, 1, :], v[:, :, 0, :], s, ALU.mult))
                    for d in dsts:
                        last = V.tensor_tensor(d, tA[:, 0:n * HD].rearrange("p (h d) -> p h d", d=HD),
                                               tB[:, 0:n * HD].rearrange("p (h d) -> p h d", d=HD), ALU.add)
                    return last

                V.memset(xin[:, :, :, 0:3], 0.0)
                for n in range(2):
                    for t in range(TT):
                        rot = G[:, t, :, :].rearrange("p a b -> p (a b)")
                        d = rot[:, n * HALF:(n + 1) * HALF].rearrange("p (h d) -> p h d", d=HD)
                        name = (f"q{n}", t)
                        ins = rope(name, t, [d])
                        frees(ins, name)
                        steps[0] += 0
                        dve.wait_ge(*taken(name, L))
                for t in range(TT):
                    rot = G[:, t, :, :].rearrange("p a b -> p (a b)")
                    k2 = rot[:, D:D + 2 * KV_HEADS * HD].rearrange("p (h c d) -> p h c d", c=2, d=HD)
                    lk(rope(("kv", t), t, [k2[:, :, 0, :], k2[:, :, 1, :]]))
                    frees(V.tensor_copy(vv[:, t, :], ps(("kv", t))[:, KV_HEADS * HD:2 * KV_HEADS * HD]), ("kv", t))
                    dve.wait_ge(*taken(("kv", t), L))
                    dve.sem_inc(qrot_ready, 1)
                dve.wait_ge(*full("vec", L))
                frees(V.tensor_copy(vecT[:], ps("vec")[:, 0:VEC_ROWS]), "vec")
                dve.wait_ge(*taken("vec", L))

                def conv(n):
                    dve.wait_ge(*taken((f"xbc{n}", 1), L))
                    for k in (3, 2, 1, 0):
                        for i in range(4):
                            f = 4 * n + i
                            u = xin[:, n % 2, i, k:k + SEQ]
                            w = vecT[:, k * XBC_T + f:k * XBC_T + f + 1]
                            if k == 3:
                                last = V.tensor_scalar(xconv[:, f, :], u, w, vecT[:, V_CB + f:V_CB + f + 1],
                                                       ALU.mult, ALU.add)
                            else:
                                last = V.scalar_tensor_tensor(out=xconv[:, f, :], in0=u, scalar=w,
                                                              in1=xconv[:, f, :], op0=ALU.mult, op1=ALU.add)
                        if k:
                            lk(last)
                    last.then_inc(conv_done, 1)

                def shifted_scores(r):
                    t, half = ROUNDS[r]
                    per = 4 if t == 0 else 2
                    w = P if t == 0 else 192
                    mask = const("mask0") if t == 0 else const("mask1")
                    buf = P0[:, :, :] if t == 0 else P1[:, :, CHUNK:SEQ]
                    for b in range(8 // per):
                        dve.wait_ge(*full(("scores", r, b), L))
                        v = ps(("scores", r, b)).rearrange("p (h k) -> p h k", h=per)[:, :, 0:w]
                        o = (buf.rearrange("p (i c) k -> p c i k", c=2)[:, b] if t == 0 else
                             buf.rearrange("p (m i c) k -> p m c i k", m=2, c=2)[:, b // 2, b % 2])
                        frees(V.scalar_tensor_tensor(out=o, in0=v, scalar=HD ** -0.5,
                                                     in1=mask.unsqueeze(1).broadcast_to([P, per, w]),
                                                     op0=ALU.mult, op1=ALU.add), ("scores", r, b))
                    dve.wait_ge(*taken(("scores", r, 8 // per - 1), L))
                    lk(V.tensor_reduce(amax[:, 0, :], buf, AX.X, ALU.max))
                    sink = rows[:, 48 + 8 * half:56 + 8 * half]
                    lk(V.tensor_tensor(amax[:, 0, :], amax[:, 0, :], sink, ALU.max))
                    V.tensor_tensor(amax[:, 1 + (r % 2), :], sink, amax[:, 0, :], ALU.subtract)
                    V.tensor_tensor(buf, buf, amax[:, 0, :].unsqueeze(2).broadcast_to([P, 8, w]),
                                    ALU.subtract).then_inc(scores_ready, 1)

                def normalise(r):
                    t, _ = ROUNDS[r]
                    w = P if t == 0 else 192
                    buf = P0[:, :, :] if t == 0 else P1[:, :, CHUNK:SEQ]
                    dve.wait_ge(exp_done, L * 4 + (r + 1))
                    lk(V.tensor_reduce(amax[:, 5, :], buf, AX.X, ALU.add))
                    lk(V.tensor_tensor(amax[:, 5, :], amax[:, 5, :], amax[:, 3 + (r % 2), :], ALU.add))
                    lk(V.reciprocal(amax[:, 6, :], amax[:, 5, :]))
                    V.tensor_tensor(buf, buf, amax[:, 6, :].unsqueeze(2).broadcast_to([P, 8, w]),
                                    ALU.mult).then_inc(probs_ready, 1)

                dve.wait_ge(params_full, L * PARAM_INC + PARAM_INC)
                conv(0)
                shifted_scores(0)
                conv(1)
                conv(2)
                shifted_scores(1)
                conv(3)

                dve.wait_ge(*full("dt", L))
                frees(V.tensor_tensor(sm[:, 0, :].rearrange("p (t h) -> p t h", t=TT),
                                      ps("dt")[:, 0:32].rearrange("p (t h) -> p t h", t=TT),
                                      rows[:, 0:16].unsqueeze(1).broadcast_to([P, TT, 16]), ALU.add), "dt")
                dve.wait_ge(*taken("dt", L))
                V.scalar_tensor_tensor(out=sm[:, 1, :], in0=sm[:, 0, :], scalar=-1.0, in1=sm[:, 0, :],
                                       op0=ALU.mult, op1=ALU.max).then_inc(dt_pre, 1)
                V.tensor_scalar(sm[:, 4, :], sm[:, 0, :], 0.0, None, ALU.max)
                dve.wait_ge(dt_exp, L + 1)
                lk(V.tensor_scalar(sm[:, 5, :], sm[:, 2, :], 2.0, None, ALU.add))
                lk(V.reciprocal(sm[:, 6, :], sm[:, 5, :]))
                lk(V.tensor_tensor(sm[:, 7, :], sm[:, 6, :], sm[:, 2, :], ALU.mult))
                lk(V.tensor_tensor(sm[:, 8, :], sm[:, 7, :], sm[:, 7, :], ALU.mult))
                lk(V.tensor_scalar(sm[:, 9, :], sm[:, 8, :], 1.0 / 15, None, ALU.mult))
                for m in (13, 11, 9, 7, 5, 3):
                    lk(V.scalar_tensor_tensor(out=sm[:, 9, :], in0=sm[:, 9, :], scalar=1.0 / m, in1=sm[:, 8, :],
                                              op0=ALU.add, op1=ALU.mult))
                lk(V.scalar_tensor_tensor(out=sm[:, 9, :], in0=sm[:, 9, :], scalar=1.0, in1=sm[:, 7, :],
                                          op0=ALU.add, op1=ALU.mult))
                V.tensor_scalar(nega[:], sm[:, 3, 0:16], -1.0, None, ALU.mult)
                lk(V.scalar_tensor_tensor(out=dtv[:, :, :].rearrange("p a b -> p (a b)"), in0=sm[:, 9, :], scalar=2.0,
                                          in1=sm[:, 4, :], op0=ALU.mult, op1=ALU.add))
                V.tensor_tensor(dA[:, :, :], dtv[:, :, :], nega[:].unsqueeze(1).broadcast_to([P, TT, 16]),
                                ALU.mult).then_inc(dA_ready, 1)

                normalise(0)
                normalise(1)
                shifted_scores(2)
                shifted_scores(3)

                def gated(name, n, g):
                    for t in range(TT):
                        gate = G[:, g, t, n * HALF:(n + 1) * HALF]
                        dve.wait_ge(*full((name, t), L))
                        frees(V.tensor_tensor(gate, gate, ps((name, t))[:, :], ALU.mult), (name, t))

                dve.wait_ge(*taken(("g_pool1", 1), L))
                gated("b_pool0", 0, 0)
                normalise(2)
                gated("b_pool1", 1, 0)
                dve.wait_ge(*taken(("b_pool1", 1), L))
                dve.sem_inc(merge_step, 1)
                normalise(3)

                def heads(ap):
                    return ap.rearrange("p (h d) -> p h d", d=SSD_P)

                for t in range(TT):
                    dve.wait_ge(*taken(("xT", 2 * t + 1), L))
                    lk(V.tensor_tensor(heads(xdt[:, t, :]), heads(xtok[:, t, :]),
                                       dtv[:, t, :].unsqueeze(2).broadcast_to([P, 16, SSD_P]), ALU.mult))
                    lk(V.tensor_tensor(heads(xtok[:, t, :]), heads(xtok[:, t, :]),
                                       rows[:, 32:48].unsqueeze(2).broadcast_to([P, 16, SSD_P]), ALU.mult))
                V.tensor_tensor(heads(xde), heads(xdt[:, 0, :]),
                                dexp[:, 0, :].unsqueeze(2).broadcast_to([P, 16, SSD_P]),
                                ALU.mult).then_inc(xdt_ready, 1)

                def y(n):
                    g, c = SSD_ROUNDS[n]
                    name = ("y", n)
                    dst = xtok[:, c, g * GW:(g + 1) * GW]
                    dve.wait_ge(*full(name, L))
                    if c == 1:
                        V.tensor_tensor(heads(tA[:, 0:GW]), heads(ps(name)[:, GW:2 * GW]),
                                        dexp[:, 1, SSD_R * g:SSD_R * (g + 1)].unsqueeze(2)
                                        .broadcast_to([P, SSD_R, SSD_P]), ALU.mult)
                    frees(V.tensor_tensor(dst, dst, ps(name)[:, 0:GW], ALU.add), name)
                    if c == 1:
                        dve.wait_ge(*taken(name, L))
                        lk(V.tensor_tensor(dst, dst, tA[:, 0:GW], ALU.add))

                for n, (g, c) in enumerate(SSD_ROUNDS):
                    if c == 0:
                        dve.wait_ge(*full(("cb", g), L))
                        V.tensor_tensor(cbm[:, g % 2, 0:2, :], ps(("cb", g))[:, 0:2 * P].rearrange("p (a b) -> p a b", a=2),
                                        upto.unsqueeze(1).broadcast_to([P, 2, P]), ALU.mult)
                        frees(V.tensor_copy(cbm[:, g % 2, 2, :], ps(("cb", g))[:, 2 * P:3 * P]), ("cb", g))
                        dve.wait_ge(*taken(("cb", g), L))
                    dve.wait_ge(*taken(("seg", n), L))
                    V.tensor_tensor(E[:, n % 2, :, :], E[:, n % 2, :, :],
                                    cbm[:, g % 2, c, :].unsqueeze(1).broadcast_to([P, SSD_R, P]),
                                    ALU.mult).then_inc(decay_ready, 1)
                    if n >= 1:
                        y(n - 1)
                y(len(SSD_ROUNDS) - 1)

                zs = qT[:, :, :].rearrange("p a b -> p (a b)").rearrange("p (t d) -> p t d", t=TT)
                sq = xdt
                dve.wait_ge(*taken(("z1", 1), L))
                for t in range(TT):
                    last = V.tensor_tensor(xtok[:, t, :], xtok[:, t, :], zs[:, t, :], ALU.mult)
                lk(last)
                for t in range(TT):
                    last = V.tensor_tensor(sq[:, t, :], xtok[:, t, :], xtok[:, t, :], ALU.mult)
                lk(last)
                lk(V.tensor_reduce(gss[:, 2], sq[:, :, :].rearrange("p t (g d) -> p t g d", g=SSD_GROUPS), AX.X, ALU.add))
                V.tensor_scalar(gss[:, 0], gss[:, 2], 1.0 / GW, EPS, ALU.mult, ALU.add).then_inc(gy_ms, 1)
                dve.wait_ge(gy_sqrt, L + 1)
                lk(V.reciprocal(gss[:, 2], gss[:, 1]))
                for t in range(TT):
                    v = xtok[:, t, :].rearrange("p (g d) -> p g d", g=SSD_GROUPS)
                    V.tensor_tensor(v, v, gss[:, 2, t, :].unsqueeze(2).broadcast_to([P, SSD_GROUPS, GW]),
                                    ALU.mult).then_inc(ssd_ready, 1)
                dve.wait_ge(*taken(("g_att1", 1), L))
                gated("b_att0", 0, 1)
                gated("b_att1", 1, 1)
                dve.wait_ge(*taken(("b_att1", 1), L))
                V.tensor_tensor(G[:, 0].rearrange("p a b -> p (a b)"), G[:, 0].rearrange("p a b -> p (a b)"),
                                G[:, 1].rearrange("p a b -> p (a b)"), ALU.add).then_inc(merge_step, 1)
                dve.wait_ge(merge_step, L * 2 + 2)
                dve.wait_ge(*taken(("g_ssd1", 1), L))
                for t in range(TT):
                    for n in range(2):
                        name = (f"b_ssd{n}", t)
                        gate = G[:, 1, t, n * HALF:(n + 1) * HALF]
                        dve.wait_ge(*full(name, L))
                        frees(V.tensor_tensor(gate, gate, ps(name)[:, :], ALU.mult), name)
                    dve.wait_ge(*taken(name, L))
                    V.tensor_tensor(G[:, 0, t, :], G[:, 0, t, :], G[:, 1, t, :], ALU.add).then_inc(merged_ready, 1)

                def moments(t):
                    for j in range(2):
                        last = V.bn_stats(stats[:, t, j, :], h[:, t, j * HALF:(j + 1) * HALF])
                    lk(last)
                    dve.sem_inc(passed_wait, 1)
                    lk(V.bn_aggr(mv[:, t, :], stats[:, t, :, :].rearrange("p a b -> p (a b)")))
                    V.tensor_scalar(mv[:, t, 1:2], mv[:, t, 1:2], EPS, None, ALU.add).then_inc(var_ready, 1)

                def normalised(i, t):
                    if t == 0:
                        dve.wait_ge(lnp_full, L * 96 + 32 * (i + 1))
                    dve.wait_ge(sqrt_done, L * 6 + (2 * i + t + 1))
                    V.reciprocal(rstd[:, 1, t:t + 1], rstd[:, 0, t:t + 1])
                    lk(V.scalar_tensor_tensor(out=h[:, t, :], in0=h[:, t, :], scalar=mv[:, t, 0:1],
                                              in1=lnp[:, 0, :], op0=ALU.subtract, op1=ALU.mult))
                    V.scalar_tensor_tensor(out=h[:, t, :], in0=h[:, t, :], scalar=rstd[:, 1, t:t + 1],
                                           in1=lnp[:, 1, :], op0=ALU.mult, op1=ALU.add).then_inc(h_ready, 1)
                    if t == 1:
                        dve.wait_ge(h_ready, L * 6 + (2 * i + 4))
                        dve.sem_inc(lnp_free, 1)

                def residual(names, t):
                    for j, name in enumerate(names):
                        dve.wait_ge(*full(name, L))
                        d = h[:, t, j * HALF:(j + 1) * HALF]
                        frees(V.scalar_tensor_tensor(out=d, in0=d, scalar=ALPHA, in1=ps(name)[:, :],
                                                     op0=ALU.mult, op1=ALU.add), name)
                    dve.wait_ge(*taken(name, L))

                for t in range(TT):
                    residual([("out0", t), ("out1", t)], t)
                    moments(t)
                    normalised(0, t)

                R = [rt[:, i] for i in range(24)]
                dve.wait_ge(*full("router", L))
                lg = ps("router")[:, 0:40].rearrange("p (t n) -> p t n", t=TT)
                V.tensor_tensor(R[0][:, :, 0:4], lg[:, :, 0:4], rows[:, 64:68].unsqueeze(1).broadcast_to([P, TT, 4]), ALU.add)
                frees(V.tensor_tensor(R[1], lg[:, :, 4:20], rows[:, 68:84].unsqueeze(1).broadcast_to([P, TT, 16]),
                                      ALU.add), "router")
                dve.wait_ge(*taken("router", L))
                dve.sem_inc(params_free, 1)

                def bc(ap, n):
                    return ap.broadcast_to([P, TT, n])

                def first_max(src, m, tmp, hot):
                    lk(V.tensor_tensor(tmp[:, :, 0:4], src, bc(m, 4), ALU.is_equal))
                    lk(V.tensor_tensor(tmp[:, :, 0:4], tmp[:, :, 0:4],
                                       weight4.unsqueeze(1).broadcast_to([P, TT, 4]), ALU.mult))
                    lk(V.tensor_reduce(tmp[:, :, 4:5], tmp[:, :, 0:4], AX.X, ALU.max))
                    lk(V.tensor_tensor(hot, tmp[:, :, 0:4], bc(tmp[:, :, 4:5], 4), ALU.is_equal))

                gmax = R[4][:, :, 0:1]
                lk(V.tensor_reduce(gmax, R[0][:, :, 0:4], AX.X, ALU.max))
                V.tensor_tensor(R[2][:, :, 0:4], R[0][:, :, 0:4], bc(gmax, 4), ALU.subtract).then_inc(rexp_in, 1)
                first_max(R[0][:, :, 0:4], gmax, R[5], R[6][:, :, 0:4])
                dve.sem_inc(group_ready, 1)
                gl = R[7].rearrange("p t (g e) -> p t g e", g=MOE_G)
                lk(V.tensor_tensor(gl, R[1].rearrange("p t (g e) -> p t g e", g=MOE_G),
                                   R[6][:, :, 0:4].unsqueeze(3).broadcast_to([P, TT, MOE_G, MOE_E]), ALU.mult))
                es = R[8][:, :, 0:4]
                lk(V.tensor_reduce(es, R[7].rearrange("p t (g e) -> p t e g", g=MOE_G), AX.X, ALU.add))
                m1, m2 = R[9][:, :, 0:1], R[10][:, :, 0:1]
                lk(V.tensor_reduce(m1, es, AX.X, ALU.max))
                first_max(es, m1, R[5], R[13][:, :, 0:4])
                lk(V.scalar_tensor_tensor(out=R[14][:, :, 0:4], in0=R[13][:, :, 0:4], scalar=NEG, in1=es,
                                          op0=ALU.mult, op1=ALU.add))
                lk(V.tensor_reduce(m2, R[14][:, :, 0:4], AX.X, ALU.max))
                V.tensor_tensor(R[11][:, :, 0:1], m2, m1, ALU.subtract).then_inc(rexp_in, 1)
                first_max(R[14][:, :, 0:4], m2, R[5], R[15][:, :, 0:4])
                dve.wait_ge(rexp_out, L * 2 + 2)
                lk(V.tensor_reduce(R[16][:, :, 0:1], R[3][:, :, 0:4], AX.X, ALU.add))
                lk(V.reciprocal(R[16][:, :, 1:2], R[16][:, :, 0:1]))
                lk(V.tensor_scalar(R[17][:, :, 0:1], R[12][:, :, 0:1], 1.0, None, ALU.add))
                lk(V.reciprocal(R[17][:, :, 1:2], R[17][:, :, 0:1]))
                lk(V.tensor_tensor(R[17][:, :, 2:3], R[17][:, :, 1:2], R[16][:, :, 1:2], ALU.mult))
                lk(V.tensor_tensor(R[17][:, :, 3:4], R[17][:, :, 2:3], R[12][:, :, 0:1], ALU.mult))
                V.tensor_tensor(R[18][:, :, 0:4], R[13][:, :, 0:4], bc(R[17][:, :, 2:3], 4), ALU.mult)
                lk(V.tensor_tensor(R[19][:, :, 0:4], R[15][:, :, 0:4], bc(R[17][:, :, 3:4], 4), ALU.mult))
                lk(V.tensor_tensor(R[18][:, :, 0:4], R[18][:, :, 0:4], R[19][:, :, 0:4], ALU.add))
                for t in range(TT):
                    last = V.tensor_tensor(rt[:, COMBINE, t, :].rearrange("p (g e) -> p g e", g=MOE_G),
                                           R[6][:, t, 0:4].unsqueeze(2).broadcast_to([P, MOE_G, MOE_E]),
                                           R[18][:, t, 0:4].unsqueeze(1).broadcast_to([P, MOE_G, MOE_E]), ALU.mult)
                last.then_inc(combine_ready, 1)

                dve.wait_ge(*full("rank", L))
                cnt = ps("rank")[:, 0:12].rearrange("p (t g) -> p t g", g=MOE_G)
                lk(V.tensor_tensor(R[21][:, :, 0:4], R[6][:, :, 0:4], cnt[:, 0:2, :], ALU.mult))
                lk(V.tensor_scalar(R[21][:, :, 0:4], R[21][:, :, 0:4], -1.0, None, ALU.add))
                frees(V.tensor_reduce(R[22][:, 0, 0:1], cnt[:, 2, :], AX.X, ALU.max), "rank")
                dve.wait_ge(*taken("rank", L))
                V.tensor_scalar(overflow[:], R[22][:, 0, 0:1], float(CAP), None, ALU.is_gt).then_inc(flag_ready, 1)
                for t in range(TT):
                    last = V.tensor_tensor(sel[:, t, :].rearrange("p (g s) -> p g s", g=MOE_G),
                                           const("iota").unsqueeze(1).broadcast_to([P, MOE_G, CAP]),
                                           R[21][:, t, 0:4].unsqueeze(2).broadcast_to([P, MOE_G, CAP]), ALU.is_equal)
                last.then_inc(sel_ready, 1)

                dve.wait_ge(flag_ready, L + 1)
                dve.sem_inc(passed_wait, 1)
                with dve.If(dve.value_load(overflow[0:1, 0:1], min_val=0, max_val=1) == 0):
                    for e in range(NE):
                        u = act_t[:, e % 2, 0:2 * CAP]
                        dve.wait_ge(silu_s, L * NE + (e + 1))
                        frees(V.tensor_tensor(u, act_s[:, e % 2, 0:2 * CAP], ps(("hgu", e))[:, 2 * CAP:4 * CAP],
                                              ALU.mult), ("hgu", e))
                        dve.wait_ge(*taken(("hgu", e), L))
                        dve.wait_ge(*taken(("weight", e // MOE_E), L))
                        u2 = u.rearrange("p (f s) -> p f s", f=2)
                        V.tensor_tensor(u2, u2, wS[:, e, :].unsqueeze(1).broadcast_to([P, 2, CAP]),
                                        ALU.mult).then_inc(act_ready, 1)
                with dve.Else():
                    for e in range(NE):
                        u = act_t[:, e % 2, :]
                        dve.wait_ge(*taken(("hg", e), L))
                        dve.wait_ge(*full(("hu", e), L))
                        frees(V.tensor_tensor(u, act_s[:, e % 2, :], ps(("hu", e))[:, :], ALU.mult), ("hu", e))
                        dve.wait_ge(*taken(("hu", e), L))
                        dve.wait_ge(*taken(("comb", e // 2), L))
                        u2 = u.rearrange("p (f s) -> p f s", f=2)
                        V.tensor_tensor(u2, u2, comb[:, e, :].unsqueeze(1).broadcast_to([P, 2, SEQ]),
                                        ALU.mult).then_inc(act_ready, 1)
                residual([("acc", 0, 0), ("acc", 0, 1)], 0)
                moments(0)
                residual([("acc", 1, 0), ("acc", 1, 1)], 1)
                normalised(1, 0)
                moments(1)
                normalised(1, 1)

                for t in range(TT):
                    for j in range(2):
                        dve.wait_ge(*taken((f"pg{j}", t), L))
                        g = G[:, 0, t, j * HALF:(j + 1) * HALF]
                        lk(V.tensor_tensor(g, g, xtok[:, t, j * HALF:(j + 1) * HALF], ALU.mult))
                        d = h[:, t, j * HALF:(j + 1) * HALF]
                        lk(V.scalar_tensor_tensor(out=d, in0=d, scalar=ALPHA, in1=g, op0=ALU.mult, op1=ALU.add))
                    moments(t)
                    normalised(2, t)
                assert steps[0] == DVE_STEPS, f"DVE_STEPS = {steps[0]}"


_INS = ["x", "p", "positions", "w_in", "ssd_conv_w", "ssd_conv_b", "ssd_dt_bias", "ssd_a_log", "ssd_d",
        "ssd_norm_w", "attn_sinks", "pool_w", "pool_scale", "w_branch", "w_out", "ln1_g", "ln1_b",
        "router_group_w", "router_group_b", "router_expert_w", "router_expert_b", "exp_w_gate",
        "exp_w_up", "exp_w_down", "ln2_g", "ln2_b", "ple_w_proj", "ple_w_gate", "ln3_g", "ln3_b"]


def kernel(**inputs):
    import concourse.bacc as bacc
    from concourse.bass_utils import run_bass_kernel_spmd

    nc = bacc.Bacc("TRN2", target_bir_lowering=False, num_devices=1)
    arrays, args = {}, []
    for name in _INS + ["consts"]:
        a = shape_constants() if name == "consts" else np.ascontiguousarray(inputs[name])
        arrays[f"in_{name}"] = a
        args.append(nc.dram_tensor(f"in_{name}", a.shape, mybir.dt.from_np(a.dtype), kind="ExternalInput").ap())
    args.append(nc.dram_tensor("out_h", (1, SEQ, D), F32, kind="ExternalOutput").ap())
    program(nc, *args)
    return run_bass_kernel_spmd(nc, [arrays], core_ids=[0]).results[0]["out_h"]
```

```python
from contextlib import ExitStack

import numpy as np

import concourse.bass as bass
from concourse import mybir

F32 = mybir.dt.float32
F32R = mybir.dt.float32r
I32 = mybir.dt.int32
ALU = mybir.AluOpType
ACT = mybir.ActivationFunctionType
AX = mybir.AxisListType

P = 128
DEPTH, SEQ, D = 2, 256, 1024
TT = SEQ // P
KT = D // P
HALF = 512
PLE = 256
SSD_HEADS, SSD_P, SSD_GROUPS, SSD_N, SSD_CONV = 16, 64, 4, 128, 4
SSD_R = SSD_HEADS // SSD_GROUPS
GW = SSD_R * SSD_P
XBC = D + 2 * SSD_GROUPS * SSD_N
XBC_T = XBC // P
Q_HEADS, KV_HEADS, HD = 16, 4, 64
ROT = HD // 2
CHUNK = 64
POOL_WINDOWS = (2, 4, 8, 16)
MOE_G, MOE_E = 4, 4
NE = MOE_G * MOE_E
HID = 256
ALPHA = (2.0 * DEPTH) ** 0.25
EPS = 1e-5
NEG = -1e30
CAP = 96

COL_Z, COL_XBC = 0, D
COL_DT = COL_XBC + XBC
COL_Q = COL_DT + SSD_HEADS
COL_KV = COL_Q + Q_HEADS * HD
COL_PU = COL_KV + 2 * KV_HEADS * HD
COL_GATE = COL_PU + D

UNITS = (
    [("q", 0), ("q", 1), ("kv", 0), ("pu", 0), ("pu", 1)]
    + [("xbc", 0), ("xbc", 1), ("xbc", 2), ("pool_w", 0), ("xbc", 3), ("dt", 0)]
    + [("gate", 4), ("gate", 5), ("branch", 4), ("branch", 5), ("z", 0), ("z", 1)]
    + [("gate", 2), ("gate", 3), ("branch", 2), ("branch", 3)]
    + [("gate", 0), ("gate", 1), ("branch", 0), ("branch", 1), ("out", 0), ("out", 1)]
    + [("ple_proj", 0)]
    + [x for e in range(0, NE, 2) for x in (("gu", e), ("gu", e + 1), ("down", e))]
    + [("ple_gate", 0), ("ple_gate", 1)]
)
RING = 3
UNIT_W = 8 * HALF
NU = len(UNITS)
assert NU % RING == 0
UNIT_AT = {u: i for i, u in enumerate(UNITS)}

SPLIT_KINDS = ("q", "kv", "pu", "xbc", "gate", "branch", "z", "out", "gu", "down", "ple_gate")
PIECES = 4
PIECE_W = UNIT_W // PIECES
HI_RING = 4
SPLIT_UNITS = [u for u in UNITS if u[0] in SPLIT_KINDS]
NPIECE = PIECES * len(SPLIT_UNITS)
assert NPIECE % HI_RING == 0
MOE_UNITS = [u for u in SPLIT_UNITS if u[0] in ("gu", "down")]
PIECE_AT = {u: PIECES * i for i, u in enumerate(SPLIT_UNITS)}


def remainder_on_pool(unit):
    if unit in (("q", 0), ("out", 0), ("ple_gate", 0)):
        return (1, 2, 3)
    return (3,)


REMAINDER, REMAINDERS, MOE_REMAINDERS = [], {"dve": 0, "pool": 0}, {"dve": 0, "pool": 0}
for _unit in SPLIT_UNITS:
    for _i in range(PIECES):
        _engine = "pool" if _i in remainder_on_pool(_unit) else "dve"
        REMAINDER.append((_engine, REMAINDERS[_engine]))
        REMAINDERS[_engine] += 1
        MOE_REMAINDERS[_engine] += _unit in MOE_UNITS

ROUNDS = [(0, 0), (1, 0), (0, 1), (1, 1)]
SSD_ROUNDS = [(g, c) for g in range(SSD_GROUPS) for c in range(TT)]

SSD_FILL = {1: ("z1", ("z", 1), 1), 3: ("g_att0", ("gate", 2), 0), 5: ("g_att1", ("gate", 3), 1),
            7: ("b_att0", ("branch", 2), 0)}


def job_table():
    jobs = []

    def job(name, bank):
        jobs.append((name, bank))

    def pair(name, n):
        for t in range(TT):
            job((name, t), 2 * (n % 2) + t)

    def transposes(name):
        for t in range(TT):
            for j in range(2):
                job((name, t, j), 4 + 2 * t + j)

    transposes("hT1")
    pair("q0", 0)
    pair("q1", 1)
    pair("kv", 0)
    pair("pu0", 1)
    pair("pu1", 0)
    job("vec", 4)
    for t in range(TT):
        job(("qT", t, 0), 5)
        job(("qT", t, 1), 6)
        job(("kT", t), 7)
    pair("xbc0", 1)
    job(("scores", 0, 0), 4)
    job(("scores", 0, 1), 5)
    pair("xbc1", 0)
    for j in range(4):
        job(("pooled", j), 4 + j)
    pair("xbc2", 1)
    for j in range(4):
        job(("mixed", j), 4 + j)
    for b in range(4):
        job(("scores", 1, b), 4 + b)
    pair("xbc3", 0)
    job("dt", 2)
    pair("g_pool0", 0)
    for r, fill in enumerate(("g_pool1", "b_pool0", "b_pool1", "z0")):
        pair(fill, (r + 1) % 2)
        nb = 2 if r % 2 == 0 else 4
        for b in range(nb):
            job(("PT", r, b), 4 + b)
        for g in range(2):
            job(("PV", r, g), 4 + 2 * (r % 2 == 0) + g)
        if r + 2 < 4:
            for b in range(nb):
                job(("scores", r + 2, b), 4 + b)
    job("dsum", 4)
    for j in range(4):
        job(("xT", j), 4 + j)
    for n, (g, c) in enumerate(SSD_ROUNDS):
        if n in SSD_FILL:
            pair(SSD_FILL[n][0], SSD_FILL[n][2])
        if c == 0:
            job(("cb", g), 4)
        job(("seg", n), 5)
        if n >= 1:
            job(("y", n - 1), 6 + (n - 1) % 2)
    job(("y", len(SSD_ROUNDS) - 1), 7)
    pair("b_att1", 1)
    pair("g_ssd0", 0)
    pair("g_ssd1", 1)
    transposes("yT")
    pair("b_ssd0", 0)
    pair("b_ssd1", 1)
    transposes("mT")
    pair("out0", 0)
    pair("out1", 1)
    transposes("hT2")
    job("router", 4)
    job("pT", 0)
    for t in range(TT):
        for j in range(2):
            job(("proj", t, j), [1, 2, 3, 0][2 * t + j])
    job("rank", 5)
    jobs.append(("sparse", None))
    for d in range(KT):
        job(("sorted", d), 4 + d % 4)
    for e in range(NE):
        job(("hgu", e), e % 2)
        if e == 1:
            for g in range(MOE_G):
                job(("weight", g), 2 + g % 2)
            for g in range(MOE_G):
                job(("back", g), 2 + g % 2)
        if e % 2 == 1:
            job(("uT", e - 1), 4)
            job(("uT", e), 5)
        if e % MOE_E == MOE_E - 1:
            for j in range(2):
                job(("yg", e // MOE_E, j), 2 + j)
    jobs.append(("dense", None))
    for e in range(NE):
        job(("hg", e), 2 * (e % 2))
        job(("hu", e), 2 * (e % 2) + 1)
        if e == 1:
            for b in range(NE // 2):
                job(("comb", b), 4 + b % 4)
            for b in range(NE):
                job(("pad", b), 4 + b % 2)
    jobs.append(("both", None))
    for t in range(TT):
        for j in range(2):
            job(("acc", t, j), 4 + 2 * t + j)
    transposes("hT3")
    pair("pg0", 1)
    pair("pg1", 0)
    return jobs


JOBS = job_table()
NBANK = 8
JOB_AT, BANK_JOBS = {}, [0] * NBANK
for _name, _bank in JOBS:
    if _bank is None:
        if _name == "sparse":
            _before = list(BANK_JOBS)
        elif _name == "dense":
            _after, BANK_JOBS = BANK_JOBS, _before
        else:
            assert BANK_JOBS == _after
        continue
    assert _name not in JOB_AT, _name
    JOB_AT[_name] = (_bank, BANK_JOBS[_bank])
    BANK_JOBS[_bank] += 1

BAND0 = P + POOL_WINDOWS[-1]
CONST_COLS = {}
_at = 0
for _n, _w in (("ident", P), ("inv", ROT), ("upto", P), ("after", P), ("mask0", P), ("mask1", 192),
               ("band0", 4 * BAND0), ("band1", 4 * P), ("weight4", 4), ("iota", CAP)):
    CONST_COLS[_n] = (_at, _w)
    _at += _w
NCONST = _at
NFIRST = P + ROT


def shape_constants():
    a, b = np.arange(P)[:, None], np.arange(P)[None, :]
    c = {}
    c["ident"] = a == b
    c["upto"] = a <= b
    c["after"] = a > b
    own = a // CHUNK
    c["mask0"] = np.where((own == 0) & (b // CHUNK == 1), NEG, 0.0)
    k = np.arange(192)[None, :] // CHUNK
    c["mask1"] = np.where(k - own * 1 == 2, NEG, 0.0) + np.where((own == 1) & (k == 0), NEG, 0.0)
    t, s = np.arange(P)[:, None], np.arange(BAND0)[None, :]
    band0, band1 = [], []
    for w in POOL_WINDOWS:
        inside = (t <= s) & (t > s - w)
        band0.append(inside / np.minimum(s + 1, w) - (t == s))
        band1.append(((t <= b) & (t > b - w)) / w - (t == b))
    c["band0"] = np.concatenate(band0, 1)
    c["band1"] = np.concatenate(band1, 1)
    inv = np.float32(10000.0) ** (-np.arange(0, HD, 2, dtype=np.float32) / np.float32(HD))
    c["inv"] = np.broadcast_to(inv[None, :], (P, ROT))
    c["weight4"] = np.broadcast_to(np.array([[4, 3, 2, 1]]), (P, 4))
    c["iota"] = np.broadcast_to(np.arange(CAP)[None, :], (P, CAP))
    out = np.zeros((P, NCONST), np.float32)
    for n, (o, w) in CONST_COLS.items():
        out[:, o:o + w] = c[n]
    return out


VEC_ROWS = SSD_CONV * XBC_T + XBC_T + KT + KT
V_CB = SSD_CONV * XBC_T
V_PS = V_CB + XBC_T
V_NW = V_PS + KT
RROW = 84

PARAM_INC = 10 * 16
ROUND = float(3 * 2 ** 22)
TWO_PI = (6.28125, 0.0019350051879882812, 3.019915981956753e-07)
PI_F = 3.1415925
COMBINE = 20
DVE_STEPS = 125
ROUNDED = 20 + KT + NE + 2 * MOE_G


def program(nc, x, p, positions, w_in, conv_w, conv_b, dt_bias, a_log, ssd_d, norm_w, sinks, pool_w,
            pool_scale, w_branch, w_out, ln1_g, ln1_b, rg_w, rg_b, re_w, re_b, w_gate, w_up, w_down,
            ln2_g, ln2_b, ple_proj, ple_gate, ln3_g, ln3_b, consts, out):
    with ExitStack() as ctx:
        def sb(name, shape, dt=F32):
            return ctx.enter_context(nc.sbuf_tensor(name, [P] + shape, dt))

        def sb_shared(*tensors):
            handles = []
            for i, (name, shape) in enumerate(tensors):
                last = i == len(tensors) - 1
                with nc.sbuf_tensor(name, [P] + shape, F32) if not last else ExitStack() as handle:
                    handles.append(sb(name, shape) if last else handle)
            return handles

        def sem(name):
            return ctx.enter_context(nc.semaphore(name))

        NS = MOE_G * CAP
        weight_lo, ring = sb_shared(("weight_lo", [RING, UNIT_W]), ("ring", [RING, UNIT_W]))
        cst = sb("cst", [NCONST])
        h = sb("h", [TT, D])
        hT, hT_plain = sb_shared(("hT", [KT, SEQ]), ("hT_plain", [KT, SEQ]))
        yg, G = sb_shared(("yg", [MOE_G, D]), ("G", [2, TT, D]))
        att_lo, xin = sb_shared(("att_lo", [KT, SEQ]), ("xin", [2, 4, 3 + SEQ]))
        poolT = sb("poolT", [KT, SEQ])
        hS_lo, y_split, xconv = sb_shared(("hS_lo", [KT, NS]), ("y_split", [2 * KT, SEQ]), ("xconv", [XBC_T, SEQ]))
        poolT_lo, xtok = sb_shared(("poolT_lo", [KT, SEQ]), ("xtok", [TT, D]))
        selT_all, xdt = sb_shared(("selT", [TT * D]), ("xdt", [TT, D]))
        hS, qkT = sb_shared(("hS", [KT, NS]), ("qkT", [KT + KV_HEADS, SEQ]))
        qT = qkT[:, 0:KT, :]
        kT = qkT[:, KT:KT + KV_HEADS, :]
        vv = sb("vv", [TT, KV_HEADS * HD])
        weight_hi = sb("weight_hi", [HI_RING, PIECE_W])
        hT_lo = sb("hT_lo", [KT, SEQ])
        dt_hi = sb("dt_hi", [KT, SSD_HEADS])
        P0 = sb("P0", [8, P])
        tA = P0[:, 0:4, :].rearrange("p a b -> p (a b)")
        tB = P0[:, 4:8, :].rearrange("p a b -> p (a b)")
        uT_split, p1_segs = sb_shared(("uT_split", [2048]), ("p1_segs", [2048]))
        P1 = p1_segs[:, :].rearrange("p (h k) -> p h k", h=8)
        E = p1_segs[:, 0:1024].rearrange("p (a r l) -> p a r l", a=2, r=SSD_R)
        segs = p1_segs[:, 1024:2048].rearrange("p (a r l) -> p a r l", a=2, r=SSD_R)
        prow = p1_segs[:, 0:TT * PLE].rearrange("p (t n) -> p t n", t=TT)
        act_s = p1_segs[:, 1024:2048].rearrange("p (a n) -> p a n", a=2)
        act_t = p1_segs[:, 0:1024].rearrange("p (a n) -> p a n", a=2)
        pts_cb = sb("pts_cb", [2048])
        PTs = pts_cb[:, :].rearrange("p (a b i q) -> p a b i q", a=2, b=2, i=4)
        cbm = pts_cb[:, 0:768].rearrange("p (a b l) -> p a b l", a=2, b=3)
        yoff = pts_cb[:, 1024:1024 + GW]
        lnp = sb("lnp", [2, D])
        attT = xin[:, :, :, :].rearrange("p a b c -> p (a b c)")[:, 0:D * TT].rearrange(
            "p (f s) -> p f s", f=KT)
        xde = P0[:, :, :].rearrange("p a b -> p (a b)")
        pT = pts_cb[:, 0:2 * SEQ].rearrange("p (k s) -> p k s", k=2)
        yT, yT_lo = y_split[:, 0:KT, :], y_split[:, KT:2 * KT, :]
        att_hi = poolT
        sel = xdt[:, :, :].rearrange("p a b -> p (a b)")[:, 0:TT * NS].rearrange("p (t s) -> p t s", t=TT)
        selT = selT_all[:, TT * NS:TT * NS + MOE_G * SEQ].rearrange(
            "p (g s) -> p g s", g=MOE_G)
        yg_lo = [x[:, :, :].rearrange("p a b -> p (a b)").rearrange("p (i d) -> p i d", i=2) for x in (poolT, hT_lo)]
        gate_s = p1_segs[:, 0:2 * HID].rearrange("p (i n) -> p i n", i=2)
        u_s = p1_segs[:, 2 * HID:4 * HID].rearrange("p (i n) -> p i n", i=2)
        uT_hi, uT_lo = (uT_split[:, 1024 + 384 * i:1024 + 384 * (i + 1)].rearrange("p (i k s) -> p i k s", i=2, k=2)
                        for i in range(2))
        comb = xconv
        vecrows = pts_cb[:, 1536:1536 + P]
        vecT = sb("vecT", [VEC_ROWS])
        rows = sb("rows", [RROW])
        rw = p1_segs[:, 512:512 + KT * 20].rearrange("p (k n) -> p k n", k=KT)
        posi = sb("posi", [TT], I32)
        posf = sb("posf", [TT])
        cosT = sb("cosT", [TT, ROT])
        sinT = sb("sinT", [TT, ROT])
        nsinT = sb("nsinT", [TT, ROT])
        dtv = sb("dtv", [TT, SSD_HEADS])
        dA = sb("dA", [TT, SSD_HEADS])
        nega = sb("nega", [SSD_HEADS])
        dexp = sb("dexp", [2, SSD_HEADS])
        amax = sb("amax", [8, 8])
        gss = sb("gss", [3, TT, SSD_GROUPS])
        stats = sb("stats", [TT, 2, 6])
        mv = sb("mv", [TT, 2])
        overflow = sb("overflow", [1], I32)
        rstd = sb("rstd", [2, TT])
        rt = sb("rt", [24, TT, 16])
        weight_s = rt[:, 23, 0, :]
        sm = rt[:, 0:12].rearrange("p a t n -> p a (t n)")
        ang = rt[:, 0:8].rearrange("p a t n -> p (a t n)").rearrange("p (i t d) -> p i t d", i=4, t=TT)
        bank = [ctx.enter_context(nc.psum_tensor(f"bank{i}", [P, HALF], F32)) for i in range(NBANK)]

        def const(name):
            o, w = CONST_COLS[name]
            return cst[:, o:o + w]

        ident, upto, after = const("ident"), const("upto"), const("after")
        band0 = const("band0").rearrange("p (w s) -> p w s", w=4)
        weight4 = const("weight4")
        ones = weight4[:, 3:4].to_broadcast([P, P])
        band1 = const("band1").rearrange("p (w s) -> p w s", w=4)

        unit_full = [sem(f"unit_full{s}") for s in range(RING)]
        unit_free = sem("unit_free")
        piece_free = sem("piece_free")
        piece_rounded = sem("piece_rounded")
        remainder_ready = {"dve": sem("remainder_ready_dve"), "pool": sem("remainder_ready_pool")}
        dt_rounded = sem("dt_rounded")
        dt_split = sem("dt_split")
        rounded = sem("rounded")
        att_rounded = sem("att_rounded")
        att_split = sem("att_split")
        late_params_full = sem("late_params_full")
        bank_full = [sem(f"bank_full{b}") for b in range(NBANK)]
        bank_free = [sem(f"bank_free{b}") for b in range(NBANK)]
        start_loads = [sem("ident_x0_loaded"), sem("x1_loaded")]
        const_loaded = sem("const_loaded")
        dve_step = sem("dve_step")
        pos_loaded = sem("pos_loaded")
        sines_done = sem("sines_done")
        angles_ready = sem("angles_ready")
        params_full = sem("params_full")
        params_free = sem("params_free")
        lnp_full = sem("lnp_full")
        lnp_free = sem("lnp_free")
        h_ready = sem("h_ready")
        qrot_ready = sem("qrot_ready")
        conv_done = sem("conv_done")
        silu_done = sem("silu_done")
        probs_ready = sem("probs_ready")
        scores_ready = sem("scores_ready")
        exp_done = sem("exp_done")
        dt_pre = sem("dt_pre")
        dt_exp = sem("dt_exp")
        dA_ready = sem("dA_ready")
        dsum_exp = sem("dsum_exp")
        xdt_ready = sem("xdt_ready")
        seg_built = sem("seg_built")
        seg_exp = sem("seg_exp")
        decay_ready = sem("decay_ready")
        merge_step = sem("merge_step")
        gy_ms = sem("gy_ms")
        gy_sqrt = sem("gy_sqrt")
        ssd_ready = sem("ssd_ready")
        merged_ready = sem("merged_ready")
        var_ready = sem("var_ready")
        sqrt_done = sem("sqrt_done")
        rexp_in = sem("rexp_in")
        rexp_out = sem("rexp_out")
        combine_ready = sem("combine_ready")
        act_ready = sem("act_ready")
        group_ready = sem("group_ready")
        flag_ready = sem("flag_ready")
        sel_ready = sem("sel_ready")
        silu_s = sem("silu_s")
        stored = sem("stored")
        passed_wait = sem("passed_wait")

        def full(name, L):
            b, k = JOB_AT[name]
            return bank_full[b], L * BANK_JOBS[b] + (k + 1)

        def free(name, L):
            b, k = JOB_AT[name]
            return bank_free[b], L * BANK_JOBS[b] + (k + 1)

        def taken(name, L):
            b, k = JOB_AT[name]
            return bank_free[b], L * BANK_JOBS[b] + (k + 2)

        def ps(name):
            return bank[JOB_AT[name][0]]

        def reduced(ap):
            return ap.bitcast(F32R)

        def piece(unit, i):
            whole, lo = (x[:, UNIT_AT[unit] % RING, :].rearrange("p (k n) -> p k n", k=KT) for x in (ring, weight_lo))
            hi = weight_hi[:, (PIECE_AT[unit] + i) % HI_RING, :]
            if unit[0] == "xbc":
                cols = slice(i * P, (i + 1) * P)
                return whole[:, :, cols], lo[:, :, cols], hi.rearrange("p (k n) -> p k n", k=KT)
            ks = slice(2 * i, 2 * i + 2)
            return whole[:, ks, :], lo[:, ks, :], hi.rearrange("p (k n) -> p k n", k=2)

        dt_lo = weight_lo[:, UNIT_AT[("dt", 0)] % RING, :].rearrange("p (k n) -> p k n", k=KT)[:, :, 0:SSD_HEADS]

        def split(unit, i, L):
            engine, k = REMAINDER[PIECE_AT[unit] + i]
            return remainder_ready[engine], L * REMAINDERS[engine] + (k + 1)

        def slot(unit):
            return ring[:, UNIT_AT[unit] % RING, :]

        block = ctx.enter_context(nc.Block())

        @block.sync
        def _(sp):
            sp.dma_start(cst[:, 0:NFIRST], consts[:, 0:NFIRST]).then_inc(start_loads[0], 16)
            sp.dma_start(h[:, 0, :], x[0, 0:P, :]).then_inc(start_loads[0], 16)
            with sp.Fori(0, DEPTH) as L:
                for u, (kind, n) in enumerate(UNITS):
                    dst = ring[:, u % RING, :]
                    k8 = dst.rearrange("p (k n) -> p k n", k=KT)
                    sp.wait_ge(unit_free, L * NU + (u + 1))
                    sp.sem_inc(passed_wait, 1)
                    pairs = []
                    if kind in ("q", "kv", "pu", "xbc", "gate", "z", "dt"):
                        col = {"q": COL_Q, "kv": COL_KV, "pu": COL_PU, "xbc": COL_XBC,
                               "gate": COL_GATE, "z": COL_Z, "dt": COL_DT}[kind] + n * HALF
                        w = SSD_HEADS if kind == "dt" else HALF
                        src = w_in[L].rearrange("(k p) n -> p k n", p=P)[:, :, col:col + w]
                        pairs = [(k8[:, 0:4, 0:w], src[:, 0:4]), (k8[:, 4:8, 0:w], src[:, 4:8])]
                    elif kind in ("branch", "out", "ple_gate"):
                        m = {"branch": w_branch, "out": w_out, "ple_gate": ple_gate}[kind]
                        m = m[L, n // 2] if kind == "branch" else m[L]
                        c = (n % 2) * HALF
                        src = m.rearrange("(k p) n -> p k n", p=P)[:, :, c:c + HALF]
                        pairs = [(k8[:, 0:4, :], src[:, 0:4]), (k8[:, 4:8, :], src[:, 4:8])]
                    elif kind == "gu":
                        for i, m in enumerate((w_gate, w_up)):
                            pairs.append((k8[:, :, i * HID:(i + 1) * HID],
                                          m[L, n // 4, n % 4].rearrange("(k p) n -> p k n", p=P)))
                    elif kind == "down":
                        for i in range(2):
                            e = n + i
                            pairs.append((dst[:, i * 2048:(i + 1) * 2048].rearrange("p (k n) -> p k n", k=2),
                                          w_down[L, e // 4, e % 4].rearrange("(k p) n -> p k n", p=P)))
                    elif kind == "pool_w":
                        for i in range(2):
                            pairs.append((dst[:, i * 1024:(i + 1) * 1024].rearrange("p (g k n) -> p g k n", g=2, k=2),
                                          pool_w[L, 2 * i:2 * i + 2].rearrange("g (k p) n -> p g k n", p=P)))
                    elif kind == "ple_proj":
                        for i in range(2):
                            pairs.append((dst[:, i * D:(i + 1) * D], ple_proj[L, i * P:(i + 1) * P, :]))
                    for d, s in pairs:
                        sp.dma_start(d, s).then_inc(unit_full[u % RING], 16)
            for t in range(TT):
                sp.wait_ge(h_ready, 12 * DEPTH + 2 * t + 2)
                sp.dma_start(out[0, t * P:(t + 1) * P, :], h[:, t, :]).then_inc(stored, 16)
            sp.wait_ge(stored, 32)

        @block.tensor
        def _(pe):
            mm, tr = nc.tensor.matmul, nc.tensor.transpose

            def done(ins, name):
                ins.then_inc(bank_full[JOB_AT[name][0]], 1)

            pe.sem_inc(unit_free, RING - 1)
            pe.sem_inc(piece_free, HI_RING)
            for b in range(NBANK):
                pe.sem_inc(bank_free[b], 1)
            pe.wait_ge(start_loads[0], 32)
            pe.wait_ge(start_loads[1], 16)
            with pe.Fori(0, DEPTH) as L:

                def arrived(unit):
                    u = UNIT_AT[unit]
                    pe.wait_ge(unit_full[u % RING], L * (NU // RING * 32) + 32 * (u // RING + 1))

                def transposes(name, t, src, ready):
                    for j in range(2):
                        pe.wait_ge(ready[0], ready[1] + j if ready[0] is h_ready else ready[1])
                        pe.wait_ge(*free((name, t, j), L))
                        for i in range(4):
                            f = (4 * j + i) * P
                            last = tr(ps((name, t, j))[:, i * P:(i + 1) * P], src[:, t, f:f + P], ident)
                        done(last, (name, t, j))

                def product(out_, a, b, first, last, piece_done):
                    (ah, al), (bh, bl) = a, b
                    start = mm(out_, reduced(al), reduced(bh), start=first, stop=False)
                    middle = mm(out_, reduced(ah), reduced(bh), start=False, stop=False)
                    if piece_done:
                        middle.then_inc(piece_free, 1)
                    return start, mm(out_, reduced(ah), reduced(bl), start=False, stop=last)

                def token_piece(name, unit, t, i, lhs):
                    _, lo, hi = piece(unit, i)
                    for kk in range(2):
                        k = 2 * i + kk
                        cols = slice(t * P, (t + 1) * P)
                        start, last = product(
                            ps((name, t))[:, :], (lhs[0][:, k, cols], lhs[1][:, k, cols]), (hi[:, kk, :], lo[:, kk, :]),
                            k == 0, k == KT - 1, piece_done=t == TT - 1 and kk == 1)
                        if k == 0 and t == 0:
                            start.then_inc(unit_free, 1)
                        if k == KT - 1:
                            done(last, (name, t))

                def tokens(name, unit, lhs):
                    for t in range(TT):
                        pe.wait_ge(*free((name, t), L))
                    for i in range(PIECES):
                        pe.wait_ge(*split(unit, i, L))
                        for t in range(TT):
                            token_piece(name, unit, t, i, lhs)

                def tokens_in_turn(name, unit, lhs, operand=None, then=None):
                    if operand is not None:
                        operand[1](0)
                    for t in range(TT):
                        if operand is not None:
                            pe.wait_ge(*taken((operand[0], t, 1), L))
                        pe.wait_ge(*free((name, t), L))
                        for i in range(PIECES):
                            if t == 0:
                                pe.wait_ge(*split(unit, i, L))
                            token_piece(name, unit, t, i, lhs)
                            if operand is not None and t == 0 and i == 2:
                                operand[1](1)
                            if then is not None and t == 1 and i == 2:
                                then()

                def features(name, unit):
                    for b in range(2):
                        pe.wait_ge(*free((name, b), L))
                        for i in range(2):
                            pe.wait_ge(*split(unit, 2 * b + i, L))
                            _, lo, hi = piece(unit, 2 * b + i)
                            for k in range(KT):
                                o = ps((name, b))[:, i * SEQ:(i + 1) * SEQ]
                                start = mm(o, reduced(hi[:, k, :]), reduced(hT_lo[:, k, :]), start=k == 0, stop=False)
                                if b + i + k == 0:
                                    start.then_inc(unit_free, 1)
                                middle = mm(o, reduced(hi[:, k, :]), reduced(hT[:, k, :]), start=False, stop=False)
                                if k == KT - 1:
                                    middle.then_inc(piece_free, 1)
                                last = mm(o, reduced(lo[:, k, :]), reduced(hT[:, k, :]), start=False,
                                          stop=k == KT - 1)
                        done(last, (name, b))

                def qk_transposes(t):
                    pe.wait_ge(qrot_ready, L * TT + (t + 1))
                    rot = G[:, t, :, :].rearrange("p a b -> p (a b)")
                    for n, name in enumerate((("qT", t, 0), ("qT", t, 1), ("kT", t))):
                        pe.wait_ge(*free(name, L))
                        for i in range(4):
                            last = tr(ps(name)[:, i * P:(i + 1) * P],
                                      rot[:, (4 * n + i) * P:(4 * n + i + 1) * P], ident)
                        done(last, name)

                def scores(r):
                    t, half = ROUNDS[r]
                    per = 4 if t == 0 else 2
                    pe.wait_ge(*taken(("kT", 1), L))
                    for b in range(8 // per):
                        pe.wait_ge(*free(("scores", r, b), L))
                        for i in range(per):
                            head = 8 * half + (2 * i + b if t == 0 else 4 * (b // 2) + 2 * i + b % 2)
                            q0 = HD * (head % 2)
                            if t == 0:
                                o = ps(("scores", r, b))[:, i * P:(i + 1) * P]
                                keys = slice(0, P)
                            else:
                                o = ps(("scores", r, b))[:, i * 256:i * 256 + 192]
                                keys = slice(CHUNK, SEQ)
                            last = mm(o, qT[q0:q0 + HD, head // 2, t * P:(t + 1) * P],
                                      kT[q0:q0 + HD, head // 4, keys], start=True, stop=True)
                        done(last, ("scores", r, b))

                def probs_transposes(r):
                    t, half = ROUNDS[r]
                    pe.wait_ge(probs_ready, L * 4 + (r + 1))
                    for b in range(2 if t == 0 else 4):
                        name = ("PT", r, b)
                        pe.wait_ge(*free(name, L))
                        for i in range(4):
                            src = P0[:, 4 * b + i, :] if t == 0 else \
                                P1[:, 4 * (b // 2) + i, (b % 2) * P:(b % 2 + 1) * P]
                            last = tr(ps(name)[:, i * P:(i + 1) * P], src, ident)
                        done(last, name)

                def values(r):
                    t, half = ROUNDS[r]
                    for g in range(2):
                        name = ("PV", r, g)
                        kv = 2 * half + g
                        pe.wait_ge(*free(name, L))
                        for kb in range(t + 1):
                            b = g if t == 0 else 2 * g + kb
                            pe.wait_ge(*taken(("PT", r, b), L))
                            last = mm(ps(name)[0:HD, :], vv[:, kb, kv * HD:(kv + 1) * HD],
                                      PTs[:, b // 2, b % 2, :, :].rearrange("p a b -> p (a b)") if t else
                                      PTs[:, 0, b, :, :].rearrange("p a b -> p (a b)"),
                                      start=kb == 0, stop=kb == t)
                        done(last, name)

                def h_transposed(name, t, i):
                    transposes(name, t, h, (h_ready, L * 12 + (4 * i + 2 * t + 1)))

                h2 = (hT, hT_lo)
                tokens_in_turn("q0", ("q", 0), h2, ("hT1", lambda t: h_transposed("hT1", t, 0)))
                tokens("q1", ("q", 1), h2)
                tokens("kv", ("kv", 0), h2)
                tokens("pu0", ("pu", 0), h2)
                tokens("pu1", ("pu", 1), h2)

                pe.wait_ge(params_full, L * PARAM_INC + PARAM_INC)
                pe.wait_ge(*free("vec", L))
                done(tr(ps("vec")[:, 0:VEC_ROWS], vecrows[0:VEC_ROWS, :], ident[0:VEC_ROWS, 0:VEC_ROWS]), "vec")
                for t in range(TT):
                    qk_transposes(t)
                features("xbc0", ("xbc", 0))
                scores(0)
                features("xbc1", ("xbc", 1))

                pe.wait_ge(const_loaded, 16)
                pe.wait_ge(*taken(("pu1", 1), L))
                for j in range(4):
                    pe.wait_ge(*free(("pooled", j), L))
                    for i in range(2):
                        f = 2 * j + i
                        o = ps(("pooled", j))[:, i * SEQ:(i + 1) * SEQ]
                        mm(o[:, 0:P], xtok[:, 0, f * P:(f + 1) * P], band0[:, j, 0:P], start=True, stop=True)
                        mm(o[:, P:SEQ], xtok[:, 1, f * P:(f + 1) * P], band1[:, j, :], start=True, stop=False)
                        last = mm(o[:, P:BAND0], xtok[:, 0, f * P:(f + 1) * P], band0[:, j, P:BAND0],
                                  start=False, stop=True)
                    done(last, ("pooled", j))
                features("xbc2", ("xbc", 2))
                arrived(("pool_w", 0))
                w = slot(("pool_w", 0))[:, 0:2048].rearrange("p (g k n) -> p g k n", g=4, k=2)
                pooled = xdt[:, :, :].rearrange("p a b -> p (a b)").rearrange("p (f s) -> p f s", f=KT)
                for j in range(4):
                    pe.wait_ge(*taken(("pooled", j), L))
                    pe.wait_ge(*free(("mixed", j), L))
                    for i in range(2):
                        for k in range(2):
                            last = mm(ps(("mixed", j))[:, i * SEQ:(i + 1) * SEQ], w[:, j, k, i * P:(i + 1) * P],
                                      pooled[:, 2 * j + k, :], start=k == 0, stop=k == 1)
                            if i + j + k == 0:
                                last.then_inc(unit_free, 1)
                    done(last, ("mixed", j))
                scores(1)
                features("xbc3", ("xbc", 3))

                pe.wait_ge(dt_split, L + 1)
                pe.wait_ge(*free("dt", L))
                for t in range(TT):
                    for k in range(KT):
                        cols = slice(t * P, (t + 1) * P)
                        start, last = product(ps("dt")[:, t * 16:(t + 1) * 16], (hT[:, k, cols], hT_lo[:, k, cols]),
                                              (dt_hi[:, k, :], dt_lo[:, k, :]), k == 0, k == KT - 1, False)
                        if t + k == 0:
                            start.then_inc(unit_free, 1)
                done(last, "dt")

                tokens("g_pool0", ("gate", 4), h2)
                tokens("g_pool1", ("gate", 5), h2)
                probs_transposes(0)
                values(0)
                scores(2)
                pe.wait_ge(*taken(("mixed", 3), L))
                tokens("b_pool0", ("branch", 4), (poolT, poolT_lo))
                probs_transposes(1)
                values(1)
                scores(3)
                tokens("b_pool1", ("branch", 5), (poolT, poolT_lo))
                probs_transposes(2)
                values(2)
                tokens("z0", ("z", 0), h2)
                probs_transposes(3)
                values(3)

                pe.wait_ge(dA_ready, L + 1)
                pe.wait_ge(*free("dsum", L))
                mm(ps("dsum")[:, 0:16], after, dA[:, 0, :], start=True, stop=True)
                done(mm(ps("dsum")[:, 16:32], upto, dA[:, 1, :], start=True, stop=True), "dsum")
                pe.wait_ge(silu_done, L * 4 + 4)
                for j in range(4):
                    t, half = j // 2, j % 2
                    pe.wait_ge(*free(("xT", j), L))
                    for i in range(4):
                        last = tr(ps(("xT", j))[:, i * P:(i + 1) * P],
                                  xconv[:, 4 * half + i, t * P:(t + 1) * P], ident)
                    done(last, ("xT", j))

                def y(n):
                    g, c = SSD_ROUNDS[n]
                    pe.wait_ge(decay_ready, L * 8 + (n + 1))
                    pe.wait_ge(*free(("y", n), L))
                    for r in range(SSD_R):
                        hd = SSD_R * g + r
                        last = mm(ps(("y", n))[:, r * SSD_P:(r + 1) * SSD_P], E[:, n % 2, r, :],
                                  xdt[:, c, hd * SSD_P:(hd + 1) * SSD_P], start=True, stop=True)
                    if c == 1:
                        last = mm(ps(("y", n))[:, GW:2 * GW], cbm[:, g % 2, 2, :],
                                  xde[:, g * GW:(g + 1) * GW], start=True, stop=True)
                    done(last, ("y", n))

                for n, (g, c) in enumerate(SSD_ROUNDS):
                    if n == 7:
                        pe.wait_ge(att_split, L + 1)
                    if n in SSD_FILL:
                        tokens(SSD_FILL[n][0], SSD_FILL[n][1], (att_hi, att_lo) if n == 7 else h2)
                    if c == 0:
                        pe.wait_ge(*free(("cb", g), L))
                        for i, (s, l) in enumerate(((0, 0), (1, 1), (0, 1))):
                            last = mm(ps(("cb", g))[:, i * P:(i + 1) * P], xconv[:, 8 + g, s * P:(s + 1) * P],
                                      xconv[:, 12 + g, l * P:(l + 1) * P], start=True, stop=True)
                        done(last, ("cb", g))
                    pe.wait_ge(seg_built, L * 8 + (n + 1))
                    pe.wait_ge(*free(("seg", n), L))
                    for r in range(SSD_R):
                        last = mm(ps(("seg", n))[:, r * P:(r + 1) * P], segs[:, n % 2, r, :], upto,
                                  start=True, stop=True)
                    done(last, ("seg", n))
                    if n == 1:
                        pe.wait_ge(xdt_ready, L + 1)
                    if n >= 1:
                        y(n - 1)
                y(len(SSD_ROUNDS) - 1)
                tokens("b_att1", ("branch", 3), (att_hi, att_lo))
                tokens("g_ssd0", ("gate", 0), h2)
                for t in range(TT):
                    transposes("yT", t, xtok, (ssd_ready, L * TT + (t + 1)))
                tokens("g_ssd1", ("gate", 1), h2)
                pe.wait_ge(*taken(("yT", 1, 1), L))
                tokens_in_turn("b_ssd0", ("branch", 0), (yT, yT_lo))

                def merged_transposes(t):
                    transposes("mT", t, G[:, 0, :, :], (merged_ready, L * TT + (t + 1)))

                tokens_in_turn("b_ssd1", ("branch", 1), (yT, yT_lo), then=lambda: merged_transposes(0))
                tokens_in_turn("out0", ("out", 0), h2, ("mT", lambda t: t and merged_transposes(t)))
                tokens_in_turn("out1", ("out", 1), h2)

                pe.wait_ge(late_params_full, L * 48 + 48)
                pe.wait_ge(*free("pT", L))
                for k in range(2):
                    for t in range(TT):
                        last = tr(ps("pT")[:, k * SEQ + t * P:k * SEQ + (t + 1) * P],
                                  prow[:, t, k * P:(k + 1) * P], ident)
                done(last, "pT")
                arrived(("ple_proj", 0))
                wp = slot(("ple_proj", 0))[:, 0:2 * D].rearrange("p (k n) -> p k n", k=2)

                def projection(t, *halves):
                    for j in halves or range(2):
                        name = ("proj", t, j)
                        pe.wait_ge(*free(name, L))
                        for k in range(2):
                            last = mm(ps(name)[:, :], pT[:, k, t * P:(t + 1) * P],
                                      wp[:, k, j * HALF:(j + 1) * HALF], start=k == 0, stop=k == 1)
                            if t + j + k == 0:
                                last.then_inc(unit_free, 1)
                        done(last, name)

                h_transposed("hT2", 0, 1)
                pe.wait_ge(*taken("pT", L))
                projection(0)
                for t in range(TT):
                    if t == 1:
                        h_transposed("hT2", 1, 1)
                    pe.wait_ge(*taken(("hT2", t, 1), L))
                    if t == 0:
                        pe.wait_ge(*free("router", L))
                    for k in range(KT):
                        last = mm(ps("router")[:, t * 20:(t + 1) * 20], hT_plain[:, k, t * P:(t + 1) * P],
                                  rw[:, k, :], start=k == 0, stop=k == KT - 1)
                done(last, "router")
                projection(1, 0)
                pe.wait_ge(group_ready, L + 1)
                pe.wait_ge(*free("rank", L))
                hot = rt[:, 6, :, 0:MOE_G]
                mm(ps("rank")[:, 0:4], upto, hot[:, 0, :], start=True, stop=True)
                mm(ps("rank")[:, 4:8], upto, hot[:, 1, :], start=True, stop=False)
                mm(ps("rank")[:, 4:8], ones, hot[:, 0, :], start=False, stop=True)
                mm(ps("rank")[:, 8:12], ones, hot[:, 0, :], start=True, stop=False)
                done(mm(ps("rank")[:, 8:12], ones, hot[:, 1, :], start=False, stop=True), "rank")

                projection(1, 1)

                def gate_up(e):
                    arrived(("gu", e))
                    w = slot(("gu", e)).rearrange("p (k n) -> p k n", k=KT)
                    for i, name in enumerate((("hg", e), ("hu", e))):
                        pe.wait_ge(*free(name, L))
                        for f in range(2):
                            c = (2 * i + f) * P
                            for k in range(KT):
                                last = mm(ps(name)[:, f * SEQ:(f + 1) * SEQ], w[:, k, c:c + P],
                                          hT_plain[:, k, :], start=k == 0, stop=k == KT - 1)
                                if i + f + k == 0:
                                    last.then_inc(unit_free, 1)
                        done(last, name)

                def free_acc():
                    for t in range(TT):
                        for j in range(2):
                            pe.wait_ge(*free(("acc", t, j), L))

                pe.wait_ge(flag_ready, L + 1)
                pe.sem_inc(passed_wait, 1)
                with pe.If(pe.value_load(overflow[0:1, 0:1], min_val=0, max_val=1) == 0):
                    pe.wait_ge(sel_ready, L + 1)
                    for d in range(KT):
                        name = ("sorted", d)
                        pe.wait_ge(*free(name, L))
                        for t in range(TT):
                            last = mm(ps(name)[:, 0:NS], h[:, t, d * P:(d + 1) * P], sel[:, t, :],
                                      start=t == 0, stop=t == 1)
                        done(last, name)
                    pe.wait_ge(*taken(("sorted", KT - 1), L))

                    def gate_up_piece(e, i):
                        pe.wait_ge(*split(("gu", e), i, L))
                        _, lo, hi = piece(("gu", e), i)
                        slots = slice(e // MOE_E * CAP, (e // MOE_E + 1) * CAP)
                        for kk in range(2):
                            k = 2 * i + kk
                            start, last = product(ps(("hgu", e))[0:CAP, :], (hS[:, k, slots], hS_lo[:, k, slots]),
                                                  (hi[:, kk, :], lo[:, kk, :]), k == 0, k == KT - 1, kk == 1)
                            if k == 0:
                                start.then_inc(unit_free, 1)
                            if k == KT - 1:
                                done(last, ("hgu", e))

                    def expert_transposes(e):
                        pe.wait_ge(act_ready, L * NE + (e + 1))
                        pe.wait_ge(*free(("uT", e), L))
                        for k in range(2):
                            last = tr(ps(("uT", e))[:, k * CAP:(k + 1) * CAP], u_s[0:CAP, e % 2, k * P:(k + 1) * P],
                                      ident[0:CAP, 0:CAP])
                        done(last, ("uT", e))

                    def down_piece(e, i):
                        g, x, k = e // MOE_E, e % MOE_E, i % 2
                        unit = ("down", e - e % 2)
                        if k == 0:
                            pe.wait_ge(*taken(("uT", e), L))
                        pe.wait_ge(*split(unit, i, L))
                        _, lo, hi = piece(unit, i)
                        for j in range(2):
                            if x + k == 0:
                                pe.wait_ge(*free(("yg", g, j), L))
                            start, last = product(
                                ps(("yg", g, j))[0:CAP, :], (uT_hi[:, e % 2, k, :], uT_lo[:, e % 2, k, :]),
                                (hi[:, j, :], lo[:, j, :]), x + k == 0, x + k == MOE_E, j == 1)
                            if i + j == 0:
                                start.then_inc(unit_free, 1)
                            if x + k == MOE_E:
                                done(last, ("yg", g, j))

                    def slot_weights(g):
                        pe.wait_ge(combine_ready, L + 1)
                        pe.wait_ge(*free(("weight", g), L))
                        for t in range(TT):
                            last = mm(ps(("weight", g))[0:CAP, 0:MOE_E], sel[:, t, g * CAP:(g + 1) * CAP],
                                      rt[:, COMBINE, t, g * MOE_E:(g + 1) * MOE_E], start=t == 0, stop=t == 1)
                        done(last, ("weight", g))

                    def selection_transposes(g):
                        pe.wait_ge(*free(("back", g), L))
                        for t in range(TT):
                            last = tr(ps(("back", g))[0:CAP, t * P:(t + 1) * P],
                                      sel[:, t, g * CAP:(g + 1) * CAP], ident)
                        done(last, ("back", g))

                    for e in range(0, NE, 2):
                        pe.wait_ge(*free(("hgu", e), L))
                        for i in range(PIECES):
                            gate_up_piece(e, i)
                        pe.wait_ge(*free(("hgu", e + 1), L))
                        for i in range(PIECES):
                            gate_up_piece(e + 1, i)
                            if e == 0 and i < 2:
                                slot_weights(2 * i)
                                slot_weights(2 * i + 1)
                            elif e == 0:
                                selection_transposes(2 * i - 4)
                                selection_transposes(2 * i - 3)
                            if i == 2:
                                expert_transposes(e)
                        down_piece(e, 0)
                        expert_transposes(e + 1)
                        down_piece(e, 1)
                        down_piece(e + 1, 2)
                        down_piece(e + 1, 3)
                    free_acc()
                    for g in range(MOE_G):
                        pe.wait_ge(*taken(("yg", g, 1), L))
                        for t in range(TT):
                            for j in range(2):
                                rows_, cols = reduced(selT[0:CAP, g, t * P:(t + 1) * P]), slice(j * HALF, (j + 1) * HALF)
                                mm(ps(("acc", t, j))[:, :], rows_, reduced(yg_lo[g // 2][0:CAP, g % 2, cols]),
                                   start=g == 0, stop=False)
                                last = mm(ps(("acc", t, j))[:, :], rows_, reduced(yg[0:CAP, g, cols]),
                                          start=False, stop=g == MOE_G - 1)
                                if g == MOE_G - 1:
                                    done(last, ("acc", t, j))
                with pe.Else():
                    for e in range(0, NE, 2):
                        gate_up(e)
                        gate_up(e + 1)
                        if e == 0:
                            pe.wait_ge(combine_ready, L + 1)
                            for b in range(NE // 2):
                                pe.wait_ge(*free(("comb", b), L))
                                for i in range(2):
                                    x1 = 2 * b + i
                                    for t in range(TT):
                                        last = mm(ps(("comb", b))[:, i * SEQ + t * P:i * SEQ + (t + 1) * P],
                                                  rt[:, COMBINE, t, x1:x1 + 1].to_broadcast([P, P]), ident,
                                                  start=True, stop=True)
                                done(last, ("comb", b))
                            free_acc()
                            pe.sem_inc(bank_full[4], NE // 2)
                            pe.sem_inc(bank_full[5], NE // 2)
                        arrived(("down", e))
                        for i in range(2):
                            w = slot(("down", e))[:, i * 2048:(i + 1) * 2048].rearrange("p (k n) -> p k n", k=2)
                            pe.wait_ge(act_ready, L * NE + (e + i + 1))
                            for t in range(TT):
                                for j in range(2):
                                    for k in range(2):
                                        last = mm(ps(("acc", t, j))[:, :],
                                                  act_t[:, i, k * SEQ + t * P:k * SEQ + (t + 1) * P],
                                                  w[:, k, j * HALF:(j + 1) * HALF],
                                                  start=e + i + k == 0, stop=e + i + k == NE)
                                        if i + t + j + k == 0:
                                            last.then_inc(unit_free, 1)
                                    if e + i == NE - 1:
                                        done(last, ("acc", t, j))

                    pe.sem_inc(piece_free, PIECES * len(MOE_UNITS))
                tokens_in_turn("pg0", ("ple_gate", 0), h2, ("hT3", lambda t: h_transposed("hT3", t, 2)))
                tokens_in_turn("pg1", ("ple_gate", 1), h2)

        @block.scalar
        def _(act):
            def ev(out_, name, L, func=ACT.Copy, in_=None, last=True, **kw):
                ins = nc.scalar.activation(out_, ps(name)[:, :] if in_ is None else in_, func, **kw)
                if last:
                    ins.then_inc(bank_free[JOB_AT[name][0]], 1)

            act.dma_start(h[:, 1, :], x[0, P:2 * P, :]).then_inc(start_loads[1], 16)
            act.wait_ge(angles_ready, 1)
            nc.scalar.activation(sinT[:], ang[:, 2], ACT.Sin)
            nc.scalar.activation(cosT[:], ang[:, 3], ACT.Sin).then_inc(sines_done, 1)
            act.dma_start(cst[:, NFIRST:NCONST], consts[:, NFIRST:NCONST]).then_inc(const_loaded, 16)
            with act.Fori(0, DEPTH) as L:

                def evict_split(name, dst, t):
                    for j in range(2):
                        act.wait_ge(*full((name, t, j), L))
                        nc.scalar.activation(reduced(dst[:, 4 * j:4 * j + 4, t * P:(t + 1) * P]),
                                             ps((name, t, j)).rearrange("p (a b) -> p a b", a=4),
                                             ACT.Copy).then_inc(rounded, 1)

                def rounding(unit, pieces=range(PIECES)):
                    u = UNIT_AT[unit]
                    act.wait_ge(unit_full[u % RING], L * (NU // RING * 32) + 32 * (u // RING + 1))
                    for i in pieces:
                        whole, _, hi = piece(unit, i)
                        act.wait_ge(piece_free, L * NPIECE + (PIECE_AT[unit] + i + 1))
                        nc.scalar.activation(reduced(hi), whole, ACT.Copy).then_inc(piece_rounded, 1)

                def evict_transposed(name, dst):
                    for t in range(TT):
                        for j in range(2):
                            act.wait_ge(*full((name, t, j), L))
                            ev(dst[:, 4 * j:4 * j + 4, t * P:(t + 1) * P], (name, t, j), L,
                               in_=ps((name, t, j)).rearrange("p (a b) -> p a b", a=4))

                def evict_pair(name, n, dst, func):
                    for t in range(TT):
                        act.wait_ge(*full((name, t), L))
                        ev(dst[:, t, n * HALF:(n + 1) * HALF], (name, t), L, func)

                def xbc(n):
                    for b in range(2):
                        act.wait_ge(*full((f"xbc{n}", b), L))
                        if n >= 2 and b == 0:
                            act.wait_ge(conv_done, L * 4 + (n - 1))
                        ev(xin[:, n % 2, 2 * b:2 * b + 2, 3:3 + SEQ], (f"xbc{n}", b), L,
                           in_=ps((f"xbc{n}", b)).rearrange("p (a b) -> p a b", a=2))

                def silu(n):
                    act.wait_ge(conv_done, L * 4 + (n + 1))
                    v = xconv[:, 4 * n:4 * n + 4, :]
                    nc.scalar.activation(v, v, ACT.Silu).then_inc(silu_done, 1)

                def exp_scores(r):
                    t, _ = ROUNDS[r]
                    act.wait_ge(scores_ready, L * 4 + (r + 1))
                    v = P0[:, :, :] if t == 0 else P1[:, :, CHUNK:SEQ]
                    nc.scalar.activation(amax[:, 3 + (r % 2), :], amax[:, 1 + (r % 2), :], ACT.Exp)
                    nc.scalar.activation(v, v, ACT.Exp).then_inc(exp_done, 1)

                def probs_values(r):
                    t, half = ROUNDS[r]
                    for b in range(2 if t == 0 else 4):
                        act.wait_ge(*full(("PT", r, b), L))
                        o = PTs[:, 0, b] if t == 0 else PTs[:, b // 2, b % 2]
                        ev(o.rearrange("p a b -> p (a b)"), ("PT", r, b), L)
                    for g in range(2):
                        act.wait_ge(*full(("PV", r, g), L))
                        v = ps(("PV", r, g))[0:HD, :].rearrange("p (a b c) -> p a b c", a=2, b=2)
                        f = 4 * half + 2 * g
                        for b in range(2):
                            ev(attT[b * HD:(b + 1) * HD, f:f + 2, t * P:(t + 1) * P], ("PV", r, g), L,
                               in_=v[:, :, b, :], last=b == 1)

                rounding(("q", 0), (0,))
                evict_split("hT1", hT, 0)
                rounding(("q", 0), (1, 2, 3))
                evict_split("hT1", hT, 1)
                rounding(("q", 1))
                rounding(("kv", 0))
                rounding(("pu", 0))
                rounding(("pu", 1))
                evict_pair("pu0", 0, xtok, ACT.Copy)
                rounding(("xbc", 0))
                evict_pair("pu1", 1, xtok, ACT.Copy)
                for t in range(TT):
                    for j in range(2):
                        act.wait_ge(*full(("qT", t, j), L))
                        ev(qT[:, 4 * j:4 * j + 4, t * P:(t + 1) * P], ("qT", t, j), L,
                           in_=ps(("qT", t, j)).rearrange("p (a b) -> p a b", a=4))
                    act.wait_ge(*full(("kT", t), L))
                    ev(kT[:, :, t * P:(t + 1) * P], ("kT", t), L,
                       in_=ps(("kT", t)).rearrange("p (a b) -> p a b", a=4))
                rounding(("xbc", 1))
                xbc(0)
                rounding(("xbc", 2), (0, 1))
                xbc(1)
                pooled = xdt[:, :, :].rearrange("p a b -> p (a b)")
                for j in range(4):
                    act.wait_ge(*full(("pooled", j), L))
                    ev(pooled[:, j * HALF:(j + 1) * HALF], ("pooled", j), L)
                    if j == 1:
                        rounding(("xbc", 2), (2, 3))
                silu(0)
                rounding(("xbc", 3))
                xbc(2)
                for j in range(4):
                    act.wait_ge(*full(("mixed", j), L))
                    for i in range(2):
                        f = 2 * j + i
                        ins = nc.scalar.activation(reduced(poolT[:, f, :]), ps(("mixed", j))[:, i * SEQ:(i + 1) * SEQ],
                                                   ACT.Copy, scale=vecT[:, V_PS + f:V_PS + f + 1])
                    ins.then_inc(rounded, 1)
                silu(1)
                u = UNIT_AT[("dt", 0)]
                act.wait_ge(unit_full[u % RING], L * (NU // RING * 32) + 32 * (u // RING + 1))
                nc.scalar.activation(reduced(dt_hi[:, :, :]),
                                     slot(("dt", 0)).rearrange("p (k n) -> p k n", k=KT)[:, :, 0:SSD_HEADS],
                                     ACT.Copy).then_inc(dt_rounded, 1)
                rounding(("gate", 4))
                xbc(3)
                silu(2)
                rounding(("gate", 5), (0, 1))
                silu(3)
                rounding(("gate", 5), (2, 3))
                act.wait_ge(dt_pre, L + 1)
                nc.scalar.activation(sm[:, 2, :], sm[:, 1, :], ACT.Exp, scale=-1.0)
                nc.scalar.activation(sm[:, 3, 0:16], rows[:, 16:32], ACT.Exp).then_inc(dt_exp, 1)
                exp_scores(0)
                exp_scores(1)
                rounding(("branch", 4), (0, 1))
                evict_pair("g_pool0", 0, G[:, 0], ACT.Sigmoid)
                rounding(("branch", 4), (2, 3))
                probs_values(0)
                evict_pair("g_pool1", 1, G[:, 0], ACT.Sigmoid)
                exp_scores(2)
                rounding(("branch", 5))
                probs_values(1)
                exp_scores(3)
                rounding(("z", 0))
                probs_values(2)
                rounding(("z", 1))
                zs = qT.rearrange("p a b -> p (a b)").rearrange("p (t d) -> p t d", t=TT)
                probs_values(3)
                act.wait_ge(*full("dsum", L))
                ev(dexp[:, :, :], "dsum", L, ACT.Exp,
                   in_=ps("dsum")[:, 0:32].rearrange("p (a b) -> p a b", a=2))
                for j in range(4):
                    act.wait_ge(*full(("xT", j), L))
                    ev(xtok[:, j // 2, (j % 2) * HALF:(j % 2 + 1) * HALF], ("xT", j), L)
                for n in range(len(SSD_ROUNDS)):
                    if n in SSD_FILL:
                        rounding(SPLIT_UNITS[SPLIT_UNITS.index(SSD_FILL[n][1]) + 1])
                    act.wait_ge(*full(("seg", n), L))
                    ev(E[:, n % 2, :, :].rearrange("p a b -> p (a b)"), ("seg", n), L, ACT.Exp)
                    if n == 0:
                        evict_pair("z0", 0, zs, ACT.Silu)
                    if n == 2:
                        evict_pair("z1", 1, zs, ACT.Silu)
                    if n in (4, 6):
                        evict_pair(f"g_att{n // 2 - 2}", n // 2 - 2, G[:, 1], ACT.Sigmoid)
                    if n == 3:
                        for t in range(TT):
                            last = nc.scalar.activation(reduced(att_hi[:, 4 * t:4 * t + 4, :]),
                                                        attT[:, 4 * t:4 * t + 4, :], ACT.Copy)
                        last.then_inc(att_rounded, 1)
                rounding(("gate", 0), (0, 1, 2))
                act.wait_ge(gy_ms, L + 1)
                nc.scalar.activation(gss[:, 1], gss[:, 0], ACT.Sqrt).then_inc(gy_sqrt, 1)
                rounding(("gate", 0), (3,))
                rounding(("gate", 1))
                act.wait_ge(merge_step, L + 1)
                evict_pair("g_ssd0", 0, G[:, 1], ACT.Sigmoid)
                for t in range(TT):
                    for j in range(2):
                        act.wait_ge(*full(("yT", t, j), L))
                        for i in range(4):
                            f = 4 * j + i
                            ins = nc.scalar.activation(reduced(yT[:, f, t * P:(t + 1) * P]),
                                                       ps(("yT", t, j))[:, i * P:(i + 1) * P],
                                                       ACT.Copy, scale=vecT[:, V_NW + f:V_NW + f + 1])
                        ins.then_inc(rounded, 1)
                    rounding(("branch", 0), (0,) if t == 0 else (1, 2, 3))
                evict_pair("g_ssd1", 1, G[:, 1], ACT.Sigmoid)
                rounding(("branch", 1))
                rounding(("out", 0), (0, 1, 2))
                evict_split("mT", hT, 0)
                rounding(("out", 0), (3,))
                evict_split("mT", hT, 1)
                rounding(("out", 1))

                def ln_sqrt(i, t):
                    act.wait_ge(var_ready, L * 6 + (2 * i + t + 1))
                    nc.scalar.activation(rstd[:, 0, t:t + 1], mv[:, t, 1:2], ACT.Sqrt).then_inc(sqrt_done, 1)

                ln_sqrt(0, 0)
                act.wait_ge(*full("pT", L))
                ev(pts_cb[:, 0:2 * SEQ], "pT", L)
                ln_sqrt(0, 1)
                evict_transposed("hT2", hT_plain)
                act.wait_ge(rexp_in, L * 2 + 1)
                nc.scalar.activation(rt[:, 3, :, 0:4], rt[:, 2, :, 0:4], ACT.Exp).then_inc(rexp_out, 1)
                for t in range(TT):
                    for j in range(2):
                        act.wait_ge(*full(("proj", t, j), L))
                        ev(xtok[:, t, j * HALF:(j + 1) * HALF], ("proj", t, j), L)
                act.wait_ge(rexp_in, L * 2 + 2)
                nc.scalar.activation(rt[:, 12, :, 0:1], rt[:, 11, :, 0:1], ACT.Exp).then_inc(rexp_out, 1)

                def act_s_free(e):
                    if e >= 2:
                        act.wait_ge(act_ready, L * NE + (e - 1))

                act.wait_ge(flag_ready, L + 1)
                act.sem_inc(passed_wait, 1)
                with act.If(act.value_load(overflow[0:1, 0:1], min_val=0, max_val=1) == 0):
                    rounding(("gu", 0), (0, 1))
                    for d in range(KT):
                        act.wait_ge(*full(("sorted", d), L))
                        nc.scalar.activation(reduced(hS[:, d, :]), ps(("sorted", d))[:, 0:NS],
                                             ACT.Copy).then_inc(rounded, 1)
                        if d < 2:
                            rounding(("gu", 0), (2 + d,))

                    def silu_gate(e):
                        act.wait_ge(*full(("hgu", e), L))
                        act_s_free(e)
                        nc.scalar.activation(gate_s[0:CAP, e % 2, :], ps(("hgu", e))[0:CAP, 0:HID],
                                             ACT.Silu).then_inc(silu_s, 1)

                    def slot_weights(g):
                        act.wait_ge(*full(("weight", g), L))
                        ev(weight_s[0:CAP, MOE_E * g:MOE_E * (g + 1)], ("weight", g), L,
                           in_=ps(("weight", g))[0:CAP, 0:MOE_E])

                    def selection(g):
                        act.wait_ge(*full(("back", g), L))
                        ev(reduced(selT[0:CAP, g, :]), ("back", g), L, in_=ps(("back", g))[0:CAP, 0:SEQ])

                    def group_rounded(g, j):
                        act.wait_ge(*full(("yg", g, j), L))
                        nc.scalar.activation(reduced(yg[0:CAP, g, j * HALF:(j + 1) * HALF]),
                                             ps(("yg", g, j))[0:CAP, :], ACT.Copy).then_inc(rounded, 1)

                    def expert_rounded(e):
                        act.wait_ge(*full(("uT", e), L))
                        nc.scalar.activation(reduced(uT_hi[:, e % 2]),
                                             ps(("uT", e))[:, 0:2 * CAP].rearrange("p (k s) -> p k s", k=2),
                                             ACT.Copy).then_inc(rounded, 1)

                    for e in range(0, NE, 2):
                        rounding(("gu", e + 1), (0, 1, 2))
                        if e >= 2 and e % MOE_E == 0:
                            g = e // MOE_E - 1
                            for j in range(2):
                                group_rounded(g, j)
                        rounding(("gu", e + 1), (3,))
                        silu_gate(e)
                        if e == 0:
                            slot_weights(0)
                            slot_weights(1)
                        rounding(("down", e), (0,))
                        if e == 0:
                            slot_weights(2)
                            slot_weights(3)
                        if e == 0:
                            selection(0)
                            selection(1)
                        expert_rounded(e)
                        rounding(("down", e), (1,))
                        if e == 0:
                            selection(2)
                            selection(3)
                        silu_gate(e + 1)
                        rounding(("down", e), (2, 3))
                        after_down = SPLIT_UNITS[SPLIT_UNITS.index(("down", e)) + 1]
                        expert_rounded(e + 1)
                        if e < NE - 2:
                            rounding(after_down)
                        else:
                            rounding(after_down, (0, 1, 2))
                            for j in range(2):
                                group_rounded(MOE_G - 1, j)
                            rounding(after_down, (3,))
                with act.Else():
                    for e in range(NE):
                        act.wait_ge(*full(("hg", e), L))
                        act_s_free(e)
                        ev(act_s[:, e % 2, :], ("hg", e), L, ACT.Silu)
                        if e == 1:
                            for b in range(NE // 2):
                                act.wait_ge(*full(("comb", b), L))
                                ev(comb[:, 2 * b:2 * b + 2, :].rearrange("p a b -> p (a b)"), ("comb", b), L)
                            act.sem_inc(bank_free[4], NE // 2)
                            act.sem_inc(bank_free[5], NE // 2)
                    act.sem_inc(silu_s, NE)
                    act.sem_inc(rounded, KT + NE + 2 * MOE_G)
                    act.sem_inc(piece_rounded, PIECES * len(MOE_UNITS))
                    rounding(("ple_gate", 0))
                ln_sqrt(1, 0)
                ln_sqrt(1, 1)
                evict_split("hT3", hT, 0)
                evict_split("hT3", hT, 1)
                rounding(("ple_gate", 1))
                for j in range(2):
                    evict_pair(f"pg{j}", j, G[:, 0], ACT.Sigmoid)
                ln_sqrt(2, 0)
                ln_sqrt(2, 1)

        @block.gpsimd
        def _(pool):
            with nc.allow_non_contiguous_dma(reason="256 positions, once"):
                pool.dma_start(posi[:], positions[0].rearrange("(t p) -> p t", p=P)).then_inc(pos_loaded, 16)
            with pool.Fori(0, DEPTH) as L:
                def remainders(unit):
                    for i in remainder_on_pool(unit):
                        whole, lo, hi = piece(unit, i)
                        pool.wait_ge(piece_rounded, L * NPIECE + (PIECE_AT[unit] + i + 1))
                        nc.gpsimd.tensor_tensor(reduced(lo), whole, hi, ALU.subtract).then_inc(remainder_ready["pool"], 1)

                remainders(("q", 0))
                pool.wait_ge(params_free, L + 1)
                pool.sem_inc(passed_wait, 1)
                T = XBC_T
                loads = [
                    (vecrows[0:SSD_CONV * T, :], conv_w[L].rearrange("k (c p) -> (k c) p", p=P)),
                    (vecrows[V_CB:V_CB + T, :], conv_b[L].rearrange("(c p) -> c p", p=P)),
                    (vecrows[V_PS:V_PS + KT, :], pool_scale[L].rearrange("(c p) -> c p", p=P)),
                    (vecrows[V_NW:V_NW + KT, :], norm_w[L].rearrange("(c p) -> c p", p=P)),
                    (rows[:, 0:16], dt_bias[L].unsqueeze(0).broadcast_to([P, 16])),
                    (rows[:, 16:32], a_log[L].unsqueeze(0).broadcast_to([P, 16])),
                    (rows[:, 32:48], ssd_d[L].unsqueeze(0).broadcast_to([P, 16])),
                    (rows[:, 48:64], sinks[L].unsqueeze(0).broadcast_to([P, 16])),
                    (rows[:, 64:68], rg_b[L].unsqueeze(0).broadcast_to([P, 4])),
                    (rows[:, 68:84], re_b[L].unsqueeze(0).broadcast_to([P, 16])),
                ]
                assert 16 * len(loads) == PARAM_INC
                for n, unit in enumerate(SPLIT_UNITS[1:4]):
                    for d, s in loads[n * len(loads) // 3:(n + 1) * len(loads) // 3]:
                        pool.dma_start(d, s).then_inc(params_full, 16)
                    remainders(unit)

                def ln_params(i, g, b):
                    pool.wait_ge(lnp_free, L * 3 + (i + 1))
                    pool.sem_inc(passed_wait, 1)
                    for j, v in enumerate((g, b)):
                        pool.dma_start(lnp[:, j, :], v[L].unsqueeze(0).broadcast_to([P, D])).then_inc(lnp_full, 16)

                ln_params(0, ln1_g, ln1_b)
                for unit in SPLIT_UNITS[4:SPLIT_UNITS.index(("z", 0)) + 1]:
                    remainders(unit)
                pool.wait_ge(dA_ready, L + 1)
                pool.wait_ge(*full(("PT", 3, 3), L))
                fills = {0: ("z", 1), 2: ("gate", 2), 4: ("gate", 3), 6: ("branch", 2), 7: ("branch", 3)}
                for n, (g, c) in enumerate(SSD_ROUNDS):
                    if n >= 2:
                        pool.wait_ge(*full(("seg", n - 2), L))
                    nc.gpsimd.tensor_tensor(
                        segs[:, n % 2, :, :], after.unsqueeze(1).broadcast_to([P, SSD_R, P]),
                        dA[:, c, SSD_R * g:SSD_R * (g + 1)].unsqueeze(2).broadcast_to([P, SSD_R, P]),
                        ALU.mult).then_inc(seg_built, 1)
                    if n in fills:
                        remainders(fills[n])
                pool.wait_ge(*full(("y", len(SSD_ROUNDS) - 1), L))
                pool.sem_inc(passed_wait, 1)
                for d, s in ((prow[:, :, :], p[L, 0].rearrange("(t p) n -> p t n", p=P)),
                             (rw[:, :, 0:4], rg_w[L].rearrange("(k p) n -> p k n", p=P)),
                             (rw[:, :, 4:20], re_w[L].rearrange("(k p) n -> p k n", p=P))):
                    pool.dma_start(d, s).then_inc(late_params_full, 16)
                remainders(("gate", 0))
                pool.wait_ge(*taken(("b_att1", 1), L))
                nc.gpsimd.tensor_tensor(G[:, 0], G[:, 0], G[:, 1], ALU.add).then_inc(merge_step, 1)
                for unit in SPLIT_UNITS[SPLIT_UNITS.index(("gate", 1)):SPLIT_UNITS.index(MOE_UNITS[0])]:
                    remainders(unit)
                ln_params(1, ln2_g, ln2_b)
                pool.wait_ge(flag_ready, L + 1)
                pool.sem_inc(passed_wait, 1)
                with pool.If(pool.value_load(overflow[0:1, 0:1], min_val=0, max_val=1) == 0):
                    for unit in MOE_UNITS:
                        remainders(unit)
                with pool.Else():
                    pool.sem_inc(remainder_ready["pool"], MOE_REMAINDERS["pool"])
                remainders(("ple_gate", 0))
                remainders(("ple_gate", 1))
                ln_params(2, ln3_g, ln3_b)

        @block.vector
        def _(dve):
            V = nc.vector
            steps = [0]

            def link(ins, base):
                steps[0] += 1
                ins.then_inc(dve_step, 1)
                dve.wait_ge(dve_step, base + steps[0])

            def frees(ins, name):
                ins.then_inc(bank_free[JOB_AT[name][0]], 1)

            V.memset(xin[:, :, :, 0:3], 0.0).then_inc(h_ready, 4)
            for t in range(TT):
                dve.wait_ge(start_loads[t], 32 - 16 * t)
            dve.wait_ge(pos_loaded, 16)
            link(V.tensor_copy(posf[:], posi[:]), 0)
            for t in range(TT):
                last = V.tensor_scalar(ang[:, 0, t, :], const("inv"), posf[:, t:t + 1], None, ALU.mult)
            link(last, 0)
            link(V.tensor_scalar(ang[:, 1], ang[:, 0], float(1 / (2 * np.pi)), None, ALU.mult), 0)
            link(V.tensor_scalar(ang[:, 1], ang[:, 1], ROUND, None, ALU.add), 0)
            link(V.tensor_scalar(ang[:, 1], ang[:, 1], -ROUND, None, ALU.add), 0)
            link(V.scalar_tensor_tensor(out=ang[:, 2], in0=ang[:, 1], scalar=-TWO_PI[0], in1=ang[:, 0],
                                        op0=ALU.mult, op1=ALU.add), 0)
            for part in TWO_PI[1:]:
                link(V.scalar_tensor_tensor(out=ang[:, 2], in0=ang[:, 1], scalar=-part, in1=ang[:, 2],
                                            op0=ALU.mult, op1=ALU.add), 0)
            link(V.tensor_scalar(ang[:, 2], ang[:, 2], PI_F, -PI_F, ALU.min, ALU.max), 0)
            link(V.tensor_scalar(ang[:, 3], ang[:, 2], float(np.pi / 2), None, ALU.add), 0)
            link(V.tensor_scalar(ang[:, 1], ang[:, 3], PI_F, float(-2 * np.pi), ALU.is_gt, ALU.mult), 0)
            link(V.tensor_tensor(ang[:, 3], ang[:, 3], ang[:, 1], ALU.add), 0)
            V.tensor_scalar(ang[:, 3], ang[:, 3], PI_F, -PI_F, ALU.min, ALU.max).then_inc(angles_ready, 1)
            dve.wait_ge(sines_done, 1)
            link(V.tensor_scalar(nsinT[:], sinT[:], -1.0, None, ALU.mult), 0)
            dve.sem_inc(params_free, 1)
            dve.sem_inc(lnp_free, 1)
            setup_steps = steps[0]
            with dve.Fori(0, DEPTH) as L:
                steps[0] = 0
                base = L * DVE_STEPS + setup_steps

                def lk(ins):
                    link(ins, base)

                def rope(name, t, dsts):
                    n = dsts[0].shape[1]
                    v = ps(name)[:, 0:n * HD].rearrange("p (h a d) -> p h a d", a=2, d=ROT)
                    A = tA[:, 0:n * HD].rearrange("p (h a d) -> p h a d", a=2, d=ROT)
                    B = tB[:, 0:n * HD].rearrange("p (h a d) -> p h a d", a=2, d=ROT)
                    c = cosT[:, t, :].unsqueeze(1).unsqueeze(1).broadcast_to([P, n, 2, ROT])
                    s = sinT[:, t, :].unsqueeze(1).broadcast_to([P, n, ROT])
                    ns = nsinT[:, t, :].unsqueeze(1).broadcast_to([P, n, ROT])
                    dve.wait_ge(*full(name, L))
                    V.tensor_tensor(A, v, c, ALU.mult)
                    V.tensor_tensor(B[:, :, 0, :], v[:, :, 1, :], ns, ALU.mult)
                    lk(V.tensor_tensor(B[:, :, 1, :], v[:, :, 0, :], s, ALU.mult))
                    for d in dsts:
                        last = V.tensor_tensor(d, tA[:, 0:n * HD].rearrange("p (h d) -> p h d", d=HD),
                                               tB[:, 0:n * HD].rearrange("p (h d) -> p h d", d=HD), ALU.add)
                    return last

                def remainders(unit, pieces=range(PIECES)):
                    for i in pieces:
                        if i in remainder_on_pool(unit):
                            continue
                        whole, lo, hi = piece(unit, i)
                        dve.wait_ge(piece_rounded, L * NPIECE + (PIECE_AT[unit] + i + 1))
                        V.tensor_tensor(reduced(lo), whole, hi, ALU.subtract).then_inc(remainder_ready["dve"], 1)

                split_jobs = [0]

                def rounded_job():
                    split_jobs[0] += 1
                    dve.wait_ge(rounded, L * ROUNDED + split_jobs[0])

                def transposed_remainder(name, hi, lo, t):
                    for j in range(2):
                        rounded_job()
                        block_ = (slice(None), slice(4 * j, 4 * j + 4), slice(t * P, (t + 1) * P))
                        frees(V.tensor_tensor(reduced(lo[block_]), ps((name, t, j)).rearrange("p (a b) -> p a b", a=4),
                                              hi[block_], ALU.subtract), (name, t, j))

                remainders(("q", 0))
                for t in range(TT):
                    transposed_remainder("hT1", hT, hT_lo, t)
                remainders(("q", 1))
                V.memset(xin[:, :, :, 0:3], 0.0)
                V.memset(P1[:, :, 0:CHUNK], 0.0)
                for n in range(2):
                    for t in range(TT):
                        rot = G[:, t, :, :].rearrange("p a b -> p (a b)")
                        d = rot[:, n * HALF:(n + 1) * HALF].rearrange("p (h d) -> p h d", d=HD)
                        name = (f"q{n}", t)
                        ins = rope(name, t, [d])
                        frees(ins, name)
                        dve.wait_ge(*taken(name, L))
                    remainders(("kv", 0) if n == 0 else ("pu", 0))
                for t in range(TT):
                    rot = G[:, t, :, :].rearrange("p a b -> p (a b)")
                    k2 = rot[:, D:D + 2 * KV_HEADS * HD].rearrange("p (h c d) -> p h c d", c=2, d=HD)
                    lk(rope(("kv", t), t, [k2[:, :, 0, :], k2[:, :, 1, :]]))
                    frees(V.tensor_copy(vv[:, t, :], ps(("kv", t))[:, KV_HEADS * HD:2 * KV_HEADS * HD]), ("kv", t))
                    dve.wait_ge(*taken(("kv", t), L))
                    dve.sem_inc(qrot_ready, 1)
                remainders(("pu", 1))
                remainders(("xbc", 0))
                dve.wait_ge(*full("vec", L))
                frees(V.tensor_copy(vecT[:], ps("vec")[:, 0:VEC_ROWS]), "vec")
                dve.wait_ge(*taken("vec", L))

                def conv(n):
                    dve.wait_ge(*taken((f"xbc{n}", 1), L))
                    for k in (3, 2, 1, 0):
                        for i in range(4):
                            f = 4 * n + i
                            u = xin[:, n % 2, i, k:k + SEQ]
                            w = vecT[:, k * XBC_T + f:k * XBC_T + f + 1]
                            if k == 3:
                                last = V.tensor_scalar(xconv[:, f, :], u, w, vecT[:, V_CB + f:V_CB + f + 1],
                                                       ALU.mult, ALU.add)
                            else:
                                last = V.scalar_tensor_tensor(out=xconv[:, f, :], in0=u, scalar=w,
                                                              in1=xconv[:, f, :], op0=ALU.mult, op1=ALU.add)
                        if k:
                            lk(last)
                    last.then_inc(conv_done, 1)

                def shifted_scores(r):
                    t, half = ROUNDS[r]
                    per = 4 if t == 0 else 2
                    w = P if t == 0 else 192
                    mask = const("mask0") if t == 0 else const("mask1")
                    buf = P0[:, :, :] if t == 0 else P1[:, :, CHUNK:SEQ]
                    for b in range(8 // per):
                        dve.wait_ge(*full(("scores", r, b), L))
                        v = ps(("scores", r, b)).rearrange("p (h k) -> p h k", h=per)[:, :, 0:w]
                        o = (buf.rearrange("p (i c) k -> p c i k", c=2)[:, b] if t == 0 else
                             buf.rearrange("p (m i c) k -> p m c i k", m=2, c=2)[:, b // 2, b % 2])
                        frees(V.scalar_tensor_tensor(out=o, in0=v, scalar=HD ** -0.5,
                                                     in1=mask.unsqueeze(1).broadcast_to([P, per, w]),
                                                     op0=ALU.mult, op1=ALU.add), ("scores", r, b))
                    dve.wait_ge(*taken(("scores", r, 8 // per - 1), L))
                    lk(V.tensor_reduce(amax[:, 0, :], buf, AX.X, ALU.max))
                    sink = rows[:, 48 + 8 * half:56 + 8 * half]
                    lk(V.tensor_tensor(amax[:, 0, :], amax[:, 0, :], sink, ALU.max))
                    V.tensor_tensor(amax[:, 1 + (r % 2), :], sink, amax[:, 0, :], ALU.subtract)
                    V.tensor_tensor(buf, buf, amax[:, 0, :].unsqueeze(2).broadcast_to([P, 8, w]),
                                    ALU.subtract).then_inc(scores_ready, 1)

                def normalise(r):
                    t, _ = ROUNDS[r]
                    w = P if t == 0 else 192
                    buf = P0[:, :, :] if t == 0 else P1[:, :, CHUNK:SEQ]
                    dve.wait_ge(exp_done, L * 4 + (r + 1))
                    lk(V.tensor_reduce(amax[:, 5, :], buf, AX.X, ALU.add))
                    lk(V.tensor_tensor(amax[:, 5, :], amax[:, 5, :], amax[:, 3 + (r % 2), :], ALU.add))
                    lk(V.reciprocal(amax[:, 6, :], amax[:, 5, :]))
                    V.tensor_tensor(buf, buf, amax[:, 6, :].unsqueeze(2).broadcast_to([P, 8, w]),
                                    ALU.mult).then_inc(probs_ready, 1)

                dve.wait_ge(params_full, L * PARAM_INC + PARAM_INC)
                remainders(("xbc", 1))
                conv(0)
                dve.wait_ge(const_loaded, 16)
                shifted_scores(0)
                remainders(("xbc", 2))
                conv(1)
                remainders(("xbc", 3))
                for j in range(4):
                    dve.wait_ge(*full(("mixed", j), L))
                    rounded_job()
                    for i in range(2):
                        f = 2 * j + i
                        ins = V.scalar_tensor_tensor(out=reduced(poolT_lo[:, f, :]),
                                                     in0=ps(("mixed", j))[:, i * SEQ:(i + 1) * SEQ],
                                                     scalar=vecT[:, V_PS + f:V_PS + f + 1], in1=poolT[:, f, :],
                                                     op0=ALU.mult, op1=ALU.subtract)
                    frees(ins, ("mixed", j))
                w = slot(("dt", 0)).rearrange("p (k n) -> p k n", k=KT)[:, :, 0:SSD_HEADS]
                dve.wait_ge(dt_rounded, L + 1)
                V.tensor_tensor(reduced(dt_lo), w, dt_hi[:, :, :], ALU.subtract).then_inc(dt_split, 1)
                conv(2)
                remainders(("gate", 4))
                shifted_scores(1)
                conv(3)
                remainders(("gate", 5))

                dve.wait_ge(*full("dt", L))
                frees(V.tensor_tensor(sm[:, 0, :].rearrange("p (t h) -> p t h", t=TT),
                                      ps("dt")[:, 0:32].rearrange("p (t h) -> p t h", t=TT),
                                      rows[:, 0:16].unsqueeze(1).broadcast_to([P, TT, 16]), ALU.add), "dt")
                dve.wait_ge(*taken("dt", L))
                V.scalar_tensor_tensor(out=sm[:, 1, :], in0=sm[:, 0, :], scalar=-1.0, in1=sm[:, 0, :],
                                       op0=ALU.mult, op1=ALU.max).then_inc(dt_pre, 1)
                V.tensor_scalar(sm[:, 4, :], sm[:, 0, :], 0.0, None, ALU.max)
                dve.wait_ge(dt_exp, L + 1)
                lk(V.tensor_scalar(sm[:, 5, :], sm[:, 2, :], 2.0, None, ALU.add))
                lk(V.reciprocal(sm[:, 6, :], sm[:, 5, :]))
                lk(V.tensor_tensor(sm[:, 7, :], sm[:, 6, :], sm[:, 2, :], ALU.mult))
                lk(V.tensor_tensor(sm[:, 8, :], sm[:, 7, :], sm[:, 7, :], ALU.mult))
                lk(V.tensor_scalar(sm[:, 9, :], sm[:, 8, :], 1.0 / 15, None, ALU.mult))
                for m in (13, 11, 9, 7, 5, 3):
                    lk(V.scalar_tensor_tensor(out=sm[:, 9, :], in0=sm[:, 9, :], scalar=1.0 / m, in1=sm[:, 8, :],
                                              op0=ALU.add, op1=ALU.mult))
                lk(V.scalar_tensor_tensor(out=sm[:, 9, :], in0=sm[:, 9, :], scalar=1.0, in1=sm[:, 7, :],
                                          op0=ALU.add, op1=ALU.mult))
                V.tensor_scalar(nega[:], sm[:, 3, 0:16], -1.0, None, ALU.mult)
                lk(V.scalar_tensor_tensor(out=dtv[:, :, :].rearrange("p a b -> p (a b)"), in0=sm[:, 9, :], scalar=2.0,
                                          in1=sm[:, 4, :], op0=ALU.mult, op1=ALU.add))
                V.tensor_tensor(dA[:, :, :], dtv[:, :, :], nega[:].unsqueeze(1).broadcast_to([P, TT, 16]),
                                ALU.mult).then_inc(dA_ready, 1)

                normalise(0)
                normalise(1)
                remainders(("branch", 4))
                shifted_scores(2)
                remainders(("branch", 5))
                normalise(2)
                shifted_scores(3)

                def gated(name, n, g):
                    for t in range(TT):
                        gate = G[:, g, t, n * HALF:(n + 1) * HALF]
                        dve.wait_ge(*full((name, t), L))
                        frees(V.tensor_tensor(gate, gate, ps((name, t))[:, :], ALU.mult), (name, t))

                dve.wait_ge(*taken(("g_pool1", 1), L))
                gated("b_pool0", 0, 0)
                remainders(("z", 0))
                normalise(3)
                gated("b_pool1", 1, 0)
                remainders(("z", 1))

                def heads(ap):
                    return ap.rearrange("p (h d) -> p h d", d=SSD_P)

                for t in range(TT):
                    dve.wait_ge(*taken(("xT", 2 * t + 1), L))
                    lk(V.tensor_tensor(heads(xdt[:, t, :]), heads(xtok[:, t, :]),
                                       dtv[:, t, :].unsqueeze(2).broadcast_to([P, 16, SSD_P]), ALU.mult))
                    lk(V.tensor_tensor(heads(xtok[:, t, :]), heads(xtok[:, t, :]),
                                       rows[:, 32:48].unsqueeze(2).broadcast_to([P, 16, SSD_P]), ALU.mult))
                V.tensor_tensor(heads(xde), heads(xdt[:, 0, :]),
                                dexp[:, 0, :].unsqueeze(2).broadcast_to([P, 16, SSD_P]),
                                ALU.mult).then_inc(xdt_ready, 1)

                def y(n):
                    g, c = SSD_ROUNDS[n]
                    name = ("y", n)
                    dst = xtok[:, c, g * GW:(g + 1) * GW]
                    dve.wait_ge(*full(name, L))
                    if c == 1:
                        V.tensor_tensor(heads(yoff), heads(ps(name)[:, GW:2 * GW]),
                                        dexp[:, 1, SSD_R * g:SSD_R * (g + 1)].unsqueeze(2)
                                        .broadcast_to([P, SSD_R, SSD_P]), ALU.mult)
                    frees(V.tensor_tensor(dst, dst, ps(name)[:, 0:GW], ALU.add), name)
                    if c == 1:
                        dve.wait_ge(*taken(name, L))
                        lk(V.tensor_tensor(dst, dst, yoff, ALU.add))

                for n, (g, c) in enumerate(SSD_ROUNDS):
                    if n in SSD_FILL:
                        remainders(SPLIT_UNITS[SPLIT_UNITS.index(SSD_FILL[n][1]) + 1])
                    if n == 4:
                        dve.wait_ge(att_rounded, L + 1)
                        V.tensor_tensor(reduced(att_lo[:, 0:4, :]), attT[:, 0:4, :], att_hi[:, 0:4, :], ALU.subtract)
                        V.tensor_tensor(reduced(att_lo[:, 4:8, :]), attT[:, 4:8, :], att_hi[:, 4:8, :],
                                        ALU.subtract).then_inc(att_split, 1)
                    if c == 0:
                        dve.wait_ge(*full(("cb", g), L))
                        V.tensor_tensor(cbm[:, g % 2, 0:2, :], ps(("cb", g))[:, 0:2 * P].rearrange("p (a b) -> p a b", a=2),
                                        upto.unsqueeze(1).broadcast_to([P, 2, P]), ALU.mult)
                        frees(V.tensor_copy(cbm[:, g % 2, 2, :], ps(("cb", g))[:, 2 * P:3 * P]), ("cb", g))
                        dve.wait_ge(*taken(("cb", g), L))
                    dve.wait_ge(*taken(("seg", n), L))
                    V.tensor_tensor(E[:, n % 2, :, :], E[:, n % 2, :, :],
                                    cbm[:, g % 2, c, :].unsqueeze(1).broadcast_to([P, SSD_R, P]),
                                    ALU.mult).then_inc(decay_ready, 1)
                    if n >= 1:
                        y(n - 1)
                y(len(SSD_ROUNDS) - 1)
                zs = qT[:, :, :].rearrange("p a b -> p (a b)").rearrange("p (t d) -> p t d", t=TT)
                sq = xdt
                dve.wait_ge(*taken(("z1", 1), L))
                for t in range(TT):
                    last = V.tensor_tensor(xtok[:, t, :], xtok[:, t, :], zs[:, t, :], ALU.mult)
                lk(last)
                gated("b_att0", 0, 1)
                remainders(("gate", 0), (0, 1))
                for t in range(TT):
                    last = V.tensor_tensor(sq[:, t, :], xtok[:, t, :], xtok[:, t, :], ALU.mult)
                lk(last)
                lk(V.tensor_reduce(gss[:, 2], sq[:, :, :].rearrange("p t (g d) -> p t g d", g=SSD_GROUPS), AX.X, ALU.add))
                V.tensor_scalar(gss[:, 0], gss[:, 2], 1.0 / GW, EPS, ALU.mult, ALU.add).then_inc(gy_ms, 1)
                remainders(("gate", 0), (2, 3))
                gated("b_att1", 1, 1)
                dve.wait_ge(gy_sqrt, L + 1)
                lk(V.reciprocal(gss[:, 2], gss[:, 1]))
                for t in range(TT):
                    v = xtok[:, t, :].rearrange("p (g d) -> p g d", g=SSD_GROUPS)
                    V.tensor_tensor(v, v, gss[:, 2, t, :].unsqueeze(2).broadcast_to([P, SSD_GROUPS, GW]),
                                    ALU.mult).then_inc(ssd_ready, 1)
                remainders(("gate", 1))
                for t in range(TT):
                    for j in range(2):
                        rounded_job()
                        for i in range(4):
                            f = 4 * j + i
                            cols = slice(t * P, (t + 1) * P)
                            ins = V.scalar_tensor_tensor(out=reduced(yT_lo[:, f, cols]),
                                                         in0=ps(("yT", t, j))[:, i * P:(i + 1) * P],
                                                         scalar=vecT[:, V_NW + f:V_NW + f + 1], in1=yT[:, f, cols],
                                                         op0=ALU.mult, op1=ALU.subtract)
                        frees(ins, ("yT", t, j))
                    remainders(("branch", 0), (0,) if t == 0 else (1, 2, 3))
                dve.wait_ge(merge_step, L + 1)
                dve.wait_ge(*taken(("g_ssd1", 1), L))
                remainders(("branch", 1))
                gated("b_ssd0", 0, 1)
                for t in range(TT):
                    if t == 1:
                        remainders(("out", 0))
                        transposed_remainder("mT", hT, hT_lo, 0)
                    name = ("b_ssd1", t)
                    gate = G[:, 1, t, HALF:D]
                    dve.wait_ge(*full(name, L))
                    frees(V.tensor_tensor(gate, gate, ps(name)[:, :], ALU.mult), name)
                    dve.wait_ge(*taken(name, L))
                    V.tensor_tensor(G[:, 0, t, :], G[:, 0, t, :], G[:, 1, t, :], ALU.add).then_inc(merged_ready, 1)
                transposed_remainder("mT", hT, hT_lo, 1)
                remainders(("out", 1))

                def moments(t):
                    for j in range(2):
                        last = V.bn_stats(stats[:, t, j, :], h[:, t, j * HALF:(j + 1) * HALF])
                    lk(last)
                    dve.sem_inc(passed_wait, 1)
                    lk(V.bn_aggr(mv[:, t, :], stats[:, t, :, :].rearrange("p a b -> p (a b)")))
                    V.tensor_scalar(mv[:, t, 1:2], mv[:, t, 1:2], EPS, None, ALU.add).then_inc(var_ready, 1)

                def normalised(i, t):
                    if t == 0:
                        dve.wait_ge(lnp_full, L * 96 + 32 * (i + 1))
                    dve.wait_ge(sqrt_done, L * 6 + (2 * i + t + 1))
                    V.reciprocal(rstd[:, 1, t:t + 1], rstd[:, 0, t:t + 1])
                    for j in range(2):
                        v, cols = h[:, t, j * HALF:(j + 1) * HALF], slice(j * HALF, (j + 1) * HALF)
                        lk(V.scalar_tensor_tensor(out=v, in0=v, scalar=mv[:, t, 0:1], in1=lnp[:, 0, cols],
                                                  op0=ALU.subtract, op1=ALU.mult))
                        V.scalar_tensor_tensor(out=v, in0=v, scalar=rstd[:, 1, t:t + 1], in1=lnp[:, 1, cols],
                                               op0=ALU.mult, op1=ALU.add).then_inc(h_ready, 1)
                    if t == 1:
                        dve.wait_ge(h_ready, L * 12 + (4 * i + 8))
                        dve.sem_inc(lnp_free, 1)

                def residual(names, t, first=0):
                    for j, name in enumerate(names, first):
                        dve.wait_ge(*full(name, L))
                        d = h[:, t, j * HALF:(j + 1) * HALF]
                        frees(V.scalar_tensor_tensor(out=d, in0=d, scalar=ALPHA, in1=ps(name)[:, :],
                                                     op0=ALU.mult, op1=ALU.add), name)
                    dve.wait_ge(*taken(name, L))

                residual([("out0", 0)], 0)
                residual([("out0", 1)], 1)
                for t in range(TT):
                    residual([("out1", t)], t, 1)
                    moments(t)
                    normalised(0, t)

                R = [rt[:, i] for i in range(24)]
                dve.wait_ge(*full("router", L))
                lg = ps("router")[:, 0:40].rearrange("p (t n) -> p t n", t=TT)
                V.tensor_tensor(R[0][:, :, 0:4], lg[:, :, 0:4], rows[:, 64:68].unsqueeze(1).broadcast_to([P, TT, 4]), ALU.add)
                frees(V.tensor_tensor(R[1], lg[:, :, 4:20], rows[:, 68:84].unsqueeze(1).broadcast_to([P, TT, 16]),
                                      ALU.add), "router")
                dve.wait_ge(*taken("router", L))
                dve.sem_inc(params_free, 1)

                def bc(ap, n):
                    return ap.broadcast_to([P, TT, n])

                def first_max(src, m, tmp, hot):
                    lk(V.tensor_tensor(tmp[:, :, 0:4], src, bc(m, 4), ALU.is_equal))
                    lk(V.tensor_tensor(tmp[:, :, 0:4], tmp[:, :, 0:4],
                                       weight4.unsqueeze(1).broadcast_to([P, TT, 4]), ALU.mult))
                    lk(V.tensor_reduce(tmp[:, :, 4:5], tmp[:, :, 0:4], AX.X, ALU.max))
                    lk(V.tensor_tensor(hot, tmp[:, :, 0:4], bc(tmp[:, :, 4:5], 4), ALU.is_equal))

                gmax = R[4][:, :, 0:1]
                lk(V.tensor_reduce(gmax, R[0][:, :, 0:4], AX.X, ALU.max))
                V.tensor_tensor(R[2][:, :, 0:4], R[0][:, :, 0:4], bc(gmax, 4), ALU.subtract).then_inc(rexp_in, 1)
                first_max(R[0][:, :, 0:4], gmax, R[5], R[6][:, :, 0:4])
                dve.sem_inc(group_ready, 1)
                gl = R[7].rearrange("p t (g e) -> p t g e", g=MOE_G)
                lk(V.tensor_tensor(gl, R[1].rearrange("p t (g e) -> p t g e", g=MOE_G),
                                   R[6][:, :, 0:4].unsqueeze(3).broadcast_to([P, TT, MOE_G, MOE_E]), ALU.mult))
                es = R[8][:, :, 0:4]
                lk(V.tensor_reduce(es, R[7].rearrange("p t (g e) -> p t e g", g=MOE_G), AX.X, ALU.add))

                dve.wait_ge(*full("rank", L))
                cnt = ps("rank")[:, 0:12].rearrange("p (t g) -> p t g", g=MOE_G)
                lk(V.tensor_tensor(R[21][:, :, 0:4], R[6][:, :, 0:4], cnt[:, 0:2, :], ALU.mult))
                lk(V.tensor_scalar(R[21][:, :, 0:4], R[21][:, :, 0:4], -1.0, None, ALU.add))
                frees(V.tensor_reduce(R[22][:, 0, 0:1], cnt[:, 2, :], AX.X, ALU.max), "rank")
                dve.wait_ge(*taken("rank", L))
                V.tensor_scalar(overflow[:], R[22][:, 0, 0:1], float(CAP), None, ALU.is_gt).then_inc(flag_ready, 1)
                for t in range(TT):
                    last = V.tensor_tensor(sel[:, t, :].rearrange("p (g s) -> p g s", g=MOE_G),
                                           const("iota").unsqueeze(1).broadcast_to([P, MOE_G, CAP]),
                                           R[21][:, t, 0:4].unsqueeze(2).broadcast_to([P, MOE_G, CAP]), ALU.is_equal)
                last.then_inc(sel_ready, 1)

                m1, m2 = R[9][:, :, 0:1], R[10][:, :, 0:1]
                lk(V.tensor_reduce(m1, es, AX.X, ALU.max))
                first_max(es, m1, R[5], R[13][:, :, 0:4])
                lk(V.scalar_tensor_tensor(out=R[14][:, :, 0:4], in0=R[13][:, :, 0:4], scalar=NEG, in1=es,
                                          op0=ALU.mult, op1=ALU.add))
                lk(V.tensor_reduce(m2, R[14][:, :, 0:4], AX.X, ALU.max))
                V.tensor_tensor(R[11][:, :, 0:1], m2, m1, ALU.subtract).then_inc(rexp_in, 1)
                first_max(R[14][:, :, 0:4], m2, R[5], R[15][:, :, 0:4])
                dve.wait_ge(rexp_out, L * 2 + 2)
                lk(V.tensor_reduce(R[16][:, :, 0:1], R[3][:, :, 0:4], AX.X, ALU.add))
                lk(V.reciprocal(R[16][:, :, 1:2], R[16][:, :, 0:1]))
                lk(V.tensor_scalar(R[17][:, :, 0:1], R[12][:, :, 0:1], 1.0, None, ALU.add))
                lk(V.reciprocal(R[17][:, :, 1:2], R[17][:, :, 0:1]))
                lk(V.tensor_tensor(R[17][:, :, 2:3], R[17][:, :, 1:2], R[16][:, :, 1:2], ALU.mult))
                lk(V.tensor_tensor(R[17][:, :, 3:4], R[17][:, :, 2:3], R[12][:, :, 0:1], ALU.mult))
                V.tensor_tensor(R[18][:, :, 0:4], R[13][:, :, 0:4], bc(R[17][:, :, 2:3], 4), ALU.mult)
                lk(V.tensor_tensor(R[19][:, :, 0:4], R[15][:, :, 0:4], bc(R[17][:, :, 3:4], 4), ALU.mult))
                lk(V.tensor_tensor(R[18][:, :, 0:4], R[18][:, :, 0:4], R[19][:, :, 0:4], ALU.add))
                for t in range(TT):
                    last = V.tensor_tensor(rt[:, COMBINE, t, :].rearrange("p (g e) -> p g e", g=MOE_G),
                                           R[6][:, t, 0:4].unsqueeze(2).broadcast_to([P, MOE_G, MOE_E]),
                                           R[18][:, t, 0:4].unsqueeze(1).broadcast_to([P, MOE_G, MOE_E]), ALU.mult)
                last.then_inc(combine_ready, 1)

                dve.wait_ge(flag_ready, L + 1)
                dve.sem_inc(passed_wait, 1)
                with dve.If(dve.value_load(overflow[0:1, 0:1], min_val=0, max_val=1) == 0):
                    remainders(("gu", 0), (0,))
                    for d in range(KT):
                        rounded_job()
                        frees(V.tensor_tensor(reduced(hS_lo[:, d, :]), ps(("sorted", d))[:, 0:NS], hS[:, d, :],
                                              ALU.subtract), ("sorted", d))
                        if d < 3:
                            remainders(("gu", 0), (1 + d,))

                    def expert(e):
                        dve.wait_ge(silu_s, L * NE + (e + 1))
                        dve.wait_ge(*taken(("weight", e // MOE_E), L))
                        name = ("hgu", e)
                        frees(V.scalar_tensor_tensor(out=u_s[0:CAP, e % 2, :], in0=ps(name)[0:CAP, HID:2 * HID],
                                                     scalar=weight_s[0:CAP, e:e + 1], in1=gate_s[0:CAP, e % 2, :],
                                                     op0=ALU.mult, op1=ALU.mult), name)
                        dve.wait_ge(*taken(name, L))
                        dve.sem_inc(act_ready, 1)

                    def expert_remainder(e):
                        rounded_job()
                        frees(V.tensor_tensor(reduced(uT_lo[:, e % 2]),
                                              ps(("uT", e))[:, 0:2 * CAP].rearrange("p (k s) -> p k s", k=2),
                                              uT_hi[:, e % 2], ALU.subtract), ("uT", e))

                    def group_remainder(g):
                        for j in range(2):
                            rounded_job()
                            cols = slice(j * HALF, (j + 1) * HALF)
                            frees(V.tensor_tensor(reduced(yg_lo[g // 2][0:CAP, g % 2, cols]), ps(("yg", g, j))[0:CAP, :],
                                                  yg[0:CAP, g, cols], ALU.subtract), ("yg", g, j))

                    for e in range(0, NE, 2):
                        remainders(("gu", e + 1), (0, 1, 2))
                        if e >= 2 and e % MOE_E == 0:
                            group_remainder(e // MOE_E - 1)
                        remainders(("gu", e + 1), (3,))
                        expert(e)
                        remainders(("down", e), (0,))
                        expert_remainder(e)
                        remainders(("down", e), (1,))
                        expert(e + 1)
                        remainders(("down", e), (2, 3))
                        expert_remainder(e + 1)
                        if e < NE - 2:
                            remainders(("gu", e + 2))
                        else:
                            group_remainder(MOE_G - 1)
                with dve.Else():
                    for e in range(NE):
                        u = act_t[:, e % 2, :]
                        dve.wait_ge(*taken(("hg", e), L))
                        dve.wait_ge(*full(("hu", e), L))
                        frees(V.tensor_tensor(u, act_s[:, e % 2, :], ps(("hu", e))[:, :], ALU.mult), ("hu", e))
                        dve.wait_ge(*taken(("hu", e), L))
                        dve.wait_ge(*taken(("comb", e // 2), L))
                        u2 = u.rearrange("p (f s) -> p f s", f=2)
                        V.tensor_tensor(u2, u2, comb[:, e, :].unsqueeze(1).broadcast_to([P, 2, SEQ]),
                                        ALU.mult).then_inc(act_ready, 1)
                    dve.sem_inc(remainder_ready["dve"], MOE_REMAINDERS["dve"])
                assert split_jobs[0] == ROUNDED - 4
                remainders(("ple_gate", 0))
                residual([("acc", 0, 0), ("acc", 0, 1)], 0)
                moments(0)
                residual([("acc", 1, 0)], 1)
                normalised(1, 0)
                residual([("acc", 1, 1)], 1, 1)
                moments(1)
                transposed_remainder("hT3", hT, hT_lo, 0)
                normalised(1, 1)
                transposed_remainder("hT3", hT, hT_lo, 1)
                remainders(("ple_gate", 1))
                assert split_jobs[0] == ROUNDED
                for j in range(2):
                    for t in range(TT):
                        dve.wait_ge(*taken((f"pg{j}", t), L))
                        g = G[:, 0, t, j * HALF:(j + 1) * HALF]
                        lk(V.tensor_tensor(g, g, xtok[:, t, j * HALF:(j + 1) * HALF], ALU.mult))
                        d = h[:, t, j * HALF:(j + 1) * HALF]
                        lk(V.scalar_tensor_tensor(out=d, in0=d, scalar=ALPHA, in1=g, op0=ALU.mult, op1=ALU.add))
                        if j == 1:
                            moments(t)
                            normalised(2, t)
                assert steps[0] == DVE_STEPS, f"DVE_STEPS = {steps[0]}"


_INS = ["x", "p", "positions", "w_in", "ssd_conv_w", "ssd_conv_b", "ssd_dt_bias", "ssd_a_log", "ssd_d",
        "ssd_norm_w", "attn_sinks", "pool_w", "pool_scale", "w_branch", "w_out", "ln1_g", "ln1_b",
        "router_group_w", "router_group_b", "router_expert_w", "router_expert_b", "exp_w_gate",
        "exp_w_up", "exp_w_down", "ln2_g", "ln2_b", "ple_w_proj", "ple_w_gate", "ln3_g", "ln3_b"]


def kernel(**inputs):
    import concourse.bacc as bacc
    from concourse.bass_utils import run_bass_kernel_spmd

    nc = bacc.Bacc("TRN2", target_bir_lowering=False, num_devices=1)
    arrays, args = {}, []
    for name in _INS + ["consts"]:
        a = shape_constants() if name == "consts" else np.ascontiguousarray(inputs[name])
        arrays[f"in_{name}"] = a
        args.append(nc.dram_tensor(f"in_{name}", a.shape, mybir.dt.from_np(a.dtype), kind="ExternalInput").ap())
    args.append(nc.dram_tensor("out_h", (1, SEQ, D), F32, kind="ExternalOutput").ap())
    program(nc, *args)
    return run_bass_kernel_spmd(nc, [arrays], core_ids=[0]).results[0]["out_h"]
```
